# Optimizing a Trainium2 kernel written in Bass

```python
import jax, jax.numpy as jnp
from jax import lax
import numpy as np

D_MODEL = 1024
BATCH = 1
SEQ = 1024
DEPTH = 1
DEC_BATCH = 8
DEC_SEQ = 1
PAST_LEN = 8192
PAGE_SIZE = 128

HEAD_DIM = 64
D_MIX = D_MODEL
N_Q_HEADS = 8
N_KV_HEADS = 2
Q_PER_KV = N_Q_HEADS // N_KV_HEADS
D_ATTN = N_Q_HEADS * HEAD_DIM
D_KV = N_KV_HEADS * HEAD_DIM
D_CONV = D_MIX - D_ATTN
WINDOW = 128
ATT_BLOCK = 128
CONV_WIDTH = 31
CONV_STATE = CONV_WIDTH - 1
D_IN = D_ATTN + 2 * D_KV + 2 * D_CONV
N_KEYS = 128
N_EXPERTS = N_KEYS * N_KEYS
PEER_HEADS = 8
PEER_TOPK = 16
D_KEY = 256
D_HALF = D_KEY // 2
PEER_CHUNK = 256
D_PLE = 256
EPS = 1e-6
NEG = -1e30

kernel_name = 'hymba_conformer_swa_peer_step'

def rmsnorm(x, g):
    xf = x.astype(jnp.float32)
    y = xf * lax.rsqrt(jnp.mean(xf * xf, axis=-1, keepdims=True) + EPS)
    return (y * g.astype(jnp.float32)).astype(x.dtype)

def layernorm(x, g, b):
    xf = x.astype(jnp.float32)
    mu = jnp.mean(xf, axis=-1, keepdims=True)
    xc = xf - mu
    y = xc * lax.rsqrt(jnp.mean(xc * xc, axis=-1, keepdims=True) + EPS)
    return (y * g.astype(jnp.float32) + b.astype(jnp.float32)).astype(x.dtype)

def alibi_slopes():
    s = np.array([2.0 ** (-8.0 * (h + 1) / N_Q_HEADS) for h in range(N_Q_HEADS)], np.float32)
    return jnp.asarray(s).reshape(N_KV_HEADS, Q_PER_KV, 1, 1)

def mixer_inputs(h, w_in, q_gain, k_gain):
    z = h @ w_in
    lead = h.shape[:-1]
    o1, o2, o3, o4 = D_ATTN, D_ATTN + D_KV, D_ATTN + 2 * D_KV, D_ATTN + 2 * D_KV + D_CONV
    q = rmsnorm(z[..., :o1].reshape(*lead, N_Q_HEADS, HEAD_DIM), q_gain)
    k = rmsnorm(z[..., o1:o2].reshape(*lead, N_KV_HEADS, HEAD_DIM), k_gain)
    v = z[..., o2:o3].reshape(*lead, N_KV_HEADS, HEAD_DIM)
    glu = z[..., o3:o4] * jax.nn.sigmoid(z[..., o4:])
    return q, k, v, glu

def sink_attention(q, k, v, sinks, dist, valid):
    s = jnp.einsum('...qhgd,...khd->...hgqk', q, k).astype(jnp.float32) * (HEAD_DIM ** -0.5)
    s = s - alibi_slopes() * dist.astype(jnp.float32)
    s = jnp.where(valid, s, NEG)
    sink = sinks.astype(jnp.float32).reshape(N_KV_HEADS, Q_PER_KV, 1, 1)
    m = jnp.maximum(jnp.max(s, axis=-1, keepdims=True), sink)
    e = jnp.exp(s - m)
    probs = e / (jnp.sum(e, axis=-1, keepdims=True) + jnp.exp(sink - m))
    return jnp.einsum('...hgqk,...khd->...qhgd', probs.astype(v.dtype), v)

def prompt_window_attention(q, k, v, sinks):
    B, S = q.shape[0], q.shape[1]
    nb = S // ATT_BLOCK
    qb = q.reshape(B, nb, ATT_BLOCK, N_KV_HEADS, Q_PER_KV, HEAD_DIM)
    kb = k.reshape(B, nb, ATT_BLOCK, N_KV_HEADS, HEAD_DIM)
    vb = v.reshape(B, nb, ATT_BLOCK, N_KV_HEADS, HEAD_DIM)
    prev = lambda t: jnp.concatenate([jnp.zeros_like(t[:, :1]), t[:, :-1]], axis=1)
    kk = jnp.concatenate([prev(kb), kb], axis=2)
    vv = jnp.concatenate([prev(vb), vb], axis=2)
    i = jnp.arange(ATT_BLOCK)[:, None]
    j = jnp.arange(2 * ATT_BLOCK)[None, :]
    dist = ATT_BLOCK + i - j
    band = (dist >= 0) & (dist <= WINDOW)
    has_prev = (jnp.arange(nb)[:, None, None] > 0) | (j >= ATT_BLOCK)[None]
    valid = (band[None] & has_prev)[:, None, None]
    out = sink_attention(qb, kk, vv, sinks, dist, valid)
    return out.reshape(B, S, D_ATTN)

def sample_window_attention(q, k, v, ck, cv, sinks):
    DB, T = q.shape[0], q.shape[1]
    kk = jnp.concatenate([ck, k], axis=1)
    vv = jnp.concatenate([cv, v], axis=1)
    qs = q.reshape(DB, T, N_KV_HEADS, Q_PER_KV, HEAD_DIM)
    i = jnp.arange(T)[:, None]
    j = jnp.arange(WINDOW + T)[None, :]
    dist = WINDOW + i - j
    valid = (dist >= 0) & (dist <= WINDOW)
    out = sink_attention(qs, kk, vv, sinks, dist, valid)
    return out.reshape(DB, T, D_ATTN), kk[:, -WINDOW:], vv[:, -WINDOW:]

def conv_branch(glu_hist, dw_w, dw_b, ln_g, ln_b):
    y = lax.conv_general_dilated(glu_hist, dw_w[:, None, :], window_strides=(1,), padding='VALID',
                                 dimension_numbers=('NWC', 'WIO', 'NWC'), feature_group_count=D_CONV)
    y = layernorm(y + dw_b, ln_g, ln_b)
    return jax.nn.silu(y)

def peer(h, w_pq, sub_keys, u_tab, v_tab):
    lead = h.shape[:-1]
    flat = h.reshape(-1, D_MODEL)
    n = flat.shape[0]
    pad = (-n) % PEER_CHUNK
    chunks = jnp.pad(flat, ((0, pad), (0, 0))).reshape(-1, PEER_CHUNK, D_MODEL)

    def one(xc):
        q = (xc @ w_pq).reshape(PEER_CHUNK, PEER_HEADS, 2, D_HALF)
        s = jnp.einsum('nhpd,pkd->nhpk', q, sub_keys).astype(jnp.float32)
        s1, i1 = lax.top_k(s[:, :, 0], PEER_TOPK)
        s2, i2 = lax.top_k(s[:, :, 1], PEER_TOPK)
        cand = (s1[..., :, None] + s2[..., None, :]).reshape(PEER_CHUNK, PEER_HEADS, PEER_TOPK * PEER_TOPK)
        cid = (i1[..., :, None] * N_KEYS + i2[..., None, :]).reshape(PEER_CHUNK, PEER_HEADS, PEER_TOPK * PEER_TOPK)
        top_s, pos = lax.top_k(cand, PEER_TOPK)
        eid = jnp.take_along_axis(cid, pos, axis=-1)
        g = jax.nn.softmax(top_s, axis=-1)
        act = jax.nn.gelu(jnp.einsum('nhkd,nd->nhk', u_tab[eid], xc).astype(jnp.float32), approximate=False)
        w = (g * act).astype(xc.dtype)
        return jnp.einsum('nhk,nhkd->nd', w, v_tab[eid])

    out = lax.map(one, chunks).reshape(-1, D_MODEL)[:n]
    return out.reshape(*lead, D_MODEL)

def finish(x, mixed, p, w_out, norm_ffn, peer_wq, peer_sub_keys, peer_u, peer_v, norm_ple, w_ple_proj, w_ple_gate):
    x = x + mixed @ w_out
    x = x + peer(rmsnorm(x, norm_ffn), peer_wq, peer_sub_keys, peer_u, peer_v)
    gate = jax.nn.sigmoid(rmsnorm(x, norm_ple) @ w_ple_gate)
    return x + (p @ w_ple_proj) * gate

def setup_inputs(seed: int = 0) -> dict:
    key = jax.random.key(seed)
    ks = jax.random.split(key, 26)
    nrm = lambda k, shape, s: s * jax.random.normal(k, shape, jnp.float32)
    L = DEPTH
    return {
        'x_prompt': nrm(ks[0], (BATCH, SEQ, D_MODEL), 1.0),
        'x_sample': nrm(ks[1], (DEC_BATCH, DEC_SEQ, D_MODEL), 1.0),
        'cache_k': nrm(ks[2], (L, DEC_BATCH, WINDOW, N_KV_HEADS, HEAD_DIM), 1.0),
        'cache_v': nrm(ks[3], (L, DEC_BATCH, WINDOW, N_KV_HEADS, HEAD_DIM), 1.0),
        'state_conv': nrm(ks[4], (L, DEC_BATCH, CONV_STATE, D_CONV), 0.5),
        'p_prompt': nrm(ks[5], (L, BATCH, SEQ, D_PLE), 1.0),
        'p_sample': nrm(ks[6], (L, DEC_BATCH, DEC_SEQ, D_PLE), 1.0),
        'norm_mix': 1.0 + nrm(ks[7], (L, D_MODEL), 0.01),
        'w_in': nrm(ks[8], (L, D_MODEL, D_IN), D_MODEL ** -0.5),
        'q_gain': 1.0 + nrm(ks[9], (L, HEAD_DIM), 0.01),
        'k_gain': 1.0 + nrm(ks[10], (L, HEAD_DIM), 0.01),
        'attn_sinks': nrm(ks[11], (L, N_Q_HEADS), 0.5),
        'conv_dw_w': nrm(ks[12], (L, CONV_WIDTH, D_CONV), CONV_WIDTH ** -0.5),
        'conv_dw_b': nrm(ks[13], (L, D_CONV), 0.01),
        'conv_ln_g': 1.0 + nrm(ks[14], (L, D_CONV), 0.01),
        'conv_ln_b': nrm(ks[15], (L, D_CONV), 0.01),
        'w_out': nrm(ks[16], (L, D_MIX, D_MODEL), D_MIX ** -0.5),
        'norm_ffn': 1.0 + nrm(ks[17], (L, D_MODEL), 0.01),
        'peer_wq': nrm(ks[18], (L, D_MODEL, PEER_HEADS * D_KEY), D_MODEL ** -0.5),
        'peer_sub_keys': nrm(ks[19], (L, 2, N_KEYS, D_HALF), D_HALF ** -0.5),
        'peer_u': nrm(ks[20], (L, N_EXPERTS, D_MODEL), D_MODEL ** -0.5),
        'peer_v': nrm(ks[21], (L, N_EXPERTS, D_MODEL), PEER_HEADS ** -0.5),
        'norm_ple': 1.0 + nrm(ks[22], (L, D_MODEL), 0.01),
        'w_ple_proj': nrm(ks[23], (L, D_PLE, D_MODEL), D_PLE ** -0.5),
        'w_ple_gate': nrm(ks[24], (L, D_MODEL, D_MODEL), D_MODEL ** -0.5),
    }

def reference(x_prompt, x_sample, cache_k, cache_v, state_conv, p_prompt, p_sample,
              norm_mix, w_in, q_gain, k_gain, attn_sinks, conv_dw_w, conv_dw_b, conv_ln_g, conv_ln_b,
              w_out, norm_ffn, peer_wq, peer_sub_keys, peer_u, peer_v, norm_ple, w_ple_proj, w_ple_gate):
    xp, xs = x_prompt, x_sample
    nk_p, nv_p, nc_p, nk_s, nv_s, nc_s = [], [], [], [], [], []
    for i in range(DEPTH):
        h = rmsnorm(xp, norm_mix[i])
        q, k, v, glu = mixer_inputs(h, w_in[i], q_gain[i], k_gain[i])
        att = prompt_window_attention(q, k, v, attn_sinks[i])
        conv_in = jnp.concatenate([jnp.zeros((glu.shape[0], CONV_STATE, D_CONV), glu.dtype), glu], axis=1)
        cvo = conv_branch(conv_in, conv_dw_w[i], conv_dw_b[i], conv_ln_g[i], conv_ln_b[i])
        mixed = jnp.concatenate([att, cvo], axis=-1)
        nk_p.append(k[:, -WINDOW:])
        nv_p.append(v[:, -WINDOW:])
        nc_p.append(conv_in[:, -CONV_STATE:])
        xp = finish(xp, mixed, p_prompt[i], w_out[i], norm_ffn[i], peer_wq[i], peer_sub_keys[i],
                    peer_u[i], peer_v[i], norm_ple[i], w_ple_proj[i], w_ple_gate[i])

        h = rmsnorm(xs, norm_mix[i])
        q, k, v, glu = mixer_inputs(h, w_in[i], q_gain[i], k_gain[i])
        att, kw, vw = sample_window_attention(q, k, v, cache_k[i], cache_v[i], attn_sinks[i])
        conv_in = jnp.concatenate([state_conv[i], glu], axis=1)
        cvo = conv_branch(conv_in, conv_dw_w[i], conv_dw_b[i], conv_ln_g[i], conv_ln_b[i])
        mixed = jnp.concatenate([att, cvo], axis=-1)
        nk_s.append(kw)
        nv_s.append(vw)
        nc_s.append(conv_in[:, -CONV_STATE:])
        xs = finish(xs, mixed, p_sample[i], w_out[i], norm_ffn[i], peer_wq[i], peer_sub_keys[i],
                    peer_u[i], peer_v[i], norm_ple[i], w_ple_proj[i], w_ple_gate[i])
    return (xp, xs, jnp.stack(nk_p), jnp.stack(nv_p), jnp.stack(nc_p), jnp.stack(nk_s), jnp.stack(nv_s), jnp.stack(nc_s))


_drawn_inputs = setup_inputs


def setup_inputs(seed=0):
    import zlib

    import numpy as np

    out = dict(_drawn_inputs(seed))
    spreads = {}
    factors = {'norm_mix': 4.67,
     'q_gain': 8.0,
     'k_gain': 5.15,
     'conv_dw_b': 3.571,
     'conv_ln_g': 21.601,
     'conv_ln_b': 18.775,
     'norm_ffn': 12.784,
     'norm_ple': 200.0,
     'attn_sinks': 33.562}
    for name, (base, spread) in spreads.items():
        noise = np.random.default_rng([zlib.crc32(name.encode()), seed]).standard_normal(out[name].shape)
        drawn = base * np.exp(spread * noise) if base else spread * noise
        out[name] = __import__('jax').numpy.asarray(drawn.astype(out[name].dtype))
    for name, factor in factors.items():
        out[name] = (out[name] * factor).astype(out[name].dtype)
    return out
```

```python
import concourse.bass as bass
from concourse import mybir
from contextlib import ExitStack

F32 = mybir.dt.float32
U32 = mybir.dt.uint32
ALU = mybir.AluOpType
ACT = mybir.ActivationFunctionType
AX = mybir.AxisListType

P = 128
D = 1024
KD = D // P
SEQ = 1024
NT = SEQ // P
NB = 8
HEADS, KV, HD = 8, 2, 64
GROUP = HEADS // KV
QW, KW = HEADS * HD, KV * HD
CONV = D - QW
CT = CONV // P
TAPS = 31
HIST = TAPS - 1
DIN = QW + 2 * KW + 2 * CONV
ZK, ZV, ZA, ZG = QW, QW + KW, QW + 2 * KW, QW + 2 * KW + CONV
WIN = 2 * P
SKEYS = P + 1
EPS = 1e-6
NEG = -1e30
ARENA = 52900
BANK = 512
PH = 8
TOPK = 16
NKEY = 128
CHOICES = PH * TOPK
DPLE = 256
RING = 8


class Chain:

    def __init__(self, eng, sem, base=0):
        self.eng, self.sem, self.base, self.n = eng, sem, base, 0

    def link(self, ins):
        self.n += 1
        ins.then_inc(self.sem, 1)
        self.eng.wait_ge(self.sem, self.base + self.n)


def carve(arena, start):
    at = [start]

    def take(*shape):
        size = 1
        for s in shape:
            size *= s
        view = arena[:, at[0]:at[0] + size]
        at[0] += size
        if len(shape) == 2:
            view = view.rearrange("p (a b) -> p a b", b=shape[1])
        elif len(shape) == 3:
            view = view.rearrange("p (a b c) -> p a b c", b=shape[1], c=shape[2])
        return view
    take.at = at
    return take


def over_partitions(vector, n):
    return vector.partition_broadcast(n)


def hymba_step(nc, x_prompt, x_sample, cache_k, cache_v, state_conv, p_prompt, p_sample, norm_mix, w_in,
               q_gain, k_gain, attn_sinks, conv_dw_w, conv_dw_b, conv_ln_g, conv_ln_b, w_out, norm_ffn,
               peer_wq, peer_sub_keys, peer_u, peer_v, norm_ple, w_ple_proj, w_ple_gate,
               y_prompt, y_sample, new_k_prompt, new_v_prompt, new_conv_prompt,
               new_k_sample, new_v_sample, new_conv_sample):
    with ExitStack() as ctx:
        def sb(name, shape, dt=F32):
            return ctx.enter_context(nc.sbuf_tensor(name, shape, dt))

        ident = sb("ident", [P, P])
        eps = sb("eps", [P, 1])
        norm_cols = sb("norm_cols", [P, 2, KD])
        arena = sb("arena", [P, ARENA])
        x1 = nc.dram_tensor("x1", (NT + 1, P, D), F32, kind="Internal").ap()

        mixer(nc, ident, eps, norm_cols, arena, x1, x_prompt, x_sample, cache_k[0], cache_v[0], state_conv[0],
              norm_mix, w_in[0], q_gain, k_gain, attn_sinks, conv_dw_w[0], conv_dw_b, conv_ln_g, conv_ln_b,
              w_out[0], norm_ple, new_k_prompt, new_v_prompt, new_conv_prompt, new_k_sample, new_v_sample,
              new_conv_sample)
        experts(nc, ident, eps, norm_cols, arena, x1, p_prompt[0], p_sample[0], norm_ffn, peer_wq[0],
                peer_sub_keys[0], peer_u[0], peer_v[0], w_ple_proj[0], w_ple_gate[0], y_prompt, y_sample)


def mixer(nc, ident, eps, norm_cols, arena, x1, x_prompt, x_sample, cache_k, cache_v, state_conv, norm_mix, w_in,
          q_gain, k_gain, attn_sinks, conv_dw_w, conv_dw_b, conv_ln_g, conv_ln_b, w_out, norm_ple,
          new_k_prompt, new_v_prompt, new_conv_prompt, new_k_sample, new_v_sample, new_conv_sample):
    with ExitStack() as ctx:
        sems = {}

        def sem(name):
            sems[name] = ctx.enter_context(nc.semaphore(name))
            return sems[name]

        ZB = ctx.enter_context(nc.psum_tensor("ZB", [P, 4 * BANK], F32))
        TB = ctx.enter_context(nc.psum_tensor("TB", [P, 4 * BANK], F32))

        take = carve(arena, 0)
        win_w = take(KD, DIN)
        wout_w = take(KD, D)
        x_in = take(D)
        x_res = take(D)
        xn = take(D)
        hT = take(KD, P)
        squares = take(D)
        qk = take(QW + KW)
        vwin = take(2, KW)
        glu = take(CONV)
        gate = take(CONV)
        kwin = take(WIN)
        qT = take(GROUP, P)
        gluT = take(CT, HIST + P)
        bias = take(HEADS, WIN)
        bias_prev = take(HEADS, P)
        probs = take(HEADS, WIN)
        probsT = take(2 * HEADS, P)
        mixedT = take(KD, P)
        acc = take(CT, P)
        conv_y = take(CT, P)
        conv_s = take(CT, P)
        chan_rows = take(CONV)
        chan = take(CT, TAPS + 3)
        norm_rows = take(P)
        qg = take(HD)
        kg = take(HD)
        sinks = take(HEADS)
        sink_rows = take(1)
        stat = take(64)
        s_take = carve(arena, take.at[0])
        sbias = s_take(P + 4)
        new_rows = s_take(P)
        own = s_take(NB)
        new_T = s_take(P)
        take.at[0] = s_take.at[0]
        q_blocks = bias_prev.rearrange("p a b -> p (a b)")[:, 0:NB * 72]
        k_rows = probsT[:, 0:8, :]
        v_rows = probsT[:, 8:16, :]
        keysT = bias.rearrange("p a b -> p (a b)")[:, 0:NB * SKEYS].rearrange("p (b k) -> p b k", k=SKEYS)
        st_rows = probs.rearrange("p a b -> p (a b)")[:, 0:2 * CONV].rearrange("p (g c) -> p g c", g=2)
        hist = hT.rearrange("p a b -> p (a b)")[:, 0:CT * NB * TAPS].rearrange("p (c b j) -> p c b j", c=CT, b=NB)
        prod = squares[:, 0:CT * NB * TAPS].rearrange("p (c b j) -> p c b j", c=CT, b=NB)
        assert take.at[0] <= ARENA, take.at[0]
        s_qT = TB[:, 0:QW].rearrange("p (i t) -> p i t", t=P)

        ssq, rms, rstd = stat[:, 0:1], stat[:, 1:2], stat[:, 2:3]
        ss10, rms10, rstd10 = stat[:, 3:13], stat[:, 13:23], stat[:, 23:33]
        top, ntop, esink = stat[:, 33:41], stat[:, 41:49], stat[:, 49:57]
        more = take(64)
        den, rden = more[:, 0:8], more[:, 8:16]
        bn6, mv, rms_c, rstd_c, dsink = more[:, 16:22], more[:, 22:24], more[:, 24:25], more[:, 25:26], more[:, 26:34]
        assert take.at[0] <= ARENA, take.at[0]

        const_made, const_in, weights_in, out_w_in = sem("const_made"), sem("const_in"), sem("w_in_in"), sem("w_out_in")
        rows_in, cols_T, cols_made = sem("const_rows_in"), sem("const_cols_T"), sem("const_cols_made")
        window_cleared = sem("window_cleared")
        x_landed, res_landed, x1_stored = sem("x_landed"), sem("x_res_landed"), sem("x1_stored")
        squared, xn_ready, xT_ready, hT_ready, z_ready = (sem(n) for n in ("x_squared", "xn_ready", "xT_ready", "hT_ready", "z_ready"))
        qk_squared, qk_summed, qk_rms, sig_ready = sem("qk_squared"), sem("qk_summed"), sem("qk_rms_ready"), sem("gate_ready")
        v_ready = sem("v_ready")
        qk_ready, glu_ready, qkT_ready, gluT_ready = sem("qk_ready"), sem("glu_ready"), sem("qkT_ready"), sem("gluT_ready")
        qk_copied, s_ready, m_ready, bias_set, e_ready = sem("qk_copied"), sem("scores_ready"), sem("max_ready"), sem("bias_set"), sem("exp_ready")
        p_ready, pT_ready, pT_copied, att_ready, att_copied = sem("probs_ready"), sem("probsT_ready"), sem("probsT_copied"), sem("att_ready"), sem("att_copied")
        conv_done, c_ready, cvar_ready, crms_ready = sem("conv_done"), sem("conv_tok_ready"), sem("conv_var_ready"), sem("conv_rms_ready")
        ln_ready, lnT_ready, cy_ready, mix_ready, o_ready, x1_ready = (sem(n) for n in ("ln_ready", "lnT_ready", "conv_affine_ready", "mixed_ready", "w_out_ready", "x1_ready"))
        tail_stored, samples_in, outs_stored, copied_over = sem("prompt_tail_stored"), sem("samples_in"), sem("outs_stored"), sem("caches_copied")
        sbias_in, kT_ready, kT_copied, stT_ready, hist_ready = sem("sbias_in"), sem("cacheT_ready"), sem("cacheT_copied"), sem("stateT_ready"), sem("hist_ready")
        zero_stored = sem("x1_pad_stored")
        act_step, dve_step, act_on, dve_on, pool_on = sem("act_step"), sem("dve_step"), sem("act_on"), sem("dve_on"), sem("pool_on")
        kT_new, bias_out = sem("new_key_copied"), sem("bias_row_stored")
        bias_row = nc.dram_tensor("bias_row", (1, HEADS, SKEYS), F32, kind="Internal").ap()
        zero_ready, hT_free = sem("zeros_ready"), sem("stateT_ready_hT_free")
        s_probs = qT.rearrange("p i t -> p (i t)")[0:HEADS * NB, 0:SKEYS]
        s_probsT = qT.rearrange("p i t -> p (i t)")[:, 256:256 + HEADS * NB]
        pool_step = sem("pool_step")

        def hold(eng, carrier, s, value):
            eng.wait_ge(s, value)
            eng.sem_inc(carrier, 1)

        block = ctx.enter_context(nc.Block())

        @block.sync
        def _(sp):
            sp.dma_start(chan_rows[0:TAPS, :], conv_dw_w).then_inc(rows_in, 16)
            sp.dma_start(chan_rows[TAPS:TAPS + 1, :], conv_dw_b).then_inc(rows_in, 16)
            sp.dma_start(chan_rows[TAPS + 1:TAPS + 2, :], conv_ln_g).then_inc(rows_in, 16)
            sp.dma_start(chan_rows[TAPS + 2:TAPS + 3, :], conv_ln_b).then_inc(rows_in, 16)
            sp.dma_start(norm_rows[0:KD, :], norm_mix[0].rearrange("(k p) -> k p", p=P)).then_inc(rows_in, 16)
            sp.dma_start(norm_rows[KD:2 * KD, :], norm_ple[0].rearrange("(k p) -> k p", p=P)).then_inc(rows_in, 16)
            sp.dma_start(x_in, x_prompt[0, 0:P, :]).then_inc(x_landed, 16)
            for k in range(KD):
                sp.dma_start(win_w[:, k, :], w_in[k * P:(k + 1) * P, :]).then_inc(weights_in, 16)
            sp.dma_start(qg, over_partitions(q_gain[0], P)).then_inc(const_in, 16)
            sp.dma_start(kg, over_partitions(k_gain[0], P)).then_inc(const_in, 16)
            sp.dma_start(sinks, over_partitions(attn_sinks[0], P)).then_inc(const_in, 16)
            for b in range(NB):
                sp.dma_start(sink_rows[b * HEADS:(b + 1) * HEADS, :],
                             attn_sinks[0].rearrange("(h o) -> h o", o=1)).then_inc(const_in, 16)
            for kv in range(KV):
                sp.dma_start(wout_w[kv * HD:(kv + 1) * HD, 0:GROUP, :],
                             w_out[kv * GROUP * HD:(kv + 1) * GROUP * HD, :].rearrange("(i d) n -> d i n", d=HD)
                             ).then_inc(out_w_in, 16)
            sp.dma_start(wout_w[:, GROUP:KD, :], w_out[QW:D, :].rearrange("(k p) n -> p k n", p=P)).then_inc(out_w_in, 16)
            sp.dma_start(x_res, x_prompt[0, 0:P, :]).then_inc(res_landed, 16)
            for b in range(NB):
                sp.dma_start(new_k_sample[0, b, 0:P - 1], cache_k[b, 1:P]).then_inc(copied_over, 16)
                sp.dma_start(new_v_sample[0, b, 0:P - 1], cache_v[b, 1:P]).then_inc(copied_over, 16)
            sp.dma_start(new_conv_sample[0, :, 0:HIST - 1, :], state_conv[:, 1:HIST, :]).then_inc(copied_over, 16)
            with sp.Fori(1, NT) as t:
                sp.wait_ge(xn_ready, t)
                sp.dma_start(x_in, x_prompt[0, bass.ds(t * P, P), :]).then_inc(x_landed, 16)
                sp.wait_ge(x1_ready, t)
                sp.dma_start(x1[bass.ds(t - 1, 1), :, :].rearrange("o p d -> (o p) d"), x_res).then_inc(x1_stored, 16)
                sp.wait_ge(x1_stored, t * 16)
                sp.dma_start(x_res, x_prompt[0, bass.ds(t * P, P), :]).then_inc(res_landed, 16)
            sp.wait_ge(xn_ready, NT)
            sp.dma_start(x_in[0:NB, :], x_sample[:, 0, :]).then_inc(x_landed, 16)
            sp.wait_ge(bias_set, NT + 1)
            sp.dma_start(bias_row, bias[0:1, :, 0:SKEYS]).then_inc(bias_out, 16)
            sp.wait_ge(bias_out, 16)
            for b in range(NB):
                sp.dma_start(sbias[b * HEADS:(b + 1) * HEADS, 0:SKEYS], bias_row[0]).then_inc(sbias_in, 16)
            sp.wait_ge(att_ready, NT)
            sp.dma_start(k_rows, cache_k.rearrange("b w h d -> w b (h d)")).then_inc(samples_in, 16)
            sp.dma_start(v_rows, cache_v.rearrange("b w h d -> w b (h d)")).then_inc(samples_in, 16)
            for g in range(2):
                sp.dma_start(st_rows[0:4 * HIST, g, :],
                             state_conv[4 * g:4 * g + 4].rearrange("b j c -> (b j) c")).then_inc(samples_in, 16)
            sp.wait_ge(qk_ready, NT)
            sp.dma_start(new_k_prompt[0, 0].rearrange("w h d -> w (h d)"), qk[:, QW:QW + KW]).then_inc(tail_stored, 16)
            sp.wait_ge(v_ready, NT)
            sp.dma_start(new_v_prompt[0, 0].rearrange("w h d -> w (h d)"), vwin[:, 1, :]).then_inc(tail_stored, 16)
            sp.wait_ge(glu_ready, NT)
            sp.dma_start(new_conv_prompt[0, 0], glu[P - HIST:P, :]).then_inc(tail_stored, 16)
            sp.wait_ge(x1_ready, NT)
            sp.dma_start(x1[NT - 1], x_res).then_inc(x1_stored, 16)
            sp.wait_ge(x1_stored, NT * 16)
            sp.dma_start(x_res[0:NB, :], x_sample[:, 0, :]).then_inc(res_landed, 16)
            sp.wait_ge(zero_ready, 1)
            sp.dma_start(x1[NT, NB:P, :], probs.rearrange("p a b -> p (a b)")[NB:P, 2 * CONV:2 * CONV + D]).then_inc(zero_stored, 16)
            sp.wait_ge(qk_ready, NT + 1)
            sp.dma_start(new_k_sample[0, :, P - 1].rearrange("b h d -> b (h d)"), qk[0:NB, QW:QW + KW]).then_inc(outs_stored, 16)
            sp.wait_ge(v_ready, NT + 1)
            sp.dma_start(new_v_sample[0, :, P - 1].rearrange("b h d -> b (h d)"), vwin[0:NB, 1, :]).then_inc(outs_stored, 16)
            sp.wait_ge(glu_ready, NT + 1)
            sp.dma_start(new_conv_sample[0, :, HIST - 1, :], glu[0:NB, :]).then_inc(outs_stored, 16)
            sp.wait_ge(x1_ready, NT + 1)
            sp.dma_start(x1[NT, 0:NB, :], x_res[0:NB, :]).then_inc(x1_stored, 16)
            sp.wait_ge(x1_stored, (NT + 1) * 16)
            sp.wait_ge(zero_stored, 16)
            sp.wait_ge(tail_stored, 3 * 16)
            sp.wait_ge(copied_over, (2 * NB + 1) * 16)
            sp.wait_ge(outs_stored, 3 * 16)

        @block.gpsimd
        def _(pool):
            steps = Chain(pool, pool_step)
            steps.link(nc.gpsimd.memset(ident[:, :], 0.0))
            nc.gpsimd.affine_select(out=ident[:, :], in_=ident[:, :], compare_op=ALU.not_equal, fill=1.0, base=0,
                                    pattern=[[-1, P]], channel_multiplier=1).then_inc(const_made, 1)
            nc.gpsimd.memset(eps[:, :], EPS).then_inc(const_made, 1)
            nc.gpsimd.memset(kwin[:, 0:P], 0.0).then_inc(window_cleared, 1)
            nc.gpsimd.memset(vwin[:, 0, :], 0.0).then_inc(window_cleared, 1)
            nc.gpsimd.memset(gluT[:, :, 0:HIST], 0.0).then_inc(window_cleared, 1)
            steps.link(nc.gpsimd.iota(probs[:, 0, :], [[-1, WIN]], base=P, channel_multiplier=1,
                                      allow_small_or_imprecise_dtypes=True))
            for h in range(HEADS):
                last = nc.gpsimd.tensor_scalar(bias[:, h, :], probs[:, 0, :], -2.0 ** (-8.0 * (h + 1) / HEADS), 0.0,
                                               ALU.mult, ALU.add)
            steps.link(last)
            steps.link(nc.gpsimd.affine_select(out=bias[:, :, :], in_=bias[:, :, :], compare_op=ALU.is_ge, fill=NEG, base=P,
                                               pattern=[[0, HEADS], [-1, WIN]], channel_multiplier=1))
            steps.link(nc.gpsimd.affine_select(out=bias[:, :, :], in_=bias[:, :, :], compare_op=ALU.is_ge, fill=NEG, base=0,
                                               pattern=[[0, HEADS], [1, WIN]], channel_multiplier=-1))
            steps.link(nc.gpsimd.tensor_copy(bias_prev[:, :, :], bias[:, :, 0:P]))
            nc.gpsimd.memset(bias[:, :, 0:P], NEG).then_inc(bias_set, 1)
            steps.link(nc.gpsimd.memset(own[0:HEADS * NB, :], 1.0))
            steps.link(nc.gpsimd.affine_select(out=own[0:HEADS * NB, :], in_=own[0:HEADS * NB, :], compare_op=ALU.is_ge,
                                               fill=0.0, base=0, pattern=[[-HEADS, NB]], channel_multiplier=1))
            steps.link(nc.gpsimd.affine_select(out=own[0:HEADS * NB, :], in_=own[0:HEADS * NB, :], compare_op=ALU.is_ge,
                                               fill=0.0, base=HEADS - 1, pattern=[[HEADS, NB]], channel_multiplier=-1))
            nc.gpsimd.memset(new_rows[:, :], 0.0).then_inc(const_made, 1)
            with pool.Fori(0, NT) as t:
                hold(pool, pool_on, m_ready, t + 1)
                nc.gpsimd.tensor_copy(bias[:, :, 0:P], bias_prev[:, :, :]).then_inc(bias_set, 1)
            pool.wait_ge(bias_set, NT + 1)
            nc.gpsimd.memset(q_blocks, 0.0).then_inc(const_made, 1)
            pool.wait_ge(pT_ready, NT)
            nc.gpsimd.memset(probs.rearrange("p a b -> p (a b)")[:, 2 * CONV:2 * CONV + D], 0.0).then_inc(zero_ready, 1)

        A_STEPS = 11

        @block.scalar
        def _(act):
            def norm_and_gate(t, R, steps):
                hold(act, act_on, x_landed, (t + 1) * 16)
                steps.link(nc.scalar.activation(squares[0:R, :], x_in[0:R, :], ACT.Square, accum_out=ssq[0:R, :]))
                nc.scalar.activation(rms[0:R, :], ssq[0:R, :], ACT.Sqrt, bias=eps[0:R, :], scale=1.0 / D).then_inc(squared, 1)
                act.wait_ge(z_ready, t + 1)
                nc.scalar.activation(squares[0:R, 0:QW + KW], ZB[0:R, 0:QW + KW], ACT.Square).then_inc(qk_squared, 1)
                if R == NB:
                    act.wait_ge(tail_stored, 48)
                nc.scalar.activation(vwin[0:R, 1, :], ZB[0:R, ZV:ZV + KW], ACT.Copy).then_inc(v_ready, 1)
                nc.scalar.activation(gate[0:R, :], ZB[0:R, ZG:ZG + CONV], ACT.Sigmoid).then_inc(sig_ready, 1)
                act.wait_ge(qk_summed, t + 1)
                nc.scalar.activation(rms10[0:R, :], ss10[0:R, :], ACT.Sqrt, bias=eps[0:R, :], scale=1.0 / HD).then_inc(qk_rms, 1)

            def conv_affine(t, R, steps):
                act.wait_ge(cvar_ready, t + 1)
                nc.scalar.activation(rms_c[0:R, :], mv[0:R, 1:2], ACT.Sqrt, bias=eps[0:R, :]).then_inc(crms_ready, 1)
                act.wait_ge(lnT_ready, t + 1)
                for c in range(CT):
                    scale, shift = chan[:, c, TAPS + 1:TAPS + 2], chan[:, c, TAPS + 2:TAPS + 3]
                    src = TB[:, BANK + c * P:BANK + c * P + R]
                    nc.scalar.activation(conv_y[:, c, 0:R], src, ACT.Identity, bias=shift, scale=scale)
                    last = nc.scalar.activation(conv_s[:, c, 0:R], src, ACT.Sigmoid, bias=shift, scale=scale)
                last.then_inc(cy_ready, 1)

            act.wait_ge(cols_T, 1)
            nc.scalar.activation(chan[:, :, :], TB[:, 0:CT * P].rearrange("p (c j) -> p c j", c=CT)[:, :, 0:TAPS + 3], ACT.Copy).then_inc(cols_made, 1)
            nc.scalar.activation(norm_cols[:, :, :], TB[:, BANK:BANK + 2 * KD].rearrange("p (a k) -> p a k", a=2), ACT.Copy).then_inc(cols_made, 1)
            act.wait_ge(const_made, 3)
            act.wait_ge(window_cleared, 3)
            with act.Fori(0, NT) as t:
                steps = Chain(act, act_step, t * A_STEPS)
                norm_and_gate(t, P, steps)
                act.wait_ge(qkT_ready, t + 1)
                nc.scalar.activation(qT[:, :, :], TB[:, 0:QW].rearrange("p (i t) -> p i t", t=P), ACT.Copy)
                nc.scalar.activation(kwin[:, P:WIN], TB[:, QW:QW + P], ACT.Copy).then_inc(qk_copied, 1)
                act.wait_ge(m_ready, t + 1)
                for h in range(HEADS):
                    steps.link(nc.scalar.activation(probs[:, h, :], probs[:, h, :], ACT.Exp, bias=ntop[:, h:h + 1],
                                                    accum_out=den[:, h:h + 1]))
                nc.scalar.activation(esink[:, :], dsink[:, :], ACT.Exp).then_inc(e_ready, 1)
                act.wait_ge(pT_ready, t + 1)
                nc.scalar.activation(probsT[:, :, :], TB[:, :].rearrange("p (a b) -> p a b", b=P), ACT.Copy).then_inc(pT_copied, 1)
                act.wait_ge(att_ready, t + 1)
                nc.scalar.activation(mixedT[:, 0:GROUP, :], ZB[:, 0:QW].rearrange("p (i t) -> p i t", t=P), ACT.Copy).then_inc(att_copied, 1)
                steps.link(nc.scalar.activation(kwin[:, 0:P], kwin[:, P:WIN], ACT.Copy))
                steps.link(nc.scalar.activation(vwin[:, 0, :], vwin[:, 1, :], ACT.Copy))
                conv_affine(t, P, steps)
                assert steps.n == A_STEPS, steps.n

            t, R, rows = NT, NB, HEADS * NB
            steps = Chain(act, act_step, t * A_STEPS)
            norm_and_gate(t, R, steps)
            act.wait_ge(qkT_ready, t + 1)
            act.wait_ge(const_made, 4)
            for kv in range(KV):
                half = slice(kv * HD, (kv + 1) * HD)
                nc.scalar.activation(q_blocks[half, :].rearrange("p (b s) -> p b s", s=72)[:, :, kv * GROUP:(kv + 1) * GROUP],
                                     s_qT[half, :, 0:NB].rearrange("p i b -> p b i"), ACT.Copy)
            act.wait_ge(sbias_in, NB * 16)
            nc.scalar.activation(keysT[:, :, P], TB[:, QW:QW + NB], ACT.Copy).then_inc(kT_new, 1)
            act.wait_ge(kT_ready, 1)
            nc.scalar.activation(keysT[:, :, 0:P], ZB[:, 0:NB * P].rearrange("p (b k) -> p b k", k=P), ACT.Copy).then_inc(kT_copied, 1)
            act.wait_ge(gluT_ready, t + 1)
            act.wait_ge(hT_free, 1)
            for g in range(2):
                nc.scalar.activation(hist[:, :, 4 * g:4 * g + 4, 0:HIST],
                                     ZB[:, 2 * BANK + g * CT * P:2 * BANK + (g + 1) * CT * P].rearrange("p (c k) -> p c k", c=CT)
                                     [:, :, 0:4 * HIST].rearrange("p c (b j) -> p c b j", j=HIST), ACT.Copy)
            nc.scalar.activation(hist[:, :, :, HIST], TB[:, 2 * BANK:2 * BANK + CT * P].rearrange("p (c k) -> p c k", c=CT)[:, :, 0:NB],
                                 ACT.Copy).then_inc(hist_ready, 1)
            act.wait_ge(m_ready, t + 1)
            steps.link(nc.scalar.activation(s_probs, s_probs, ACT.Exp, bias=ntop[0:rows, 0:1], accum_out=den[0:rows, 0:1]))
            nc.scalar.activation(esink[0:rows, 0:1], dsink[0:rows, 0:1], ACT.Exp).then_inc(e_ready, 1)
            act.wait_ge(pT_ready, t + 1)
            nc.scalar.activation(s_probsT, TB[:, BANK:BANK + rows], ACT.Copy)
            nc.scalar.activation(new_T[0:NB, 0:rows], TB[0:NB, 2 * BANK:2 * BANK + rows], ACT.Copy).then_inc(pT_copied, 1)
            act.wait_ge(att_ready, t + 1)
            for kv in range(KV):
                half = slice(kv * HD, (kv + 1) * HD)
                last = nc.scalar.activation(mixedT[half, 0:GROUP, 0:NB],
                                            TB[half, 3 * BANK:3 * BANK + rows].rearrange("p (b h) -> p h b", h=HEADS)
                                            [:, kv * GROUP:(kv + 1) * GROUP, :], ACT.Copy)
            last.then_inc(att_copied, 1)
            conv_affine(t, R, steps)

        D_STEPS = 43
        TT = nc.vector.tensor_tensor

        @block.vector
        def _(dve):
            def norm_and_gate(t, R, steps):
                dve.wait_ge(squared, t + 1)
                steps.link(nc.vector.reciprocal(rstd[0:R, :], rms[0:R, :]))
                nc.vector.tensor_scalar(xn[0:R, :], x_in[0:R, :], rstd[0:R, :], None, ALU.mult).then_inc(xn_ready, 1)
                dve.wait_ge(xT_ready, t + 1)
                TT(hT[:, :, 0:R], TB[:, 0:D].rearrange("p (k t) -> p k t", k=KD)[:, :, 0:R],
                   norm_cols[:, 0, :].unsqueeze(2).to_broadcast([P, KD, R]), ALU.mult).then_inc(hT_ready, 1)
                dve.wait_ge(qk_squared, t + 1)
                nc.vector.tensor_reduce(ss10[0:R, :], squares[0:R, 0:QW + KW].rearrange("p (h d) -> p h d", d=HD), AX.X,
                                        ALU.add).then_inc(qk_summed, 1)
                dve.wait_ge(qk_rms, t + 1)
                steps.link(nc.vector.reciprocal(rstd10[0:R, :], rms10[0:R, :]))
                if R == NB:
                    dve.wait_ge(tail_stored, 48)
                q_out = qk[0:R, 0:QW].rearrange("p (i kv d) -> p kv i d", kv=KV, i=GROUP)
                k_out = qk[0:R, QW:].rearrange("p (h d) -> p h d", d=HD)
                q_by_head = qk[0:R, 0:QW].rearrange("p (h d) -> p h d", d=HD)
                TT(q_out, ZB[0:R, 0:QW].rearrange("p (kv i d) -> p kv i d", kv=KV, i=GROUP),
                   rstd10[0:R, 0:HEADS].rearrange("p (kv i) -> p kv i", kv=KV).unsqueeze(3).to_broadcast([R, KV, GROUP, HD]),
                   ALU.mult)
                steps.link(TT(k_out, ZB[0:R, ZK:ZV].rearrange("p (h d) -> p h d", d=HD),
                              rstd10[0:R, HEADS:].unsqueeze(2).to_broadcast([R, KV, HD]), ALU.mult))
                TT(q_by_head, q_by_head, qg[0:R, :].unsqueeze(1).to_broadcast([R, HEADS, HD]), ALU.mult)
                TT(k_out, k_out, kg[0:R, :].unsqueeze(1).to_broadcast([R, KV, HD]), ALU.mult).then_inc(qk_ready, 1)
                dve.wait_ge(sig_ready, t + 1)
                TT(glu[0:R, :], ZB[0:R, ZA:ZA + CONV], gate[0:R, :], ALU.mult).then_inc(glu_ready, 1)

            def conv_norm_and_residual(t, R, steps):
                dve.wait_ge(c_ready, t + 1)
                steps.link(nc.vector.bn_stats(bn6[0:R, :], TB[0:R, 0:CONV]))
                hold(dve, dve_on, dve_step, steps.base + steps.n)
                nc.vector.bn_aggr(mv[0:R, :], bn6[0:R, :]).then_inc(cvar_ready, 1)
                dve.wait_ge(crms_ready, t + 1)
                steps.link(nc.vector.reciprocal(rstd_c[0:R, :], rms_c[0:R, :]))
                nc.vector.tensor_scalar(xn[0:R, 0:CONV], TB[0:R, 0:CONV], mv[0:R, 0:1], rstd_c[0:R, :], ALU.subtract,
                                        ALU.mult).then_inc(ln_ready, 1)
                dve.wait_ge(cy_ready, t + 1)
                TT(mixedT[:, GROUP:KD, 0:R], conv_y[:, :, 0:R], conv_s[:, :, 0:R], ALU.mult).then_inc(mix_ready, 1)
                dve.wait_ge(o_ready, t + 1)
                dve.wait_ge(res_landed, (t + 1) * 16)
                TT(x_res[0:R, :], ZB[0:R, 0:D], x_res[0:R, :], ALU.add).then_inc(x1_ready, 1)

            dve.wait_ge(cols_made, 2)
            dve.wait_ge(const_in, (3 + NB) * 16)
            dve.wait_ge(window_cleared, 3)
            dve.wait_ge(const_made, 3)
            with dve.Fori(0, NT) as t:
                steps = Chain(dve, dve_step, t * D_STEPS)
                norm_and_gate(t, P, steps)
                dve.wait_ge(gluT_ready, t + 1)
                steps.link(nc.vector.tensor_copy(gluT[:, :, HIST:HIST + P], TB[:, 2 * BANK:2 * BANK + CT * P].rearrange("p (c t) -> p c t", c=CT)))
                dve.wait_ge(s_ready, t + 1)
                dve.wait_ge(bias_set, t + 1)
                flat = probs.rearrange("p h k -> p (h k)")
                steps.link(nc.vector.scalar_tensor_tensor(out=flat, in0=ZB[:, :], scalar=HD ** -0.5,
                                                          in1=bias.rearrange("p h k -> p (h k)"), op0=ALU.mult, op1=ALU.add))
                steps.link(nc.vector.tensor_reduce(top[:, :], probs[:, :, :], AX.X, ALU.max))
                steps.link(TT(top[:, :], top[:, :], sinks[:, :], ALU.max))
                steps.link(TT(dsink[:, :], sinks[:, :], top[:, :], ALU.subtract))
                nc.vector.tensor_scalar(ntop[:, :], top[:, :], -1.0, None, ALU.mult).then_inc(m_ready, 1)
                dve.wait_ge(e_ready, t + 1)
                steps.link(TT(den[:, :], den[:, :], esink[:, :], ALU.add))
                steps.link(nc.vector.reciprocal(rden[:, :], den[:, :]))
                TT(probs[:, :, :], probs[:, :, :], rden[:, :].unsqueeze(2).to_broadcast([P, HEADS, WIN]), ALU.mult).then_inc(p_ready, 1)
                for j in range(TAPS):
                    for c in range(CT):
                        src, w = gluT[:, c, j:j + P], chan[:, c, j:j + 1]
                        if j == 0:
                            last = nc.vector.tensor_scalar(acc[:, c, :], src, w, chan[:, c, TAPS:TAPS + 1], ALU.mult, ALU.add)
                        else:
                            last = nc.vector.scalar_tensor_tensor(out=acc[:, c, :], in0=src, scalar=w, in1=acc[:, c, :],
                                                                  op0=ALU.mult, op1=ALU.add)
                    if j < TAPS - 1:
                        steps.link(last)
                last.then_inc(conv_done, 1)
                steps.link(nc.vector.tensor_copy(gluT[:, :, 0:HIST], gluT[:, :, P:P + HIST]))
                conv_norm_and_residual(t, P, steps)
                assert steps.n == D_STEPS, steps.n

            t, R, rows = NT, NB, HEADS * NB
            steps = Chain(dve, dve_step, t * D_STEPS)
            norm_and_gate(t, R, steps)
            dve.wait_ge(s_ready, t + 1)
            dve.wait_ge(sbias_in, NB * 16)
            s0 = sink_rows[0:rows, :]
            steps.link(nc.vector.scalar_tensor_tensor(out=s_probs, in0=TB[0:rows, 0:SKEYS], scalar=HD ** -0.5,
                                                      in1=sbias[0:rows, 0:SKEYS], op0=ALU.mult, op1=ALU.add))
            steps.link(nc.vector.tensor_reduce(top[0:rows, 0:1], s_probs, AX.X, ALU.max))
            steps.link(TT(top[0:rows, 0:1], top[0:rows, 0:1], s0, ALU.max))
            steps.link(TT(dsink[0:rows, 0:1], s0, top[0:rows, 0:1], ALU.subtract))
            nc.vector.tensor_scalar(ntop[0:rows, 0:1], top[0:rows, 0:1], -1.0, None, ALU.mult).then_inc(m_ready, 1)
            dve.wait_ge(hist_ready, 1)
            steps.link(TT(prod, hist, chan[:, :, 0:TAPS].unsqueeze(2).to_broadcast([P, CT, NB, TAPS]), ALU.mult))
            steps.link(nc.vector.tensor_reduce(acc[:, :, 0:NB], prod, AX.X, ALU.add))
            TT(acc[:, :, 0:NB], acc[:, :, 0:NB], chan[:, :, TAPS:TAPS + 1].to_broadcast([P, CT, NB]), ALU.add).then_inc(conv_done, 1)
            dve.wait_ge(e_ready, t + 1)
            steps.link(TT(den[0:rows, 0:1], den[0:rows, 0:1], esink[0:rows, 0:1], ALU.add))
            steps.link(nc.vector.reciprocal(rden[0:rows, 0:1], den[0:rows, 0:1]))
            steps.link(nc.vector.tensor_scalar(s_probs, s_probs, rden[0:rows, 0:1], None, ALU.mult))
            nc.vector.tensor_scalar(new_rows[0:rows, 0:NB], own[0:rows, :], s_probs[:, P:P + 1], None, ALU.mult).then_inc(p_ready, 1)
            conv_norm_and_residual(t, R, steps)

        @block.tensor
        def _(pe):
            def transpose(out, src, rows):
                return nc.tensor.transpose(out, src, ident[0:rows, 0:rows])

            def project(t, R):
                pe.wait_ge(xn_ready, t + 1)
                for k in range(KD):
                    last = transpose(TB[:, k * P:k * P + R], xn[0:R, k * P:(k + 1) * P], R)
                last.then_inc(xT_ready, 1)
                pe.wait_ge(hT_ready, t + 1)
                for c in range(0, DIN, BANK):
                    n = min(BANK, DIN - c)
                    for k in range(KD):
                        last = nc.tensor.matmul(ZB[0:R, c:c + n], hT[:, k, 0:R], win_w[:, k, c:c + n], start=(k == 0),
                                                stop=(k == KD - 1))
                last.then_inc(z_ready, 1)
                pe.wait_ge(qk_ready, t + 1)
                for i in range(GROUP):
                    transpose(TB[:, i * P:i * P + R], qk[0:R, i * P:(i + 1) * P], R)
                transpose(TB[:, QW:QW + R], qk[0:R, QW:QW + KW], R).then_inc(qkT_ready, 1)
                pe.wait_ge(glu_ready, t + 1)
                for c in range(CT):
                    last = transpose(TB[:, 2 * BANK + c * P:2 * BANK + c * P + R], glu[0:R, c * P:(c + 1) * P], R)
                last.then_inc(gluT_ready, 1)

            def conv_norm_and_out(t, R):
                pe.wait_ge(conv_done, t + 1)
                pe.wait_ge(pT_copied, t + 1)
                for c in range(CT):
                    last = transpose(TB[0:R, c * P:(c + 1) * P], acc[:, c, 0:R], P)
                last.then_inc(c_ready, 1)
                pe.wait_ge(ln_ready, t + 1)
                for c in range(CT):
                    last = transpose(TB[:, BANK + c * P:BANK + c * P + R], xn[0:R, c * P:(c + 1) * P], R)
                last.then_inc(lnT_ready, 1)
                pe.wait_ge(mix_ready, t + 1)
                pe.wait_ge(att_copied, t + 1)
                for c in range(0, D, BANK):
                    for k in range(KD):
                        last = nc.tensor.matmul(ZB[0:R, c:c + BANK], mixedT[:, k, 0:R], wout_w[:, k, c:c + BANK],
                                                start=(k == 0), stop=(k == KD - 1))
                last.then_inc(o_ready, 1)

            pe.wait_ge(const_made, 1)
            pe.wait_ge(rows_in, 6 * 16)
            for c in range(CT):
                transpose(TB[:, c * P:c * P + TAPS + 3], chan_rows[0:TAPS + 3, c * P:(c + 1) * P], TAPS + 3)
            transpose(TB[:, BANK:BANK + 2 * KD], norm_rows[0:2 * KD, :], 2 * KD).then_inc(cols_T, 1)
            pe.wait_ge(cols_made, 2)
            pe.wait_ge(weights_in, KD * 16)
            pe.wait_ge(out_w_in, 3 * 16)
            with pe.Fori(0, NT) as t:
                project(t, P)
                pe.wait_ge(qk_copied, t + 1)
                for h in range(HEADS):
                    kv, i = divmod(h, GROUP)
                    half = slice(kv * HD, (kv + 1) * HD)
                    last = nc.tensor.matmul(ZB[:, h * WIN:(h + 1) * WIN], qT[half, i, :], kwin[half, :], start=True, stop=True)
                last.then_inc(s_ready, 1)
                pe.wait_ge(p_ready, t + 1)
                for h in range(HEADS):
                    for blk in range(2):
                        s = 2 * h + blk
                        last = transpose(TB[:, s * P:(s + 1) * P], probs[:, h, blk * P:(blk + 1) * P], P)
                last.then_inc(pT_ready, 1)
                pe.wait_ge(pT_copied, t + 1)
                for h in range(HEADS):
                    kv, i = divmod(h, GROUP)
                    half = slice(kv * HD, (kv + 1) * HD)
                    for blk in range(2):
                        last = nc.tensor.matmul(ZB[half, i * P:(i + 1) * P], vwin[:, blk, half], probsT[:, 2 * h + blk, :],
                                                start=(blk == 0), stop=(blk == 1))
                last.then_inc(att_ready, 1)
                conv_norm_and_out(t, P)

            t, rows = NT, HEADS * NB
            project(t, NB)
            pe.wait_ge(samples_in, 4 * 16)
            for b in range(NB):
                last = transpose(ZB[:, b * P:(b + 1) * P], k_rows[:, b, :], P)
            last.then_inc(kT_ready, 1)
            for g in range(2):
                for c in range(CT):
                    at = 2 * BANK + (g * CT + c) * P
                    last = transpose(ZB[:, at:at + 4 * HIST], st_rows[0:4 * HIST, g, c * P:(c + 1) * P], 4 * HIST)
            last.then_inc(hT_free, 1)
            pe.wait_ge(kT_copied, 1)
            pe.wait_ge(hist_ready, 1)
            for b in range(NB):
                last = nc.tensor.matmul(TB[0:rows, 0:SKEYS], q_blocks[:, b * rows:(b + 1) * rows], keysT[:, b, :],
                                        start=(b == 0), stop=(b == NB - 1))
            last.then_inc(s_ready, 1)
            pe.wait_ge(p_ready, t + 1)
            transpose(TB[:, BANK:BANK + rows], s_probs[:, 0:P], rows)
            transpose(TB[:, 2 * BANK:2 * BANK + rows], new_rows[0:rows, :], rows).then_inc(pT_ready, 1)
            pe.wait_ge(pT_copied, t + 1)
            out = TB[:, 3 * BANK:3 * BANK + rows]
            nc.tensor.matmul(out, vwin[0:NB, 1, :], new_T[0:NB, 0:rows], start=True, stop=False)
            for b in range(NB):
                cols = slice(b * HEADS, (b + 1) * HEADS)
                last = nc.tensor.matmul(out[:, cols], v_rows[:, b, :], s_probsT[:, cols], start=False, stop=(b == NB - 1))
            last.then_inc(att_ready, 1)
            conv_norm_and_out(t, NB)


def experts(nc, ident, eps, norm_cols, arena, x1, p_prompt, p_sample, norm_ffn, peer_wq, sub_keys, peer_u, peer_v,
            w_ple_proj, w_ple_gate, y_prompt, y_sample):
    with ExitStack() as ctx:
        def sem(name):
            return ctx.enter_context(nc.semaphore(name))

        QB = ctx.enter_context(nc.psum_tensor("QB", [P, 4 * BANK], F32))
        TP = ctx.enter_context(nc.psum_tensor("TP", [P, 2 * BANK], F32))
        VA = ctx.enter_context(nc.psum_tensor("VA", [P, 2 * BANK], F32))

        take = carve(arena, 0)
        wq = take(KD, 2 * PH * P)
        w_gate = take(KD, D)
        w_ple = take(DPLE // P, D)
        rows = take(RING, D)
        diag = take(RING, P)
        xq = take(D)
        h = take(D)
        xf = take(D)
        h3 = take(D)
        ple = take(D)
        hT = take(KD, P)
        q_cand = take(2 * PH, P)
        scores = take(2 * PH, NKEY)
        match = take(CHOICES, TOPK)
        gain = take(D)
        keysT = take(2, NKEY)
        key_rows = take(2, P)
        p_rows = take(DPLE)
        pT = take(2, P)
        top = take(2 * PH, TOPK)
        top_i = take(2 * PH, TOPK).bitcast(U32)
        top_f = take(2 * PH, TOPK)
        best = take(PH, TOPK)
        best_i = take(PH, TOPK).bitcast(U32)
        part_i = take(CHOICES).bitcast(U32)
        part = take(CHOICES)
        first_key = take(CHOICES)
        second_key = take(CHOICES)
        chosen = take(CHOICES).bitcast(U32)
        current = take(CHOICES).bitcast(U32)
        idx = take(2, RING).bitcast(U32)
        dots16 = take(2 * RING)
        dots = take(CHOICES)
        gelu = take(CHOICES)
        weights = take(CHOICES)
        gates = take(CHOICES)
        sums = take(PH)
        iota16 = take(TOPK)
        small = take(8)
        eye8 = take(NB, NB)
        w_cols = take(NB, NB)
        idxT = take(NB).bitcast(U32)
        gatesT = take(NB)
        dots8, gelu8, w8 = take(NB), take(NB), take(NB)
        assert take.at[0] <= ARENA, take.at[0]
        h_bc = wq.rearrange("p k n -> p (k n)")[:, 0:NB * D].rearrange("p (n d) -> p n d", d=D)
        cand = q_cand.rearrange("p a b -> p (a b)").rearrange("p (h c) -> p h c", c=TOPK * TOPK)
        q_flat = q_cand.rearrange("p a b -> p (a b)")
        best_flat = best.rearrange("p h k -> p (h k)")
        ssq, rms, rstd, ssq2, rms2, rstd2 = (small[:, i:i + 1] for i in range(6))

        choice_dram = nc.dram_tensor("sample_choices", (NB, CHOICES), U32, kind="Internal").ap()
        gates_dram = nc.dram_tensor("sample_gates", (NB, CHOICES), F32, kind="Internal").ap()
        h_dram = nc.dram_tensor("sample_h", (NB, D), F32, kind="Internal").ap()

        wq_in, w_fin_in, const_in, const_made = sem("wq_in"), sem("w_finish_in"), sem("b_const_in"), sem("b_const_made")
        keysT_ready, keysT_copied = sem("keysT_ready"), sem("keysT_copied")
        xq_landed, xq_rms, hn_ready, hnT_ready, hT_copied = sem("xq_landed"), sem("xq_rms"), sem("hn_ready"), sem("hnT_ready"), sem("hT_copied")
        q_ready, q_copied, sc_ready, sc_copied = sem("q_ready"), sem("q_copied"), sem("key_scores_ready"), sem("key_scores_copied")
        chosen_ready, chosen_taken, gate_shifted, gexp_ready = sem("chosen_ready"), sem("chosen_taken"), sem("gate_shifted"), sem("gate_exp_ready")
        h_copied, idx_copied = sem("h_copied"), sem("idx_copied")
        landed = [sem(f"rows_landed{i}") for i in range(RING)]
        u_used, v_used, dots_copied = sem("u_rows_used"), sem("v_rows_used"), sem("dots_copied")
        gelu_ready, weights_ready, diag_ready = sem("gelu_ready"), sem("weights_ready"), sem("diag_ready")
        xf_landed, p_landed, x2_ready, x2_rms, h3_ready = sem("xf_landed"), sem("p_landed"), sem("x2_ready"), sem("x2_rms"), sem("h3_ready")
        h3T_ready, h3T_copied, pT_ready, pT_copied = sem("h3T_ready"), sem("h3T_copied"), sem("pT_ready"), sem("pT_copied")
        fin_ready, fin_copied, y_ready, y_stored = sem("finish_products_ready"), sem("finish_copied"), sem("y_ready"), sem("y_stored")
        s_stored, hbc_landed, idxT_landed, gT_landed = (sem(n) for n in ("sample_scratch_stored", "sample_h_landed", "sample_idx_landed", "sample_gates_landed"))
        g8_ready, cols_ready = sem("sample_gates_ready"), sem("weight_cols_ready")
        act_q, act_f, dve_q, dve_f, dve_k, dve_w, dve_on, act_on, pool_on = (sem(n) for n in (
            "act_rank_step", "act_finish_step", "dve_rank_step", "dve_finish_step", "dve_choose_step", "dve_weigh_step",
            "b_dve_on", "b_act_on", "b_pool_on"))
        pool_step = sem("b_pool_step")

        def hold(eng, carrier, s, value):
            eng.wait_ge(s, value)
            eng.sem_inc(carrier, 1)

        block = ctx.enter_context(nc.Block())

        @block.sync
        def _(sp):
            def load_rank(q):
                sp.wait_ge(h_copied, q)
                sp.dma_start(xq, x1[bass.ds(q, 1), :, :].rearrange("o p d -> (o p) d")).then_inc(xq_landed, 16)

            def load_finish(f, first=False):
                if not first:
                    sp.wait_ge(y_stored, f * 16)
                    sp.wait_ge(pT_ready, f)
                sp.dma_start(xf, x1[bass.ds(f, 1), :, :].rearrange("o p d -> (o p) d")).then_inc(xf_landed, 16)
                sp.dma_start(p_rows, p_prompt[0, bass.ds(f * P, P), :]).then_inc(p_landed, 16)

            def store(f):
                sp.wait_ge(y_ready, f + 1)
                sp.dma_start(y_prompt[0, bass.ds(f * P, P), :], xf).then_inc(y_stored, 16)

            sp.dma_start(xq, x1[0]).then_inc(xq_landed, 16)
            sp.dma_start(gain, norm_ffn[0].partition_broadcast(P)).then_inc(const_in, 16)
            sp.dma_start(key_rows, sub_keys.rearrange("s k d -> k s d")).then_inc(const_in, 16)
            for k in range(KD):
                sp.dma_start(wq[:, k, :], peer_wq[k * P:(k + 1) * P, :]).then_inc(wq_in, 16)
            sp.dma_start(w_gate, w_ple_gate.rearrange("(k p) n -> p k n", p=P)).then_inc(w_fin_in, 16)
            sp.dma_start(w_ple, w_ple_proj.rearrange("(k p) n -> p k n", p=P)).then_inc(w_fin_in, 16)
            load_rank(1)
            load_finish(0, first=True)
            with sp.Fori(1, NT) as t:
                load_rank(t + 1)
                store(t - 1)
                load_finish(t)
            sp.wait_ge(hn_ready, NT + 1)
            sp.dma_start(h_dram, xq[0:NB, :]).then_inc(s_stored, 16)
            sp.wait_ge(q_ready, NT + 1)
            sp.wait_ge(s_stored, 16)
            for n in range(NB):
                sp.dma_start(h_bc[:, n, :], h_dram[n].partition_broadcast(P)).then_inc(hbc_landed, 16)
            sp.wait_ge(chosen_ready, NT + 1)
            sp.dma_start(choice_dram, chosen[0:NB, :]).then_inc(s_stored, 16)
            sp.wait_ge(s_stored, 2 * 16)
            sp.dma_start(idxT, choice_dram.rearrange("n c -> c n"), allow_slow_non_contiguous=True).then_inc(idxT_landed, 16)
            sp.wait_ge(g8_ready, 1)
            sp.dma_start(gates_dram, gates[0:NB, :]).then_inc(s_stored, 16)
            sp.wait_ge(s_stored, 3 * 16)
            sp.dma_start(gatesT, gates_dram.rearrange("n c -> c n"), allow_slow_non_contiguous=True).then_inc(gT_landed, 16)
            store(NT - 1)
            sp.wait_ge(y_stored, NT * 16)
            sp.wait_ge(pT_ready, NT)
            sp.dma_start(xf[0:NB, :], x1[NT, 0:NB, :]).then_inc(xf_landed, 16)
            sp.dma_start(p_rows[0:NB, :], p_sample[:, 0, :]).then_inc(p_landed, 16)
            sp.wait_ge(y_ready, NT + 1)
            sp.dma_start(y_sample[:, 0, :], xf[0:NB, :]).then_inc(y_stored, 16)
            sp.wait_ge(y_stored, (NT + 1) * 16)

        @block.gpsimd
        def _(pool):
            nc.gpsimd.iota(iota16, [[1, TOPK]], base=0, channel_multiplier=0,
                           allow_small_or_imprecise_dtypes=True).then_inc(const_made, 1)
            steps = Chain(pool, pool_step)
            steps.link(nc.gpsimd.memset(eye8, 0.0))
            nc.gpsimd.affine_select(out=eye8, in_=eye8, compare_op=ALU.not_equal, fill=1.0, base=0,
                                    pattern=[[1, NB], [-1, NB]], channel_multiplier=0).then_inc(const_made, 1)

            def gather(table, i, index):
                nc.gpsimd.indirect_dma_start(rows[:, i, :], None, table, bass.IndirectOffsetOnAxis(ap=index, axis=0)
                                             ).then_inc(landed[i], 16)

            def gather_pair(t, pair, table, number, before, before_at, after, after_at):
                for half in range(2):
                    nc.gpsimd.tensor_copy(idx[:, half, :], current[:, bass.ds((2 * pair + half) * RING, RING)]
                                          ).then_inc(idx_copied, 1)
                    hold(pool, pool_on, idx_copied, number + half + 1)
                    for i in range(RING):
                        if half == 0 and before is not None:
                            hold(pool, pool_on, before, before_at + i + 1)
                        if half == 1:
                            hold(pool, pool_on, after, after_at + i + 1)
                        gather(table, i, idx[:, half, i:i + 1])

            def tile(t, first):
                hold(pool, pool_on, chosen_ready, t + 1)
                nc.gpsimd.tensor_copy(current, chosen).then_inc(chosen_taken, 1)
                hold(pool, pool_on, chosen_taken, t + 1)
                at = t * CHOICES
                n = t * 2 * CHOICES // RING
                gather_pair(t, 0, peer_u, n, None if first else v_used, at - RING, u_used, at)
                with pool.Fori(1, 8) as pair:
                    gather_pair(t, pair, peer_u, n + 2 * pair, u_used, at + (2 * pair - 1) * RING, u_used, at + 2 * pair * RING)
                n += CHOICES // RING
                gather_pair(t, 0, peer_v, n, u_used, at + CHOICES - RING, v_used, at)
                with pool.Fori(1, 8) as pair:
                    gather_pair(t, pair, peer_v, n + 2 * pair, v_used, at + (2 * pair - 1) * RING, v_used, at + 2 * pair * RING)

            tile(0, True)
            with pool.Fori(1, NT) as t:
                tile(t, False)
            pool.wait_ge(idxT_landed, 16)
            for n in range(NB):
                pool.wait_ge(v_used, NT * CHOICES - RING + n + 1)
                gather(peer_u, n, idxT[:, n:n + 1])
            for n in range(NB):
                pool.wait_ge(u_used, NT * CHOICES + n + 1)
                gather(peer_v, n, idxT[:, n:n + 1])

        ACT_Q, ACT_F = 1, 1

        @block.scalar
        def _(act):
            def rank(q):
                steps = Chain(act, act_q, q * ACT_Q)
                hold(act, act_on, xq_landed, (q + 1) * 16)
                steps.link(nc.scalar.activation(q_flat[:, 0:D], xq, ACT.Square, accum_out=ssq))
                nc.scalar.activation(rms, ssq, ACT.Sqrt, bias=eps[:, :], scale=1.0 / D).then_inc(xq_rms, 1)
                act.wait_ge(hnT_ready, q + 1)
                nc.scalar.activation(hT, TP[:, :].rearrange("p (k t) -> p k t", t=P), ACT.Copy).then_inc(hT_copied, 1)
                act.wait_ge(q_ready, q + 1)
                nc.scalar.activation(q_flat, QB[:, :], ACT.Copy).then_inc(q_copied, 1)
                act.wait_ge(sc_ready, q + 1)
                nc.scalar.activation(scores.rearrange("p a b -> p (a b)"), QB[:, :], ACT.Copy).then_inc(sc_copied, 1)
                assert steps.n == ACT_Q

            def finish(f, R):
                steps = Chain(act, act_f, f * ACT_F)
                act.wait_ge(x2_ready, f + 1)
                steps.link(nc.scalar.activation(ple[0:R, :], xf[0:R, :], ACT.Square, accum_out=ssq2[0:R, :]))
                nc.scalar.activation(rms2[0:R, :], ssq2[0:R, :], ACT.Sqrt, bias=eps[0:R, :], scale=1.0 / D).then_inc(x2_rms, 1)
                act.wait_ge(pT_ready, f + 1)
                nc.scalar.activation(pT[:, :, 0:R], QB[:, 0:2 * P].rearrange("p (k t) -> p k t", t=P)[:, :, 0:R],
                                     ACT.Copy).then_inc(pT_copied, 1)
                act.wait_ge(fin_ready, f + 1)
                nc.scalar.activation(h3[0:R, :], QB[0:R, D:2 * D], ACT.Sigmoid)
                nc.scalar.activation(ple[0:R, :], QB[0:R, 0:D], ACT.Copy).then_inc(fin_copied, 1)
                assert steps.n == ACT_F

            def exponentials(q):
                act.wait_ge(gate_shifted, q + 1)
                nc.scalar.activation(gates, gates, ACT.Exp).then_inc(gexp_ready, 1)

            def diagonals(t, pair, first):
                for s in range(2 * RING):
                    i = s % RING
                    if not (first and s < RING):
                        hold(act, act_on, v_used, t * CHOICES + pair * 2 * RING + s - RING + 1)
                    nc.scalar.activation(diag[:, i, :], ident[:, :], ACT.Copy,
                                         scale=weights[:, bass.ds(pair * 2 * RING + s, 1)]).then_inc(diag_ready, 1)

            def tile(t, first):
                if not first:
                    finish(t - 1, P)
                rank(t + 1)
                act.wait_ge(dots_copied, (t + 1) * 8)
                nc.scalar.activation(gelu, dots, ACT.Gelu).then_inc(gelu_ready, 1)
                hold(act, act_on, weights_ready, t + 1)
                diagonals(t, 0, first)
                with act.Fori(1, 8) as pair:
                    diagonals(t, pair, False)
                exponentials(t + 1)

            act.wait_ge(keysT_ready, 1)
            nc.scalar.activation(keysT, TP[:, 0:2 * P].rearrange("p (s k) -> p s k", s=2), ACT.Copy).then_inc(keysT_copied, 1)
            rank(0)
            exponentials(0)
            tile(0, True)
            with act.Fori(1, NT) as t:
                tile(t, False)
            finish(NT - 1, P)
            act.wait_ge(u_used, NT * CHOICES + NB)
            nc.scalar.activation(gelu8, dots8, ACT.Gelu).then_inc(gelu_ready, 1)
            finish(NT, NB)

        DVE_Q, DVE_F, DVE_K, DVE_W = 1, 2, 21, 3
        TT = nc.vector.tensor_tensor

        @block.vector
        def _(dve):
            def normalise(q):
                steps = Chain(dve, dve_q, q * DVE_Q)
                dve.wait_ge(xq_rms, q + 1)
                steps.link(nc.vector.reciprocal(rstd, rms))
                nc.vector.scalar_tensor_tensor(out=xq, in0=xq, scalar=rstd, in1=gain, op0=ALU.mult, op1=ALU.mult).then_inc(hn_ready, 1)
                assert steps.n == DVE_Q

            def take_h(q):
                hold(dve, dve_on, hn_ready, q + 1)
                dve.wait_ge(hnT_ready, q + 1)
                nc.vector.tensor_copy(h, xq).then_inc(h_copied, 1)
                hold(dve, dve_on, h_copied, q + 1)

            def choose(q, first):
                steps = Chain(dve, dve_k, q * DVE_K)

                def step(ins):
                    steps.link(ins)
                    dve.sem_inc(dve_on, 1)

                def best16(values, n, out, out_i, lists):
                    for half in range(2):
                        part8 = slice(8 * half, 8 * half + 8)
                        for m in range(lists):
                            last = nc.vector.max(out[:, m, part8], values[:, m, :])
                        step(last)
                        for m in range(lists):
                            last = nc.vector.max_index(out_i[:, m, part8], out[:, m, part8], values[:, m, :])
                        step(last)
                        if half == 0:
                            for m in range(lists):
                                last = nc.vector.match_replace(values[:, m, :], out[:, m, part8], values[:, m, :], -3.0e38)
                            step(last)

                hold(dve, dve_on, sc_copied, q + 1)
                best16(scores, NKEY, top, top_i, 2 * PH)
                nc.vector.tensor_copy(top_f, top_i)
                pairs = cand.rearrange("p h (i j) -> p h i j", j=TOPK)
                halves = top.rearrange("p (h s) k -> p h s k", s=2)
                step(TT(pairs, halves[:, :, 0, :].unsqueeze(3).to_broadcast([P, PH, TOPK, TOPK]),
                        halves[:, :, 1, :].unsqueeze(2).to_broadcast([P, PH, TOPK, TOPK]), ALU.add))
                best16(cand, TOPK * TOPK, best, best_i, PH)
                keys = top_f.rearrange("p (h s) k -> p h s k", s=2)
                flat_i = best_i.rearrange("p h k -> p (h k)")
                for s, (op, arg, number) in enumerate(((ALU.logical_shift_right, 4, first_key), (ALU.bitwise_and, 15, second_key))):
                    steps.link(nc.vector.tensor_scalar(part_i, flat_i, arg, None, op))
                    steps.link(nc.vector.tensor_copy(part, part_i))
                    steps.link(TT(match, part.unsqueeze(2).to_broadcast([P, CHOICES, TOPK]),
                                  iota16.unsqueeze(1).to_broadcast([P, CHOICES, TOPK]), ALU.is_equal))
                    by_head = match.rearrange("p (h k) i -> p h k i", k=TOPK)
                    steps.link(TT(by_head, by_head, keys[:, :, s, :].unsqueeze(2).to_broadcast([P, PH, TOPK, TOPK]), ALU.mult))
                    steps.link(nc.vector.tensor_reduce(number, match, AX.X, ALU.add))
                if not first:
                    dve.wait_ge(chosen_taken, q)
                nc.vector.scalar_tensor_tensor(out=chosen, in0=first_key, scalar=float(NKEY), in1=second_key,
                                               op0=ALU.mult, op1=ALU.add).then_inc(chosen_ready, 1)
                TT(gates.rearrange("p (h k) -> p h k", k=TOPK), best, best[:, :, 0:1].to_broadcast([P, PH, TOPK]),
                   ALU.subtract).then_inc(gate_shifted, 1)
                assert steps.n == DVE_K, steps.n

            def dot_pair(t, pair, first):
                for s in range(2 * RING):
                    i = s % RING
                    dve.wait_ge(landed[i], (t * 2 * CHOICES // RING + 2 * pair + s // RING + 1) * 16)
                    if s == 0 and not first:
                        dve.wait_ge(dots_copied, t * 8 + pair)
                    nc.vector.tensor_tensor_reduce(out=rows[:, i, :], in0=rows[:, i, :], in1=h, scale=1.0, scalar=0.0,
                                                   op0=ALU.mult, op1=ALU.add, accum_out=dots16[:, s:s + 1]).then_inc(u_used, 1)
                hold(dve, dve_on, u_used, t * CHOICES + (pair + 1) * 2 * RING)
                nc.vector.tensor_copy(dots[:, bass.ds(pair * 2 * RING, 2 * RING)], dots16).then_inc(dots_copied, 1)

            def normalise_gates(t, R, steps):
                per_head = gates[0:R, :].rearrange("p (h k) -> p h k", k=TOPK)
                dve.wait_ge(gexp_ready, t + 1)
                steps.link(nc.vector.tensor_reduce(sums[0:R, :], per_head, AX.X, ALU.add))
                steps.link(nc.vector.reciprocal(sums[0:R, :], sums[0:R, :]))
                return TT(per_head, per_head, sums[0:R, :].unsqueeze(2).to_broadcast([R, PH, TOPK]), ALU.mult)

            def finish_norm(f, R, v_count):
                steps = Chain(dve, dve_f, f * DVE_F)
                dve.wait_ge(v_used, v_count)
                dve.wait_ge(xf_landed, (f + 1) * 16)
                TT(xf[0:R, :], VA[0:R, :], xf[0:R, :], ALU.add).then_inc(x2_ready, 1)
                dve.wait_ge(x2_rms, f + 1)
                steps.link(nc.vector.reciprocal(rstd2[0:R, :], rms2[0:R, :]))
                nc.vector.tensor_scalar(h3[0:R, :], xf[0:R, :], rstd2[0:R, :], None, ALU.mult).then_inc(h3_ready, 1)
                dve.wait_ge(h3T_ready, f + 1)
                TT(hT[:, :, 0:R], TP[:, :].rearrange("p (k t) -> p k t", t=P)[:, :, 0:R],
                   norm_cols[:, 1, :].unsqueeze(2).to_broadcast([P, KD, R]), ALU.mult).then_inc(h3T_copied, 1)

            def finish_sum(f, R):
                steps = Chain(dve, dve_f, f * DVE_F + 1)
                dve.wait_ge(fin_copied, f + 1)
                steps.link(TT(ple[0:R, :], ple[0:R, :], h3[0:R, :], ALU.mult))
                TT(xf[0:R, :], xf[0:R, :], ple[0:R, :], ALU.add).then_inc(y_ready, 1)

            def tile(t, first):
                if not first:
                    finish_norm(t - 1, P, t * CHOICES)
                normalise(t + 1)
                dot_pair(t, 0, first)
                with dve.Fori(1, 8) as pair:
                    dot_pair(t, pair, False)
                if not first:
                    finish_sum(t - 1, P)
                steps = Chain(dve, dve_w, t * DVE_W)
                steps.link(normalise_gates(t, P, steps))
                assert steps.n == DVE_W
                dve.wait_ge(gelu_ready, t + 1)
                TT(weights, gates, gelu, ALU.mult).then_inc(weights_ready, 1)
                take_h(t + 1)
                hold(dve, dve_on, weights_ready, t + 1)
                choose(t + 1, False)

            dve.wait_ge(const_in, 2 * 16)
            dve.wait_ge(const_made, 2)
            normalise(0)
            take_h(0)
            choose(0, True)
            tile(0, True)
            with dve.Fori(1, NT) as t:
                tile(t, False)
            steps = Chain(dve, dve_w, NT * DVE_W)
            normalise_gates(NT, NB, steps).then_inc(g8_ready, 1)
            finish_norm(NT - 1, P, NT * CHOICES)
            dve.wait_ge(hbc_landed, NB * 16)
            for n in range(NB):
                dve.wait_ge(landed[n], (NT * 2 * CHOICES // RING + 1) * 16)
                nc.vector.tensor_tensor_reduce(out=rows[:, n, :], in0=rows[:, n, :], in1=h_bc[:, n, :], scale=1.0, scalar=0.0,
                                               op0=ALU.mult, op1=ALU.add, accum_out=dots8[:, n:n + 1]).then_inc(u_used, 1)
            finish_sum(NT - 1, P)
            dve.wait_ge(gelu_ready, NT + 1)
            dve.wait_ge(gT_landed, 16)
            steps.link(TT(w8, gatesT, gelu8, ALU.mult))
            TT(w_cols, eye8, w8.unsqueeze(2).to_broadcast([P, NB, NB]), ALU.mult).then_inc(cols_ready, 1)
            finish_norm(NT, NB, NT * CHOICES + NB)
            finish_sum(NT, NB)

        @block.tensor
        def _(pe):
            def transpose(out, src, rows_):
                return nc.tensor.transpose(out, src, ident[0:rows_, 0:rows_])

            def rank(q):
                pe.wait_ge(hn_ready, q + 1)
                for k in range(KD):
                    last = transpose(TP[:, k * P:(k + 1) * P], xq[:, k * P:(k + 1) * P], P)
                last.then_inc(hnT_ready, 1)
                pe.wait_ge(hT_copied, q + 1)
                for m in range(2 * PH):
                    for k in range(KD):
                        last = nc.tensor.matmul(QB[:, m * P:(m + 1) * P], wq[:, k, m * P:(m + 1) * P], hT[:, k, :],
                                                start=(k == 0), stop=(k == KD - 1))
                last.then_inc(q_ready, 1)
                pe.wait_ge(q_copied, q + 1)
                for m in range(2 * PH):
                    last = nc.tensor.matmul(QB[:, m * P:(m + 1) * P], q_cand[:, m, :], keysT[:, m % 2, :], start=True, stop=True)
                last.then_inc(sc_ready, 1)

            def finish(f, R):
                pe.wait_ge(p_landed, (f + 1) * 16)
                pe.wait_ge(sc_copied, f + 2 if R == P else NT + 1)
                for k in range(2):
                    last = transpose(QB[:, k * P:k * P + R], p_rows[0:R, k * P:(k + 1) * P], R)
                last.then_inc(pT_ready, 1)
                pe.wait_ge(h3_ready, f + 1)
                for k in range(KD):
                    last = transpose(TP[:, k * P:k * P + R], h3[0:R, k * P:(k + 1) * P], R)
                last.then_inc(h3T_ready, 1)
                pe.wait_ge(h3T_copied, f + 1)
                for c in range(0, D, BANK):
                    for k in range(KD):
                        nc.tensor.matmul(QB[0:R, D + c:D + c + BANK], hT[:, k, 0:R], w_gate[:, k, c:c + BANK],
                                         start=(k == 0), stop=(k == KD - 1))
                pe.wait_ge(pT_copied, f + 1)
                for c in range(0, D, BANK):
                    for k in range(2):
                        last = nc.tensor.matmul(QB[0:R, c:c + BANK], pT[:, k, 0:R], w_ple[:, k, c:c + BANK],
                                                start=(k == 0), stop=(k == 1))
                last.then_inc(fin_ready, 1)

            def add_pair(t, pair, start=False, stop=False):
                for s in range(2 * RING):
                    i = s % RING
                    pe.wait_ge(diag_ready, t * CHOICES + pair * 2 * RING + s + 1)
                    pe.wait_ge(landed[i], ((2 * t + 1) * CHOICES // RING + 2 * pair + s // RING + 1) * 16)
                    for c in range(0, D, BANK):
                        last = nc.tensor.matmul(VA[:, c:c + BANK], diag[:, i, :], rows[:, i, c:c + BANK],
                                                start=(start and s == 0), stop=(stop and s == 2 * RING - 1))
                    last.then_inc(v_used, 1)

            def tile(t, first):
                if not first:
                    finish(t - 1, P)
                rank(t + 1)
                if not first:
                    pe.wait_ge(x2_ready, t)
                add_pair(t, 0, start=True)
                with pe.Fori(1, 7) as pair:
                    add_pair(t, pair)
                add_pair(t, 7, stop=True)

            pe.wait_ge(const_in, 2 * 16)
            for s in range(2):
                last = transpose(TP[:, s * P:(s + 1) * P], key_rows[:, s, :], P)
            last.then_inc(keysT_ready, 1)
            pe.wait_ge(keysT_copied, 1)
            pe.wait_ge(wq_in, KD * 16)
            pe.wait_ge(w_fin_in, 2 * 16)
            rank(0)
            pe.wait_ge(sc_copied, 1)
            tile(0, True)
            with pe.Fori(1, NT) as t:
                tile(t, False)
            finish(NT - 1, P)
            pe.wait_ge(cols_ready, 1)
            for n in range(NB):
                pe.wait_ge(landed[n], (NT * 2 * CHOICES // RING + 2) * 16)
                for c in range(0, D, BANK):
                    last = nc.tensor.matmul(VA[0:NB, c:c + BANK], w_cols[:, n, :], rows[:, n, c:c + BANK], start=(n == 0),
                                            stop=(n == NB - 1))
                last.then_inc(v_used, 1)
            finish(NT, NB)


_INS = ['x_prompt', 'x_sample', 'cache_k', 'cache_v', 'state_conv', 'p_prompt', 'p_sample', 'norm_mix', 'w_in', 'q_gain',
        'k_gain', 'attn_sinks', 'conv_dw_w', 'conv_dw_b', 'conv_ln_g', 'conv_ln_b', 'w_out', 'norm_ffn', 'peer_wq',
        'peer_sub_keys', 'peer_u', 'peer_v', 'norm_ple', 'w_ple_proj', 'w_ple_gate']
_OUTS = [(1, SEQ, D), (NB, 1, D), (1, 1, P, KV, HD), (1, 1, P, KV, HD), (1, 1, HIST, CONV), (1, NB, P, KV, HD),
         (1, NB, P, KV, HD), (1, NB, HIST, CONV)]


def kernel(**inputs):
    import numpy as _np
    import concourse.bacc as _bacc
    from concourse import mybir as _mybir
    from concourse.bass_utils import run_bass_kernel_spmd as _run

    nc = _bacc.Bacc("TRN2", target_bir_lowering=False, num_devices=1)
    arrays, args = {}, []
    for name in _INS:
        a = _np.ascontiguousarray(inputs[name])
        arrays[f"in_{name}_dram"] = a
        args.append(nc.dram_tensor(f"in_{name}_dram", a.shape, _mybir.dt.from_np(a.dtype), kind="ExternalInput").ap())
    for i, shape in enumerate(_OUTS):
        args.append(nc.dram_tensor(f"out_{i}_dram", shape, _mybir.dt.float32, kind="ExternalOutput").ap())
    hymba_step(nc, *args)
    r = _run(nc, [arrays], core_ids=[0])
    return tuple(r.results[0][f"out_{i}_dram"] for i in range(len(_OUTS)))
```

```python
import concourse.bass as bass
from concourse import mybir
from contextlib import ExitStack

F32 = mybir.dt.float32
U32 = mybir.dt.uint32
ALU = mybir.AluOpType
ACT = mybir.ActivationFunctionType
AX = mybir.AxisListType

P = 128
D = 1024
KD = D // P
SEQ = 1024
NT = SEQ // P
NB = 8
HEADS, KV, HD = 8, 2, 64
GROUP = HEADS // KV
QW, KW = HEADS * HD, KV * HD
CONV = D - QW
CT = CONV // P
TAPS = 31
HIST = TAPS - 1
DIN = QW + 2 * KW + 2 * CONV
ZK, ZV, ZA, ZG = QW, QW + KW, QW + 2 * KW, QW + 2 * KW + CONV
WIN = 2 * P
SKEYS = P + 1
EPS = 1e-6
NEG = -1e30
AHEAD = 42136
ARENA = 52900
BANK = 512
PH = 8
TOPK = 16
NKEY = 128
CHOICES = PH * TOPK
DPLE = 256
RING = 8
PAIRS = CHOICES // (2 * RING)
PE_PAIRS = 2
PE_SLOTS = 5
DVE_SLOTS = RING - PE_SLOTS
DIAGS = 2
PE_FIRST = PE_PAIRS * 2 * RING
MIXED_TURNS = 2 * (PAIRS - PE_PAIRS)
PE_STEPS = PE_FIRST + MIXED_TURNS * PE_SLOTS
DVE_STEPS = MIXED_TURNS * DVE_SLOTS


class Chain:

    def __init__(self, eng, sem, base=0):
        self.eng, self.sem, self.base, self.n = eng, sem, base, 0

    def link(self, ins):
        self.n += 1
        ins.then_inc(self.sem, 1)
        self.eng.wait_ge(self.sem, self.base + self.n)


def carve(arena, start):
    at = [start]

    def take(*shape):
        size = 1
        for s in shape:
            size *= s
        view = arena[:, at[0]:at[0] + size]
        at[0] += size
        if len(shape) == 2:
            view = view.rearrange("p (a b) -> p a b", b=shape[1])
        elif len(shape) == 3:
            view = view.rearrange("p (a b c) -> p a b c", b=shape[1], c=shape[2])
        return view
    take.at = at
    return take


def over_partitions(vector, n):
    return vector.partition_broadcast(n)


def hymba_step(nc, x_prompt, x_sample, cache_k, cache_v, state_conv, p_prompt, p_sample, norm_mix, w_in,
               q_gain, k_gain, attn_sinks, conv_dw_w, conv_dw_b, conv_ln_g, conv_ln_b, w_out, norm_ffn,
               peer_wq, peer_sub_keys, peer_u, peer_v, norm_ple, w_ple_proj, w_ple_gate,
               y_prompt, y_sample, new_k_prompt, new_v_prompt, new_conv_prompt,
               new_k_sample, new_v_sample, new_conv_sample):
    with ExitStack() as ctx:
        def sb(name, shape, dt=F32):
            return ctx.enter_context(nc.sbuf_tensor(name, shape, dt))

        ident = sb("ident", [P, P])
        eps = sb("eps", [P, 1])
        norm_cols = sb("norm_cols", [P, 2, KD])
        arena = sb("arena", [P, ARENA])
        ahead = carve(arena, 0)
        wq_main = ahead(KD - 1, 2 * PH * P)
        main_end = ahead.at[0]
        ahead.at[0] = AHEAD
        wq_last = ahead(2 * PH * P)
        w_gate = ahead(KD, D)
        wq_in, w_fin_in = ctx.enter_context(nc.semaphore("wq_in")), ctx.enter_context(nc.semaphore("w_finish_in"))
        weights = (wq_main, wq_last, w_gate, wq_in, w_fin_in)
        x1 = nc.dram_tensor("x1", (NT + 1, P, D), F32, kind="Internal").ap()

        mixer(nc, ident, eps, norm_cols, arena, x1, x_prompt, x_sample, cache_k[0], cache_v[0], state_conv[0],
              norm_mix, w_in[0], q_gain, k_gain, attn_sinks, conv_dw_w[0], conv_dw_b, conv_ln_g, conv_ln_b,
              w_out[0], norm_ple, new_k_prompt, new_v_prompt, new_conv_prompt, new_k_sample, new_v_sample,
              new_conv_sample, weights, peer_wq[0], w_ple_gate[0])
        experts(nc, ident, eps, norm_cols, arena, main_end, ahead.at[0], x1, p_prompt[0], p_sample[0], norm_ffn,
                peer_sub_keys[0], peer_u[0], peer_v[0], w_ple_proj[0], weights, y_prompt, y_sample)


def mixer(nc, ident, eps, norm_cols, arena, x1, x_prompt, x_sample, cache_k, cache_v, state_conv, norm_mix, w_in,
          q_gain, k_gain, attn_sinks, conv_dw_w, conv_dw_b, conv_ln_g, conv_ln_b, w_out, norm_ple,
          new_k_prompt, new_v_prompt, new_conv_prompt, new_k_sample, new_v_sample, new_conv_sample, weights,
          peer_wq, w_ple_gate):
    wq_main, wq_last, w_gate, wq_in, w_fin_in = weights
    with ExitStack() as ctx:
        def sem(name):
            return ctx.enter_context(nc.semaphore(name))

        ZB = ctx.enter_context(nc.psum_tensor("ZB", [P, 4 * BANK], F32))
        TB = ctx.enter_context(nc.psum_tensor("TB", [P, 4 * BANK], F32))

        take = carve(arena, 0)
        win_w = take(KD, DIN)
        wout_w = take(KD, D)
        x_in = take(D)
        x_res = take(D)
        xn = take(D)
        hT = take(KD, P)
        squares = take(D)
        qk = take(QW + KW)
        vwin = take(2, KW)
        glu = take(CONV)
        gate = take(CONV)
        kwin = take(WIN)
        qT = take(GROUP, P)
        gluT = take(CT, HIST + P)
        bias = take(HEADS, WIN)
        bias_prev = take(HEADS, P)
        probs = take(HEADS, WIN)
        probsT = take(2 * HEADS, P)
        mixedT = take(KD, P)
        acc = take(CT, P)
        conv_y = take(CT, P)
        conv_s = take(CT, P)
        chan_rows = take(CONV)
        chan = take(CT, TAPS + 3)
        norm_rows = take(P)
        qg = take(HD)
        kg = take(HD)
        sinks = take(HEADS)
        sink_rows = take(1)
        stat = take(64)
        s_take = carve(arena, take.at[0])
        sbias = s_take(P + 4)
        new_rows = s_take(P)
        own = s_take(NB)
        new_T = s_take(P)
        take.at[0] = s_take.at[0]
        q_blocks = bias_prev.rearrange("p a b -> p (a b)")[:, 0:NB * 72]
        k_rows = probsT[:, 0:8, :]
        v_rows = probsT[:, 8:16, :]
        keysT = bias.rearrange("p a b -> p (a b)")[:, 0:NB * SKEYS].rearrange("p (b k) -> p b k", k=SKEYS)
        st_rows = probs.rearrange("p a b -> p (a b)")[:, 0:2 * CONV].rearrange("p (g c) -> p g c", g=2)
        hist = hT.rearrange("p a b -> p (a b)")[:, 0:CT * NB * TAPS].rearrange("p (c b j) -> p c b j", c=CT, b=NB)
        prod = squares[:, 0:CT * NB * TAPS].rearrange("p (c b j) -> p c b j", c=CT, b=NB)
        assert take.at[0] <= ARENA, take.at[0]
        s_qT = TB[:, 0:QW].rearrange("p (i t) -> p i t", t=P)

        ssq, rms, rstd = stat[:, 0:1], stat[:, 1:2], stat[:, 2:3]
        ss10, rms10, rstd10 = stat[:, 3:13], stat[:, 13:23], stat[:, 23:33]
        top, ntop, esink = stat[:, 33:41], stat[:, 41:49], stat[:, 49:57]
        more = take(64)
        den, rden = more[:, 0:8], more[:, 8:16]
        bn6, mv, rms_c, rstd_c, dsink = more[:, 16:22], more[:, 22:24], more[:, 24:25], more[:, 25:26], more[:, 26:34]
        assert take.at[0] <= AHEAD, take.at[0]

        const_made, const_in, out_w_in = sem("const_made"), sem("const_in"), sem("w_out_in")
        win_in = [sem(f"w_in_in{k}") for k in range(KD)]
        rows_in, cols_T, cols_made = sem("const_rows_in"), sem("const_cols_T"), sem("const_cols_made")
        window_cleared = sem("window_cleared")
        x_landed, res_landed, x1_stored = sem("x_landed"), sem("x_res_landed"), sem("x1_stored")
        squared, xn_ready, xT_ready, hT_ready, z_ready = (sem(n) for n in ("x_squared", "xn_ready", "xT_ready", "hT_ready", "z_ready"))
        qk_squared, qk_summed, qk_rms, sig_ready = sem("qk_squared"), sem("qk_summed"), sem("qk_rms_ready"), sem("gate_ready")
        v_ready = sem("v_ready")
        qk_ready, glu_ready, qkT_ready, gluT_ready = sem("qk_ready"), sem("glu_ready"), sem("qkT_ready"), sem("gluT_ready")
        qk_copied, s_ready, m_ready, bias_set, e_ready = sem("qk_copied"), sem("scores_ready"), sem("max_ready"), sem("bias_set"), sem("exp_ready")
        p_ready, pT_ready, pT_copied, att_ready, att_copied = sem("probs_ready"), sem("probsT_ready"), sem("probsT_copied"), sem("att_ready"), sem("att_copied")
        conv_done, c_ready, cvar_ready, crms_ready = sem("conv_done"), sem("conv_tok_ready"), sem("conv_var_ready"), sem("conv_rms_ready")
        ln_ready, lnT_ready, cy_ready, mix_ready, o_ready, x1_ready = (sem(n) for n in ("ln_ready", "lnT_ready", "conv_affine_ready", "mixed_ready", "w_out_ready", "x1_ready"))
        tail_stored, samples_in, outs_stored, copied_over = sem("prompt_tail_stored"), sem("samples_in"), sem("outs_stored"), sem("caches_copied")
        sbias_in, kT_ready, kT_copied, stT_ready, hist_ready = sem("sbias_in"), sem("cacheT_ready"), sem("cacheT_copied"), sem("stateT_ready"), sem("hist_ready")
        zero_stored = sem("x1_pad_stored")
        act_step, dve_step, act_on, dve_on, pool_on = sem("act_step"), sem("dve_step"), sem("act_on"), sem("dve_on"), sem("pool_on")
        kT_new, bias_out = sem("new_key_copied"), sem("bias_row_stored")
        bias_row = nc.dram_tensor("bias_row", (1, HEADS, SKEYS), F32, kind="Internal").ap()
        gluT_copied = sem("gluT_copied")
        zero_ready, new_glu_taken = sem("zeros_ready"), sem("new_glu_taken")
        s_probs = qT.rearrange("p i t -> p (i t)")[0:HEADS * NB, 0:SKEYS]
        s_probsT = qT.rearrange("p i t -> p (i t)")[:, 256:256 + HEADS * NB]
        pool_step = sem("pool_step")

        def hold(eng, carrier, s, value):
            eng.wait_ge(s, value)
            eng.sem_inc(carrier, 1)

        block = ctx.enter_context(nc.Block())

        @block.sync
        def _(sp):
            def load_x(t):
                sp.wait_ge(xn_ready, t)
                sp.dma_start(x_in, x_prompt[0, bass.ds(t * P, P), :]).then_inc(x_landed, 16)

            sp.dma_start(x_in, x_prompt[0, 0:P, :]).then_inc(x_landed, 16)
            sp.dma_start(chan_rows[0:TAPS, :], conv_dw_w).then_inc(rows_in, 16)
            sp.dma_start(chan_rows[TAPS:TAPS + 1, :], conv_dw_b).then_inc(rows_in, 16)
            sp.dma_start(chan_rows[TAPS + 1:TAPS + 2, :], conv_ln_g).then_inc(rows_in, 16)
            sp.dma_start(chan_rows[TAPS + 2:TAPS + 3, :], conv_ln_b).then_inc(rows_in, 16)
            sp.dma_start(norm_rows[0:KD, :], norm_mix[0].rearrange("(k p) -> k p", p=P)).then_inc(rows_in, 16)
            sp.dma_start(norm_rows[KD:2 * KD, :], norm_ple[0].rearrange("(k p) -> k p", p=P)).then_inc(rows_in, 16)
            for k in range(KD):
                sp.dma_start(win_w[:, k, :], w_in[k * P:(k + 1) * P, :]).then_inc(win_in[k], 16)
            sp.dma_start(qg, over_partitions(q_gain[0], P)).then_inc(const_in, 16)
            sp.dma_start(kg, over_partitions(k_gain[0], P)).then_inc(const_in, 16)
            sp.dma_start(sinks, over_partitions(attn_sinks[0], P)).then_inc(const_in, 16)
            for b in range(NB):
                sp.dma_start(sink_rows[b * HEADS:(b + 1) * HEADS, :],
                             attn_sinks[0].rearrange("(h o) -> h o", o=1)).then_inc(const_in, 16)
            load_x(1)
            for kv in range(KV):
                sp.dma_start(wout_w[kv * HD:(kv + 1) * HD, 0:GROUP, :],
                             w_out[kv * GROUP * HD:(kv + 1) * GROUP * HD, :].rearrange("(i d) n -> d i n", d=HD)
                             ).then_inc(out_w_in, 16)
            sp.dma_start(wout_w[:, GROUP:KD, :], w_out[QW:D, :].rearrange("(k p) n -> p k n", p=P)).then_inc(out_w_in, 16)
            sp.dma_start(x_res, x_prompt[0, 0:P, :]).then_inc(res_landed, 16)
            sp.dma_start(wq_last, peer_wq[(KD - 1) * P:D, :]).then_inc(wq_in, 16)
            sp.dma_start(w_gate, w_ple_gate.rearrange("(k p) n -> p k n", p=P)).then_inc(w_fin_in, 16)
            for b in range(NB):
                sp.dma_start(new_k_sample[0, b, 0:P - 1], cache_k[b, 1:P]).then_inc(copied_over, 16)
                sp.dma_start(new_v_sample[0, b, 0:P - 1], cache_v[b, 1:P]).then_inc(copied_over, 16)
            sp.dma_start(new_conv_sample[0, :, 0:HIST - 1, :], state_conv[:, 1:HIST, :]).then_inc(copied_over, 16)
            def swap_residual(t):
                sp.wait_ge(x1_ready, t)
                sp.dma_start(x1[bass.ds(t - 1, 1), :, :].rearrange("o p d -> (o p) d"), x_res).then_inc(x1_stored, 16)
                sp.wait_ge(x1_stored, t * 16)
                sp.dma_start(x_res, x_prompt[0, bass.ds(t * P, P), :]).then_inc(res_landed, 16)

            load_x(2)
            with sp.Fori(1, NT - 2) as t:
                load_x(t + 2)
                swap_residual(t)
            sp.wait_ge(xn_ready, NT)
            sp.dma_start(x_in[0:NB, :], x_sample[:, 0, :]).then_inc(x_landed, 16)
            swap_residual(NT - 2)
            sp.wait_ge(qk_ready, NT)
            sp.dma_start(new_k_prompt[0, 0].rearrange("w h d -> w (h d)"), qk[:, QW:QW + KW]).then_inc(tail_stored, 16)
            sp.wait_ge(v_ready, NT)
            sp.dma_start(new_v_prompt[0, 0].rearrange("w h d -> w (h d)"), vwin[:, 1, :]).then_inc(tail_stored, 16)
            sp.wait_ge(glu_ready, NT)
            sp.dma_start(new_conv_prompt[0, 0], glu[P - HIST:P, :]).then_inc(tail_stored, 16)
            swap_residual(NT - 1)
            sp.wait_ge(bias_set, NT + 1)
            sp.dma_start(bias_row, bias[0:1, :, 0:SKEYS]).then_inc(bias_out, 16)
            sp.wait_ge(bias_out, 16)
            for b in range(NB):
                sp.dma_start(sbias[b * HEADS:(b + 1) * HEADS, 0:SKEYS], bias_row[0]).then_inc(sbias_in, 16)
            sp.wait_ge(att_ready, NT)
            sp.dma_start(k_rows, cache_k.rearrange("b w h d -> w b (h d)")).then_inc(samples_in, 16)
            sp.dma_start(v_rows, cache_v.rearrange("b w h d -> w b (h d)")).then_inc(samples_in, 16)
            for g in range(2):
                sp.dma_start(st_rows[0:4 * HIST, g, :],
                             state_conv[4 * g:4 * g + 4].rearrange("b j c -> (b j) c")).then_inc(samples_in, 16)
            sp.wait_ge(z_ready, NT + 1)
            for k in range(KD - 1):
                sp.dma_start(wq_main[:, k, :], peer_wq[k * P:(k + 1) * P, :]).then_inc(wq_in, 16)
            sp.wait_ge(x1_ready, NT)
            sp.dma_start(x1[NT - 1], x_res).then_inc(x1_stored, 16)
            sp.wait_ge(x1_stored, NT * 16)
            sp.dma_start(x_res[0:NB, :], x_sample[:, 0, :]).then_inc(res_landed, 16)
            sp.wait_ge(zero_ready, 1)
            sp.dma_start(x1[NT, NB:P, :], probs.rearrange("p a b -> p (a b)")[NB:P, 2 * CONV:2 * CONV + D]).then_inc(zero_stored, 16)
            sp.wait_ge(qk_ready, NT + 1)
            sp.dma_start(new_k_sample[0, :, P - 1].rearrange("b h d -> b (h d)"), qk[0:NB, QW:QW + KW]).then_inc(outs_stored, 16)
            sp.wait_ge(v_ready, NT + 1)
            sp.dma_start(new_v_sample[0, :, P - 1].rearrange("b h d -> b (h d)"), vwin[0:NB, 1, :]).then_inc(outs_stored, 16)
            sp.wait_ge(glu_ready, NT + 1)
            sp.dma_start(new_conv_sample[0, :, HIST - 1, :], glu[0:NB, :]).then_inc(outs_stored, 16)
            sp.wait_ge(x1_ready, NT + 1)
            sp.dma_start(x1[NT, 0:NB, :], x_res[0:NB, :]).then_inc(x1_stored, 16)
            sp.wait_ge(x1_stored, (NT + 1) * 16)
            sp.wait_ge(zero_stored, 16)
            sp.wait_ge(tail_stored, 3 * 16)
            sp.wait_ge(copied_over, (2 * NB + 1) * 16)
            sp.wait_ge(outs_stored, 3 * 16)

        @block.gpsimd
        def _(pool):
            steps = Chain(pool, pool_step)
            steps.link(nc.gpsimd.memset(ident[:, :], 0.0))
            nc.gpsimd.affine_select(out=ident[:, :], in_=ident[:, :], compare_op=ALU.not_equal, fill=1.0, base=0,
                                    pattern=[[-1, P]], channel_multiplier=1).then_inc(const_made, 1)
            nc.gpsimd.memset(eps[:, :], EPS).then_inc(const_made, 1)
            nc.gpsimd.memset(kwin[:, 0:P], 0.0).then_inc(window_cleared, 1)
            nc.gpsimd.memset(vwin[:, 0, :], 0.0).then_inc(window_cleared, 1)
            nc.gpsimd.memset(gluT[:, :, 0:HIST], 0.0).then_inc(window_cleared, 1)
            steps.link(nc.gpsimd.iota(probs[:, 0, :], [[-1, WIN]], base=P, channel_multiplier=1,
                                      allow_small_or_imprecise_dtypes=True))
            for h in range(HEADS):
                last = nc.gpsimd.tensor_scalar(bias[:, h, :], probs[:, 0, :], -2.0 ** (-8.0 * (h + 1) / HEADS), 0.0,
                                               ALU.mult, ALU.add)
            steps.link(last)
            steps.link(nc.gpsimd.affine_select(out=bias[:, :, :], in_=bias[:, :, :], compare_op=ALU.is_ge, fill=NEG, base=P,
                                               pattern=[[0, HEADS], [-1, WIN]], channel_multiplier=1))
            steps.link(nc.gpsimd.affine_select(out=bias[:, :, :], in_=bias[:, :, :], compare_op=ALU.is_ge, fill=NEG, base=0,
                                               pattern=[[0, HEADS], [1, WIN]], channel_multiplier=-1))
            steps.link(nc.gpsimd.tensor_copy(bias_prev[:, :, :], bias[:, :, 0:P]))
            nc.gpsimd.memset(bias[:, :, 0:P], NEG).then_inc(bias_set, 1)
            steps.link(nc.gpsimd.memset(own[0:HEADS * NB, :], 1.0))
            steps.link(nc.gpsimd.affine_select(out=own[0:HEADS * NB, :], in_=own[0:HEADS * NB, :], compare_op=ALU.is_ge,
                                               fill=0.0, base=0, pattern=[[-HEADS, NB]], channel_multiplier=1))
            steps.link(nc.gpsimd.affine_select(out=own[0:HEADS * NB, :], in_=own[0:HEADS * NB, :], compare_op=ALU.is_ge,
                                               fill=0.0, base=HEADS - 1, pattern=[[HEADS, NB]], channel_multiplier=-1))
            nc.gpsimd.memset(new_rows[:, :], 0.0).then_inc(const_made, 1)
            with pool.Fori(0, NT) as t:
                hold(pool, pool_on, m_ready, t + 1)
                nc.gpsimd.tensor_copy(bias[:, :, 0:P], bias_prev[:, :, :]).then_inc(bias_set, 1)
            pool.wait_ge(bias_set, NT + 1)
            nc.gpsimd.memset(q_blocks, 0.0).then_inc(const_made, 1)
            pool.wait_ge(pT_ready, NT)
            nc.gpsimd.memset(probs.rearrange("p a b -> p (a b)")[:, 2 * CONV:2 * CONV + D], 0.0).then_inc(zero_ready, 1)

        A_FIRST, A_STEPS = 2, 11

        @block.scalar
        def _(act):
            def x_norm(t, R, steps):
                hold(act, act_on, x_landed, (t + 1) * 16)
                steps.link(nc.scalar.activation(squares[0:R, :], x_in[0:R, :], ACT.Square, accum_out=ssq[0:R, :]))
                nc.scalar.activation(rms[0:R, :], ssq[0:R, :], ACT.Sqrt, bias=eps[0:R, :], scale=1.0 / D).then_inc(squared, 1)

            def evacuate(t, R):
                act.wait_ge(z_ready, t + 1)
                nc.scalar.activation(squares[0:R, 0:QW + KW], ZB[0:R, 0:QW + KW], ACT.Square).then_inc(qk_squared, 1)
                if R == NB:
                    act.wait_ge(tail_stored, 48)
                nc.scalar.activation(vwin[0:R, 1, :], ZB[0:R, ZV:ZV + KW], ACT.Copy).then_inc(v_ready, 1)
                act.wait_ge(qk_summed, t + 1)
                nc.scalar.activation(rms10[0:R, :], ss10[0:R, :], ACT.Sqrt, bias=eps[0:R, :], scale=1.0 / HD).then_inc(qk_rms, 1)

            def gate_sigmoid(t, R):
                nc.scalar.activation(gate[0:R, :], ZB[0:R, ZG:ZG + CONV], ACT.Sigmoid).then_inc(sig_ready, 1)

            def conv_rms(t, R):
                act.wait_ge(cvar_ready, t + 1)
                nc.scalar.activation(rms_c[0:R, :], mv[0:R, 1:2], ACT.Sqrt, bias=eps[0:R, :]).then_inc(crms_ready, 1)

            def conv_affine(t, R):
                act.wait_ge(lnT_ready, t + 1)
                for c in range(CT):
                    scale, shift = chan[:, c, TAPS + 1:TAPS + 2], chan[:, c, TAPS + 2:TAPS + 3]
                    src = TB[:, 2 * BANK + c * P:2 * BANK + c * P + R]
                    nc.scalar.activation(conv_y[:, c, 0:R], src, ACT.Identity, bias=shift, scale=scale)
                    last = nc.scalar.activation(conv_s[:, c, 0:R], src, ACT.Sigmoid, bias=shift, scale=scale)
                last.then_inc(cy_ready, 1)

            act.wait_ge(cols_T, 1)
            nc.scalar.activation(chan[:, :, :], TB[:, 0:CT * P].rearrange("p (c j) -> p c j", c=CT)[:, :, 0:TAPS + 3], ACT.Copy).then_inc(cols_made, 1)
            nc.scalar.activation(norm_cols[:, :, :], TB[:, BANK:BANK + 2 * KD].rearrange("p (a k) -> p a k", a=2), ACT.Copy).then_inc(cols_made, 1)

            def heads_copy(t):
                act.wait_ge(qkT_ready, t + 1)
                nc.scalar.activation(qT[:, :, :], TB[:, 0:QW].rearrange("p (i t) -> p i t", t=P), ACT.Copy)
                nc.scalar.activation(kwin[:, P:WIN], TB[:, QW:QW + P], ACT.Copy).then_inc(qk_copied, 1)

            def prompt_tile(t, next_rows, norm_rows):
                steps = Chain(act, act_step, t * A_STEPS + A_FIRST)
                act.wait_ge(m_ready, t + 1)
                for h in range(HEADS):
                    steps.link(nc.scalar.activation(probs[:, h, :], probs[:, h, :], ACT.Exp, bias=ntop[:, h:h + 1],
                                                    accum_out=den[:, h:h + 1]))
                nc.scalar.activation(esink[:, :], dsink[:, :], ACT.Exp).then_inc(e_ready, 1)
                if norm_rows:
                    x_norm(t + 2, norm_rows, steps)
                act.wait_ge(pT_ready, t + 1)
                nc.scalar.activation(probsT[:, :, :], TB[:, :].rearrange("p (a b) -> p a b", b=P), ACT.Copy).then_inc(pT_copied, 1)
                act.wait_ge(att_ready, t + 1)
                nc.scalar.activation(mixedT[:, 0:GROUP, :], TB[:, 0:QW].rearrange("p (i t) -> p i t", t=P), ACT.Copy).then_inc(att_copied, 1)
                steps.link(nc.scalar.activation(kwin[:, 0:P], kwin[:, P:WIN], ACT.Copy))
                steps.link(nc.scalar.activation(vwin[:, 0, :], vwin[:, 1, :], ACT.Copy))
                evacuate(t + 1, next_rows)
                conv_rms(t, P)
                gate_sigmoid(t + 1, next_rows)
                conv_affine(t, P)
                if norm_rows:
                    heads_copy(t + 1)
                assert steps.n == (A_STEPS if norm_rows else A_STEPS - 1), steps.n

            steps = Chain(act, act_step)
            act.wait_ge(const_made, 2)
            x_norm(0, P, steps)
            act.wait_ge(window_cleared, 3)
            evacuate(0, P)
            gate_sigmoid(0, P)
            heads_copy(0)
            x_norm(1, P, steps)
            assert steps.n == A_FIRST, steps.n
            with act.Fori(0, NT - 2) as t:
                prompt_tile(t, P, P)
            prompt_tile(NT - 2, P, NB)
            prompt_tile(NT - 1, NB, 0)

            t, R, rows = NT, NB, HEADS * NB
            steps = Chain(act, act_step, t * A_STEPS + A_FIRST - 1)
            act.wait_ge(gluT_ready, t + 1)
            nc.scalar.activation(hist[:, :, :, HIST], ZB[:, 0:CT * P].rearrange("p (c k) -> p c k", c=CT)[:, :, 0:NB],
                                 ACT.Copy).then_inc(new_glu_taken, 1)
            act.wait_ge(qkT_ready, t + 1)
            act.wait_ge(const_made, 4)
            for kv in range(KV):
                half = slice(kv * HD, (kv + 1) * HD)
                nc.scalar.activation(q_blocks[half, :].rearrange("p (b s) -> p b s", s=72)[:, :, kv * GROUP:(kv + 1) * GROUP],
                                     s_qT[half, :, 0:NB].rearrange("p i b -> p b i"), ACT.Copy)
            act.wait_ge(sbias_in, NB * 16)
            nc.scalar.activation(keysT[:, :, P], TB[:, QW:QW + NB], ACT.Copy).then_inc(kT_new, 1)
            act.wait_ge(kT_ready, 1)
            nc.scalar.activation(keysT[:, :, 0:P], ZB[:, 0:NB * P].rearrange("p (b k) -> p b k", k=P), ACT.Copy).then_inc(kT_copied, 1)
            act.wait_ge(stT_ready, 1)
            for g in range(2):
                last = nc.scalar.activation(hist[:, :, 4 * g:4 * g + 4, 0:HIST],
                                            TB[:, 2 * BANK + g * CT * P:2 * BANK + (g + 1) * CT * P].rearrange("p (c k) -> p c k", c=CT)
                                            [:, :, 0:4 * HIST].rearrange("p c (b j) -> p c b j", j=HIST), ACT.Copy)
            last.then_inc(hist_ready, 1)
            act.wait_ge(m_ready, t + 1)
            steps.link(nc.scalar.activation(s_probs, s_probs, ACT.Exp, bias=ntop[0:rows, 0:1], accum_out=den[0:rows, 0:1]))
            nc.scalar.activation(esink[0:rows, 0:1], dsink[0:rows, 0:1], ACT.Exp).then_inc(e_ready, 1)
            act.wait_ge(pT_ready, t + 1)
            nc.scalar.activation(s_probsT, TB[:, BANK:BANK + rows], ACT.Copy)
            nc.scalar.activation(new_T[0:NB, 0:rows], TB[0:NB, 2 * BANK:2 * BANK + rows], ACT.Copy).then_inc(pT_copied, 1)
            act.wait_ge(att_ready, t + 1)
            for kv in range(KV):
                half = slice(kv * HD, (kv + 1) * HD)
                last = nc.scalar.activation(mixedT[half, 0:GROUP, 0:NB],
                                            TB[half, 3 * BANK:3 * BANK + rows].rearrange("p (b h) -> p h b", h=HEADS)
                                            [:, kv * GROUP:(kv + 1) * GROUP, :], ACT.Copy)
            last.then_inc(att_copied, 1)
            conv_rms(t, R)
            conv_affine(t, R)

        FIRST_TAPS, EARLY_TAPS = 7, 7
        D_FIRST, D_STEPS = 4 + FIRST_TAPS, 42
        TT = nc.vector.tensor_tensor

        @block.vector
        def _(dve):
            def x_norm(t, R, steps):
                dve.wait_ge(squared, t + 1)
                steps.link(nc.vector.reciprocal(rstd[0:R, :], rms[0:R, :]))
                nc.vector.tensor_scalar(xn[0:R, :], x_in[0:R, :], rstd[0:R, :], None, ALU.mult).then_inc(xn_ready, 1)

            def x_gain(t, R):
                dve.wait_ge(xT_ready, t + 1)
                TT(hT[:, :, 0:R], ZB[:, 0:D].rearrange("p (k t) -> p k t", k=KD)[:, :, 0:R],
                   norm_cols[:, 0, :].unsqueeze(2).to_broadcast([P, KD, R]), ALU.mult).then_inc(hT_ready, 1)

            def qk_sums(t, R):
                dve.wait_ge(qk_squared, t + 1)
                nc.vector.tensor_reduce(ss10[0:R, :], squares[0:R, 0:QW + KW].rearrange("p (h d) -> p h d", d=HD), AX.X,
                                        ALU.add).then_inc(qk_summed, 1)

            def heads_and_glu(t, R, steps):
                dve.wait_ge(qk_rms, t + 1)
                steps.link(nc.vector.reciprocal(rstd10[0:R, :], rms10[0:R, :]))
                if R == NB:
                    dve.wait_ge(tail_stored, 48)
                q_out = qk[0:R, 0:QW].rearrange("p (i kv d) -> p kv i d", kv=KV, i=GROUP)
                k_out = qk[0:R, QW:].rearrange("p (h d) -> p h d", d=HD)
                q_by_head = qk[0:R, 0:QW].rearrange("p (h d) -> p h d", d=HD)
                TT(q_out, ZB[0:R, 0:QW].rearrange("p (kv i d) -> p kv i d", kv=KV, i=GROUP),
                   rstd10[0:R, 0:HEADS].rearrange("p (kv i) -> p kv i", kv=KV).unsqueeze(3).to_broadcast([R, KV, GROUP, HD]),
                   ALU.mult)
                steps.link(TT(k_out, ZB[0:R, ZK:ZV].rearrange("p (h d) -> p h d", d=HD),
                              rstd10[0:R, HEADS:].unsqueeze(2).to_broadcast([R, KV, HD]), ALU.mult))
                TT(q_by_head, q_by_head, qg[0:R, :].unsqueeze(1).to_broadcast([R, HEADS, HD]), ALU.mult)
                TT(k_out, k_out, kg[0:R, :].unsqueeze(1).to_broadcast([R, KV, HD]), ALU.mult).then_inc(qk_ready, 1)
                dve.wait_ge(sig_ready, t + 1)
                TT(glu[0:R, :], ZB[0:R, ZA:ZA + CONV], gate[0:R, :], ALU.mult).then_inc(glu_ready, 1)

            def gluT_copy(t):
                dve.wait_ge(gluT_ready, t + 1)
                nc.vector.tensor_copy(gluT[:, :, HIST:HIST + P], ZB[:, 0:CT * P].rearrange("p (c t) -> p c t", c=CT)
                                      ).then_inc(gluT_copied, 1)

            def conv_norm(t, R, steps):
                dve.wait_ge(c_ready, t + 1)
                steps.link(nc.vector.bn_stats(bn6[0:R, :], TB[0:R, BANK:2 * BANK]))
                hold(dve, dve_on, dve_step, steps.base + steps.n)
                nc.vector.bn_aggr(mv[0:R, :], bn6[0:R, :]).then_inc(cvar_ready, 1)
                dve.wait_ge(crms_ready, t + 1)
                steps.link(nc.vector.reciprocal(rstd_c[0:R, :], rms_c[0:R, :]))
                nc.vector.tensor_scalar(xn[0:R, 0:CONV], TB[0:R, BANK:2 * BANK], mv[0:R, 0:1], rstd_c[0:R, :], ALU.subtract,
                                        ALU.mult).then_inc(ln_ready, 1)

            def silu(t, R):
                dve.wait_ge(cy_ready, t + 1)
                TT(mixedT[:, GROUP:KD, 0:R], conv_y[:, :, 0:R], conv_s[:, :, 0:R], ALU.mult).then_inc(mix_ready, 1)

            def residual(t, R):
                dve.wait_ge(o_ready, t + 1)
                dve.wait_ge(res_landed, (t + 1) * 16)
                TT(x_res[0:R, :], ZB[0:R, 2 * BANK:4 * BANK], x_res[0:R, :], ALU.add).then_inc(x1_ready, 1)

            def conv_tap(j):
                for c in range(CT):
                    src, w = gluT[:, c, j:j + P], chan[:, c, j:j + 1]
                    if j == 0:
                        last = nc.vector.tensor_scalar(acc[:, c, :], src, w, chan[:, c, TAPS:TAPS + 1], ALU.mult, ALU.add)
                    else:
                        last = nc.vector.scalar_tensor_tensor(out=acc[:, c, :], in0=src, scalar=w, in1=acc[:, c, :],
                                                              op0=ALU.mult, op1=ALU.add)
                return last

            def first_taps(t, steps):
                dve.wait_ge(gluT_copied, t + 1)
                for j in range(FIRST_TAPS):
                    steps.link(conv_tap(j))

            def prompt_tile(t, next_rows, norm_rows, first=False):
                steps = Chain(dve, dve_step, t * D_STEPS + D_FIRST)
                dve.wait_ge(s_ready, t + 1)
                dve.wait_ge(bias_set, t + 1)
                flat = probs.rearrange("p h k -> p (h k)")
                steps.link(nc.vector.scalar_tensor_tensor(out=flat, in0=TB[:, :], scalar=HD ** -0.5,
                                                          in1=bias.rearrange("p h k -> p (h k)"), op0=ALU.mult, op1=ALU.add))
                steps.link(nc.vector.tensor_reduce(top[:, :], probs[:, :, :], AX.X, ALU.max))
                steps.link(TT(top[:, :], top[:, :], sinks[:, :], ALU.max))
                steps.link(TT(dsink[:, :], sinks[:, :], top[:, :], ALU.subtract))
                nc.vector.tensor_scalar(ntop[:, :], top[:, :], -1.0, None, ALU.mult).then_inc(m_ready, 1)
                x_gain(t + 1, next_rows)
                if not first:
                    residual(t - 1, P)
                for j in range(FIRST_TAPS, FIRST_TAPS + EARLY_TAPS):
                    steps.link(conv_tap(j))
                dve.wait_ge(e_ready, t + 1)
                steps.link(TT(den[:, :], den[:, :], esink[:, :], ALU.add))
                steps.link(nc.vector.reciprocal(rden[:, :], den[:, :]))
                TT(probs[:, :, :], probs[:, :, :], rden[:, :].unsqueeze(2).to_broadcast([P, HEADS, WIN]), ALU.mult).then_inc(p_ready, 1)
                for j in range(FIRST_TAPS + EARLY_TAPS, TAPS - 1):
                    steps.link(conv_tap(j))
                conv_tap(TAPS - 1).then_inc(conv_done, 1)
                steps.link(nc.vector.tensor_copy(gluT[:, :, 0:HIST], gluT[:, :, P:P + HIST]))
                qk_sums(t + 1, next_rows)
                conv_norm(t, P, steps)
                heads_and_glu(t + 1, next_rows, steps)
                silu(t, P)
                if norm_rows:
                    gluT_copy(t + 1)
                    x_norm(t + 2, norm_rows, steps)
                    first_taps(t + 1, steps)
                assert steps.n == (D_STEPS if norm_rows else D_STEPS - 1 - FIRST_TAPS), steps.n

            steps = Chain(dve, dve_step)
            dve.wait_ge(cols_made, 2)
            x_norm(0, P, steps)
            x_gain(0, P)
            dve.wait_ge(const_in, (3 + NB) * 16)
            dve.wait_ge(window_cleared, 3)
            qk_sums(0, P)
            heads_and_glu(0, P, steps)
            gluT_copy(0)
            x_norm(1, P, steps)
            first_taps(0, steps)
            dve.wait_ge(const_made, 3)
            assert steps.n == D_FIRST, steps.n
            prompt_tile(0, P, P, first=True)
            with dve.Fori(1, NT - 2) as t:
                prompt_tile(t, P, P)
            prompt_tile(NT - 2, P, NB)
            prompt_tile(NT - 1, NB, 0)

            t, R, rows = NT, NB, HEADS * NB
            steps = Chain(dve, dve_step, t * D_STEPS + D_FIRST - 1 - FIRST_TAPS)
            residual(t - 1, P)
            dve.wait_ge(s_ready, t + 1)
            dve.wait_ge(sbias_in, NB * 16)
            s0 = sink_rows[0:rows, :]
            steps.link(nc.vector.scalar_tensor_tensor(out=s_probs, in0=TB[0:rows, 0:SKEYS], scalar=HD ** -0.5,
                                                      in1=sbias[0:rows, 0:SKEYS], op0=ALU.mult, op1=ALU.add))
            steps.link(nc.vector.tensor_reduce(top[0:rows, 0:1], s_probs, AX.X, ALU.max))
            steps.link(TT(top[0:rows, 0:1], top[0:rows, 0:1], s0, ALU.max))
            steps.link(TT(dsink[0:rows, 0:1], s0, top[0:rows, 0:1], ALU.subtract))
            nc.vector.tensor_scalar(ntop[0:rows, 0:1], top[0:rows, 0:1], -1.0, None, ALU.mult).then_inc(m_ready, 1)
            dve.wait_ge(hist_ready, 1)
            steps.link(TT(prod, hist, chan[:, :, 0:TAPS].unsqueeze(2).to_broadcast([P, CT, NB, TAPS]), ALU.mult))
            steps.link(nc.vector.tensor_reduce(acc[:, :, 0:NB], prod, AX.X, ALU.add))
            TT(acc[:, :, 0:NB], acc[:, :, 0:NB], chan[:, :, TAPS:TAPS + 1].to_broadcast([P, CT, NB]), ALU.add).then_inc(conv_done, 1)
            dve.wait_ge(e_ready, t + 1)
            steps.link(TT(den[0:rows, 0:1], den[0:rows, 0:1], esink[0:rows, 0:1], ALU.add))
            steps.link(nc.vector.reciprocal(rden[0:rows, 0:1], den[0:rows, 0:1]))
            steps.link(nc.vector.tensor_scalar(s_probs, s_probs, rden[0:rows, 0:1], None, ALU.mult))
            nc.vector.tensor_scalar(new_rows[0:rows, 0:NB], own[0:rows, :], s_probs[:, P:P + 1], None, ALU.mult).then_inc(p_ready, 1)
            conv_norm(t, R, steps)
            silu(t, R)
            residual(t, R)

        @block.tensor
        def _(pe):
            def transpose(out, src, rows):
                return nc.tensor.transpose(out, src, ident[0:rows, 0:rows])

            def x_transposes(t, R, beside=None):
                if beside is not None:
                    pe.wait_ge(gluT_copied, beside + 1)
                pe.wait_ge(xn_ready, t + 1)
                for k in range(KD):
                    last = transpose(ZB[:, k * P:k * P + R], xn[0:R, k * P:(k + 1) * P], R)
                last.then_inc(xT_ready, 1)

            def product(R, c, k):
                cols = slice(c * BANK, min((c + 1) * BANK, DIN))
                return nc.tensor.matmul(ZB[0:R, cols], hT[:, k, 0:R], win_w[:, k, cols], start=(k == 0), stop=(k == KD - 1))

            def project(R, banks):
                for c in banks:
                    for k in range(KD):
                        last = product(R, c, k)
                return last

            def heads_and_glu(t, R):
                pe.wait_ge(qk_ready, t + 1)
                for i in range(GROUP):
                    transpose(TB[:, i * P:i * P + R], qk[0:R, i * P:(i + 1) * P], R)
                transpose(TB[:, QW:QW + R], qk[0:R, QW:QW + KW], R).then_inc(qkT_ready, 1)
                pe.wait_ge(glu_ready, t + 1)
                for c in range(CT):
                    last = transpose(ZB[:, c * P:c * P + R], glu[0:R, c * P:(c + 1) * P], R)
                last.then_inc(gluT_ready, 1)

            def scores(t):
                pe.wait_ge(qk_copied, t + 1)
                for h in range(HEADS):
                    kv, i = divmod(h, GROUP)
                    half = slice(kv * HD, (kv + 1) * HD)
                    last = nc.tensor.matmul(TB[:, h * WIN:(h + 1) * WIN], qT[half, i, :], kwin[half, :], start=True, stop=True)
                last.then_inc(s_ready, 1)

            def conv_norm(t, R):
                pe.wait_ge(conv_done, t + 1)
                pe.wait_ge(pT_copied, t + 1)
                for c in range(CT):
                    last = transpose(TB[0:R, BANK + c * P:BANK + (c + 1) * P], acc[:, c, 0:R], P)
                last.then_inc(c_ready, 1)
                pe.wait_ge(ln_ready, t + 1)
                for c in range(CT):
                    last = transpose(TB[:, 2 * BANK + c * P:2 * BANK + c * P + R], xn[0:R, c * P:(c + 1) * P], R)
                last.then_inc(lnT_ready, 1)

            def mixed_out(t, R, part, banks=(0, 1)):
                for c in banks:
                    for k in range(part * GROUP, (part + 1) * GROUP):
                        last = nc.tensor.matmul(ZB[0:R, (2 + c) * BANK:(3 + c) * BANK], mixedT[:, k, 0:R],
                                                wout_w[:, k, c * BANK:(c + 1) * BANK], start=(k == 0), stop=(k == KD - 1))
                return last

            pe.wait_ge(const_made, 1)
            pe.wait_ge(rows_in, 6 * 16)
            for c in range(CT):
                transpose(TB[:, c * P:c * P + TAPS + 3], chan_rows[0:TAPS + 3, c * P:(c + 1) * P], TAPS + 3)
            transpose(TB[:, BANK:BANK + 2 * KD], norm_rows[0:2 * KD, :], 2 * KD).then_inc(cols_T, 1)
            pe.wait_ge(cols_made, 2)

            def prompt_tile(t, next_rows, norm_rows, first=False):
                pe.wait_ge(hT_ready, t + 2)
                project(next_rows, (0, 1))
                pe.wait_ge(p_ready, t + 1)
                for h in range(HEADS):
                    for blk in range(2):
                        s = 2 * h + blk
                        last = transpose(TB[:, s * P:(s + 1) * P], probs[:, h, blk * P:(blk + 1) * P], P)
                last.then_inc(pT_ready, 1)
                if not first:
                    pe.wait_ge(x1_ready, t)
                project(next_rows, (2,))
                pe.wait_ge(pT_copied, t + 1)
                for h in range(HEADS):
                    kv, i = divmod(h, GROUP)
                    half = slice(kv * HD, (kv + 1) * HD)
                    for blk in range(2):
                        last = nc.tensor.matmul(TB[half, i * P:(i + 1) * P], vwin[:, blk, half], probsT[:, 2 * h + blk, :],
                                                start=(blk == 0), stop=(blk == 1))
                last.then_inc(att_ready, 1)
                project(next_rows, (3,)).then_inc(z_ready, 1)
                conv_norm(t, P)
                pe.wait_ge(att_copied, t + 1)
                heads_and_glu(t + 1, next_rows)
                if first:
                    pe.wait_ge(out_w_in, 3 * 16)
                mixed_out(t, P, 0, banks=(0,))
                if next_rows == P:
                    pe.wait_ge(cy_ready, t + 1)
                    scores(t + 1)
                mixed_out(t, P, 0, banks=(1,))
                if norm_rows:
                    x_transposes(t + 2, norm_rows, beside=t + 1)
                pe.wait_ge(mix_ready, t + 1)
                mixed_out(t, P, 1).then_inc(o_ready, 1)

            x_transposes(0, P)
            pe.wait_ge(hT_ready, 1)
            for k in range(KD):
                pe.wait_ge(win_in[k], 16)
                for c in range(4):
                    last = product(P, c, k)
            last.then_inc(z_ready, 1)
            heads_and_glu(0, P)
            scores(0)
            x_transposes(1, P, beside=0)
            prompt_tile(0, P, P, first=True)
            with pe.Fori(1, NT - 2) as t:
                prompt_tile(t, P, P)
            prompt_tile(NT - 2, P, NB)
            prompt_tile(NT - 1, NB, 0)

            t, rows = NT, HEADS * NB
            pe.wait_ge(samples_in, 4 * 16)
            pe.wait_ge(new_glu_taken, 1)
            for b in range(NB):
                last = transpose(ZB[:, b * P:(b + 1) * P], k_rows[:, b, :], P)
            last.then_inc(kT_ready, 1)
            for g in range(2):
                for c in range(CT):
                    at = 2 * BANK + (g * CT + c) * P
                    last = transpose(TB[:, at:at + 4 * HIST], st_rows[0:4 * HIST, g, c * P:(c + 1) * P], 4 * HIST)
            last.then_inc(stT_ready, 1)
            pe.wait_ge(kT_copied, 1)
            pe.wait_ge(hist_ready, 1)
            for b in range(NB):
                last = nc.tensor.matmul(TB[0:rows, 0:SKEYS], q_blocks[:, b * rows:(b + 1) * rows], keysT[:, b, :],
                                        start=(b == 0), stop=(b == NB - 1))
            last.then_inc(s_ready, 1)
            pe.wait_ge(p_ready, t + 1)
            transpose(TB[:, BANK:BANK + rows], s_probs[:, 0:P], rows)
            transpose(TB[:, 2 * BANK:2 * BANK + rows], new_rows[0:rows, :], rows).then_inc(pT_ready, 1)
            pe.wait_ge(pT_copied, t + 1)
            out = TB[:, 3 * BANK:3 * BANK + rows]
            nc.tensor.matmul(out, vwin[0:NB, 1, :], new_T[0:NB, 0:rows], start=True, stop=False)
            for b in range(NB):
                cols = slice(b * HEADS, (b + 1) * HEADS)
                last = nc.tensor.matmul(out[:, cols], v_rows[:, b, :], s_probsT[:, cols], start=False, stop=(b == NB - 1))
            last.then_inc(att_ready, 1)
            conv_norm(t, NB)
            pe.wait_ge(att_copied, t + 1)
            pe.wait_ge(x1_ready, t)
            mixed_out(t, NB, 0)
            pe.wait_ge(mix_ready, t + 1)
            mixed_out(t, NB, 1).then_inc(o_ready, 1)


def experts(nc, ident, eps, norm_cols, arena, main_end, ahead_end, x1, p_prompt, p_sample, norm_ffn, sub_keys,
            peer_u, peer_v, w_ple_proj, weights, y_prompt, y_sample):
    wq_main, wq_last, w_gate, wq_in, w_fin_in = weights
    with ExitStack() as ctx:
        def sem(name):
            return ctx.enter_context(nc.semaphore(name))

        QB = ctx.enter_context(nc.psum_tensor("QB", [P, 4 * BANK], F32))
        TP = ctx.enter_context(nc.psum_tensor("TP", [P, 2 * BANK], F32))
        VA = ctx.enter_context(nc.psum_tensor("VA", [P, 2 * BANK], F32))

        take = carve(arena, ahead_end)
        iota16 = take(TOPK)
        small = take(8)
        eye8 = take(NB, NB)
        w_cols = take(NB, NB)
        idxT = take(NB).bitcast(U32)
        gatesT = take(NB)
        dots8, gelu8, w8 = take(NB), take(NB), take(NB)
        dots16 = take(2 * RING)
        dots = take(CHOICES)
        sums = take(PH)
        idx = take(2, RING).bitcast(U32)
        assert take.at[0] <= ARENA, take.at[0]
        take = carve(arena, main_end)
        w_ple = take(DPLE // P, D)
        rows = take(RING, D)
        diag = take(DIAGS, P)
        xq = take(D)
        h = take(D)
        xf = take(D)
        h3 = take(D)
        ple = take(D)
        hT = take(KD, P)
        q_cand = take(2 * PH, P)
        scores = take(2 * PH, NKEY)
        match = take(CHOICES, TOPK)
        gain = take(D)
        keysT = take(2, NKEY)
        key_rows = take(2, P)
        p_rows = take(DPLE)
        pT = take(2, P)
        top = take(2 * PH, TOPK)
        top_i = take(2 * PH, TOPK).bitcast(U32)
        top_f = take(2 * PH, TOPK)
        best = take(PH, TOPK)
        best_i = take(PH, TOPK).bitcast(U32)
        part_i = take(CHOICES).bitcast(U32)
        part = take(CHOICES)
        first_key = take(CHOICES)
        second_key = take(CHOICES)
        chosen = take(CHOICES).bitcast(U32)
        current = take(CHOICES).bitcast(U32)
        gelu = take(CHOICES)
        weights = take(CHOICES)
        gates = take(CHOICES)
        assert take.at[0] <= AHEAD, take.at[0]
        wq = [wq_main[:, k, :] for k in range(KD - 1)] + [wq_last]
        h_bc = wq_main.rearrange("p k n -> p (k n)")[:, 0:NB * D].rearrange("p (n d) -> p n d", d=D)
        cand = q_cand.rearrange("p a b -> p (a b)").rearrange("p (h c) -> p h c", c=TOPK * TOPK)
        q_flat = q_cand.rearrange("p a b -> p (a b)")
        best_flat = best.rearrange("p h k -> p (h k)")
        ssq, rms, rstd, ssq2, rms2, rstd2 = (small[:, i:i + 1] for i in range(6))

        choice_dram = nc.dram_tensor("sample_choices", (NB, CHOICES), U32, kind="Internal").ap()
        gates_dram = nc.dram_tensor("sample_gates", (NB, CHOICES), F32, kind="Internal").ap()
        h_dram = nc.dram_tensor("sample_h", (NB, D), F32, kind="Internal").ap()

        const_in, const_made = sem("b_const_in"), sem("b_const_made")
        keysT_ready, keysT_copied = sem("keysT_ready"), sem("keysT_copied")
        xq_landed, xq_rms, hn_ready, hnT_ready, hT_copied = sem("xq_landed"), sem("xq_rms"), sem("hn_ready"), sem("hnT_ready"), sem("hT_copied")
        q_ready, q_copied, sc_ready, sc_copied = sem("q_ready"), sem("q_copied"), sem("key_scores_ready"), sem("key_scores_copied")
        chosen_ready, chosen_taken, gate_shifted, gexp_ready = sem("chosen_ready"), sem("chosen_taken"), sem("gate_shifted"), sem("gate_exp_ready")
        h_copied, idx_copied = sem("h_copied"), sem("idx_copied")
        landed = [sem(f"rows_landed{i}") for i in range(RING)]
        u_used, vp_used, vd_used, dots_copied = (sem(n) for n in ("u_rows_used", "v_rows_used_pe", "v_rows_used_dve", "dots_copied"))
        gelu_ready, weights_ready, diag_ready = sem("gelu_ready"), sem("weights_ready"), sem("diag_ready")
        xf_landed, p_landed, x2_ready, x2_rms, h3_ready = sem("xf_landed"), sem("p_landed"), sem("x2_ready"), sem("x2_rms"), sem("h3_ready")
        h3T_ready, h3T_copied, pT_ready, pT_copied = sem("h3T_ready"), sem("h3T_copied"), sem("pT_ready"), sem("pT_copied")
        fin_ready, fin_copied, y_ready, y_stored = sem("finish_products_ready"), sem("finish_copied"), sem("y_ready"), sem("y_stored")
        s_stored, hbc_landed, idxT_landed, gT_landed = (sem(n) for n in ("sample_scratch_stored", "sample_h_landed", "sample_idx_landed", "sample_gates_landed"))
        g8_ready, cols_ready = sem("sample_gates_ready"), sem("weight_cols_ready")
        act_q, act_f, dve_q, dve_f, dve_k, dve_w, dve_on, act_on, pool_on = (sem(n) for n in (
            "act_rank_step", "act_finish_step", "dve_rank_step", "dve_finish_step", "dve_choose_step", "dve_weigh_step",
            "b_dve_on", "b_act_on", "b_pool_on"))
        pool_step = sem("b_pool_step")

        def hold(eng, carrier, s, value):
            eng.wait_ge(s, value)
            eng.sem_inc(carrier, 1)

        def mixed_slot(turn, i, vp, vd):
            if i < PE_SLOTS:
                return vp_used, vp + PE_FIRST + turn * PE_SLOTS + i + 1
            return vd_used, vd + turn * DVE_SLOTS + i - PE_SLOTS + 1

        block = ctx.enter_context(nc.Block())

        @block.sync
        def _(sp):
            def load_rank(q):
                sp.wait_ge(h_copied, q)
                sp.dma_start(xq, x1[bass.ds(q, 1), :, :].rearrange("o p d -> (o p) d")).then_inc(xq_landed, 16)

            def load_finish(f, first=False):
                if not first:
                    sp.wait_ge(y_stored, f * 16)
                    sp.wait_ge(pT_ready, f)
                sp.dma_start(xf, x1[bass.ds(f, 1), :, :].rearrange("o p d -> (o p) d")).then_inc(xf_landed, 16)
                sp.dma_start(p_rows, p_prompt[0, bass.ds(f * P, P), :]).then_inc(p_landed, 16)

            def store(f):
                sp.wait_ge(y_ready, f + 1)
                sp.dma_start(y_prompt[0, bass.ds(f * P, P), :], xf).then_inc(y_stored, 16)

            sp.dma_start(xq, x1[0]).then_inc(xq_landed, 16)
            sp.dma_start(gain, norm_ffn[0].partition_broadcast(P)).then_inc(const_in, 16)
            sp.dma_start(key_rows, sub_keys.rearrange("s k d -> k s d")).then_inc(const_in, 16)
            sp.dma_start(w_ple, w_ple_proj.rearrange("(k p) n -> p k n", p=P)).then_inc(w_fin_in, 16)
            load_rank(1)
            load_finish(0, first=True)
            with sp.Fori(1, NT) as t:
                load_rank(t + 1)
                store(t - 1)
                load_finish(t)
            sp.wait_ge(hn_ready, NT + 1)
            sp.dma_start(h_dram, xq[0:NB, :]).then_inc(s_stored, 16)
            sp.wait_ge(q_ready, NT + 1)
            sp.wait_ge(s_stored, 16)
            for n in range(NB):
                sp.dma_start(h_bc[:, n, :], h_dram[n].partition_broadcast(P)).then_inc(hbc_landed, 16)
            sp.wait_ge(chosen_ready, NT + 1)
            sp.dma_start(choice_dram, chosen[0:NB, :]).then_inc(s_stored, 16)
            sp.wait_ge(s_stored, 2 * 16)
            sp.dma_start(idxT, choice_dram.rearrange("n c -> c n"), allow_slow_non_contiguous=True).then_inc(idxT_landed, 16)
            sp.wait_ge(g8_ready, 1)
            sp.dma_start(gates_dram, gates[0:NB, :]).then_inc(s_stored, 16)
            sp.wait_ge(s_stored, 3 * 16)
            sp.dma_start(gatesT, gates_dram.rearrange("n c -> c n"), allow_slow_non_contiguous=True).then_inc(gT_landed, 16)
            store(NT - 1)
            sp.wait_ge(y_stored, NT * 16)
            sp.wait_ge(pT_ready, NT)
            sp.dma_start(xf[0:NB, :], x1[NT, 0:NB, :]).then_inc(xf_landed, 16)
            sp.dma_start(p_rows[0:NB, :], p_sample[:, 0, :]).then_inc(p_landed, 16)
            sp.wait_ge(y_ready, NT + 1)
            sp.dma_start(y_sample[:, 0, :], xf[0:NB, :]).then_inc(y_stored, 16)
            sp.wait_ge(y_stored, (NT + 1) * 16)

        @block.gpsimd
        def _(pool):
            nc.gpsimd.iota(iota16, [[1, TOPK]], base=0, channel_multiplier=0,
                           allow_small_or_imprecise_dtypes=True).then_inc(const_made, 1)
            steps = Chain(pool, pool_step)
            steps.link(nc.gpsimd.memset(eye8, 0.0))
            nc.gpsimd.affine_select(out=eye8, in_=eye8, compare_op=ALU.not_equal, fill=1.0, base=0,
                                    pattern=[[1, NB], [-1, NB]], channel_multiplier=0).then_inc(const_made, 1)

            def gather(table, i, index):
                nc.gpsimd.indirect_dma_start(rows[:, i, :], None, table, bass.IndirectOffsetOnAxis(ap=index, axis=0)
                                             ).then_inc(landed[i], 16)

            def gather_pair(pair, table, number, freed):
                for half in range(2):
                    nc.gpsimd.tensor_copy(idx[:, half, :], current[:, bass.ds((2 * pair + half) * RING, RING)]
                                          ).then_inc(idx_copied, 1)
                    hold(pool, pool_on, idx_copied, number + half + 1)
                    for i in range(RING):
                        if freed(half, i) is not None:
                            hold(pool, pool_on, *freed(half, i))
                        gather(table, i, idx[:, half, i:i + 1])

            def tile(t, first):
                hold(pool, pool_on, chosen_ready, t + 1)
                nc.gpsimd.tensor_copy(current, chosen).then_inc(chosen_taken, 1)
                hold(pool, pool_on, chosen_taken, t + 1)
                u, vp, vd = t * CHOICES, t * PE_STEPS, t * DVE_STEPS
                n = t * 2 * CHOICES // RING

                def u_freed(turn, i):
                    return u_used, u + turn * RING + i + 1

                def v_freed(turn, i):
                    return vp_used, vp + turn * RING + i + 1

                def mixed_freed(turn, i):
                    return mixed_slot(turn, i, vp, vd)

                def last_tile(i):
                    return None if first else mixed_slot(0, i, vp - PE_FIRST - PE_SLOTS, vd - DVE_SLOTS)

                gather_pair(0, peer_u, n, lambda half, i: u_freed(0, i) if half else last_tile(i))
                with pool.Fori(1, PAIRS) as pair:
                    gather_pair(pair, peer_u, n + 2 * pair, lambda half, i: u_freed(2 * pair + half - 1, i))
                n += CHOICES // RING
                gather_pair(0, peer_v, n, lambda half, i: v_freed(0, i) if half else u_freed(2 * PAIRS - 1, i))
                with pool.Fori(1, PE_PAIRS) as pair:
                    gather_pair(pair, peer_v, n + 2 * pair, lambda half, i: v_freed(2 * pair + half - 1, i))
                gather_pair(PE_PAIRS, peer_v, n + 2 * PE_PAIRS,
                            lambda half, i: mixed_freed(0, i) if half else v_freed(2 * PE_PAIRS - 1, i))
                with pool.Fori(PE_PAIRS + 1, PAIRS) as pair:
                    gather_pair(pair, peer_v, n + 2 * pair, lambda half, i: mixed_freed(2 * (pair - PE_PAIRS) + half - 1, i))

            tile(0, True)
            with pool.Fori(1, NT) as t:
                tile(t, False)
            pool.wait_ge(idxT_landed, 16)
            for n in range(NB):
                pool.wait_ge(*mixed_slot(0, n, (NT - 1) * PE_STEPS + (MIXED_TURNS - 1) * PE_SLOTS, NT * DVE_STEPS - DVE_SLOTS))
                gather(peer_u, n, idxT[:, n:n + 1])
            for n in range(NB):
                pool.wait_ge(u_used, NT * CHOICES + n + 1)
                gather(peer_v, n, idxT[:, n:n + 1])

        ACT_Q, ACT_F = 1, 1

        @block.scalar
        def _(act):
            def rank_norm(q):
                steps = Chain(act, act_q, q * ACT_Q)
                hold(act, act_on, xq_landed, (q + 1) * 16)
                steps.link(nc.scalar.activation(q_flat[:, 0:D], xq, ACT.Square, accum_out=ssq))
                nc.scalar.activation(rms, ssq, ACT.Sqrt, bias=eps[:, :], scale=1.0 / D).then_inc(xq_rms, 1)
                assert steps.n == ACT_Q

            def rank(q):
                act.wait_ge(hnT_ready, q + 1)
                nc.scalar.activation(hT, TP[:, :].rearrange("p (k t) -> p k t", t=P), ACT.Copy).then_inc(hT_copied, 1)
                act.wait_ge(q_ready, q + 1)
                nc.scalar.activation(q_flat, QB[:, :], ACT.Copy).then_inc(q_copied, 1)
                act.wait_ge(sc_ready, q + 1)
                nc.scalar.activation(scores.rearrange("p a b -> p (a b)"), QB[:, :], ACT.Copy).then_inc(sc_copied, 1)

            def finish(f, R):
                steps = Chain(act, act_f, f * ACT_F)
                act.wait_ge(x2_ready, f + 1)
                steps.link(nc.scalar.activation(ple[0:R, :], xf[0:R, :], ACT.Square, accum_out=ssq2[0:R, :]))
                nc.scalar.activation(rms2[0:R, :], ssq2[0:R, :], ACT.Sqrt, bias=eps[0:R, :], scale=1.0 / D).then_inc(x2_rms, 1)
                act.wait_ge(pT_ready, f + 1)
                nc.scalar.activation(pT[:, :, 0:R], QB[:, 0:2 * P].rearrange("p (k t) -> p k t", t=P)[:, :, 0:R],
                                     ACT.Copy).then_inc(pT_copied, 1)
                act.wait_ge(fin_ready, f + 1)
                nc.scalar.activation(h3[0:R, :], QB[0:R, D:2 * D], ACT.Sigmoid)
                nc.scalar.activation(ple[0:R, :], QB[0:R, 0:D], ACT.Copy).then_inc(fin_copied, 1)
                assert steps.n == ACT_F

            def exponentials(q):
                act.wait_ge(gate_shifted, q + 1)
                nc.scalar.activation(gates, gates, ACT.Exp).then_inc(gexp_ready, 1)

            def diagonal(t, count, slot, choice, first):
                if not first:
                    hold(act, act_on, vp_used, t * PE_STEPS + count - DIAGS + 1)
                nc.scalar.activation(diag[:, slot, :], ident[:, :], ACT.Copy,
                                     scale=weights[:, bass.ds(choice, 1)]).then_inc(diag_ready, 1)

            def tile(t, first):
                rank_norm(t + 1)
                if not first:
                    finish(t - 1, P)
                rank(t + 1)
                act.wait_ge(dots_copied, (t + 1) * PAIRS)
                nc.scalar.activation(gelu, dots, ACT.Gelu).then_inc(gelu_ready, 1)
                hold(act, act_on, weights_ready, t + 1)
                for s in range(2 * RING):
                    diagonal(t, s, s % DIAGS, s, first and s < DIAGS)
                with act.Fori(1, PE_PAIRS) as pair:
                    for s in range(2 * RING):
                        diagonal(t, pair * 2 * RING + s, s % DIAGS, pair * 2 * RING + s, False)
                with act.Fori(PE_PAIRS, PAIRS) as pair:
                    for half in range(2):
                        for i in range(PE_SLOTS):
                            k = half * PE_SLOTS + i
                            diagonal(t, PE_FIRST + (pair - PE_PAIRS) * 2 * PE_SLOTS + k, k % DIAGS, (2 * pair + half) * RING + i, False)
                exponentials(t + 1)

            act.wait_ge(keysT_ready, 1)
            nc.scalar.activation(keysT, TP[:, 0:2 * P].rearrange("p (s k) -> p s k", s=2), ACT.Copy).then_inc(keysT_copied, 1)
            rank_norm(0)
            rank(0)
            exponentials(0)
            tile(0, True)
            with act.Fori(1, NT) as t:
                tile(t, False)
            finish(NT - 1, P)
            act.wait_ge(u_used, NT * CHOICES + NB)
            nc.scalar.activation(gelu8, dots8, ACT.Gelu).then_inc(gelu_ready, 1)
            finish(NT, NB)

        DVE_Q, DVE_F, DVE_K, DVE_W = 1, 2, 21, 3
        TT = nc.vector.tensor_tensor

        @block.vector
        def _(dve):
            def normalise(q):
                steps = Chain(dve, dve_q, q * DVE_Q)
                dve.wait_ge(xq_rms, q + 1)
                steps.link(nc.vector.reciprocal(rstd, rms))
                nc.vector.scalar_tensor_tensor(out=xq, in0=xq, scalar=rstd, in1=gain, op0=ALU.mult, op1=ALU.mult).then_inc(hn_ready, 1)
                assert steps.n == DVE_Q

            def take_h(q):
                hold(dve, dve_on, hn_ready, q + 1)
                dve.wait_ge(hnT_ready, q + 1)
                nc.vector.tensor_copy(h, xq).then_inc(h_copied, 1)
                hold(dve, dve_on, h_copied, q + 1)

            def choose(q, first):
                steps = Chain(dve, dve_k, q * DVE_K)

                def step(ins):
                    steps.link(ins)
                    dve.sem_inc(dve_on, 1)

                def best16(values, n, out, out_i, lists):
                    for half in range(2):
                        part8 = slice(8 * half, 8 * half + 8)
                        for m in range(lists):
                            last = nc.vector.max(out[:, m, part8], values[:, m, :])
                        step(last)
                        for m in range(lists):
                            last = nc.vector.max_index(out_i[:, m, part8], out[:, m, part8], values[:, m, :])
                        step(last)
                        if half == 0:
                            for m in range(lists):
                                last = nc.vector.match_replace(values[:, m, :], out[:, m, part8], values[:, m, :], -3.0e38)
                            step(last)

                hold(dve, dve_on, sc_copied, q + 1)
                best16(scores, NKEY, top, top_i, 2 * PH)
                nc.vector.tensor_copy(top_f, top_i)
                pairs = cand.rearrange("p h (i j) -> p h i j", j=TOPK)
                halves = top.rearrange("p (h s) k -> p h s k", s=2)
                step(TT(pairs, halves[:, :, 0, :].unsqueeze(3).to_broadcast([P, PH, TOPK, TOPK]),
                        halves[:, :, 1, :].unsqueeze(2).to_broadcast([P, PH, TOPK, TOPK]), ALU.add))
                best16(cand, TOPK * TOPK, best, best_i, PH)
                keys = top_f.rearrange("p (h s) k -> p h s k", s=2)
                flat_i = best_i.rearrange("p h k -> p (h k)")
                for s, (op, arg, number) in enumerate(((ALU.logical_shift_right, 4, first_key), (ALU.bitwise_and, 15, second_key))):
                    steps.link(nc.vector.tensor_scalar(part_i, flat_i, arg, None, op))
                    steps.link(nc.vector.tensor_copy(part, part_i))
                    steps.link(TT(match, part.unsqueeze(2).to_broadcast([P, CHOICES, TOPK]),
                                  iota16.unsqueeze(1).to_broadcast([P, CHOICES, TOPK]), ALU.is_equal))
                    by_head = match.rearrange("p (h k) i -> p h k i", k=TOPK)
                    steps.link(TT(by_head, by_head, keys[:, :, s, :].unsqueeze(2).to_broadcast([P, PH, TOPK, TOPK]), ALU.mult))
                    steps.link(nc.vector.tensor_reduce(number, match, AX.X, ALU.add))
                if not first:
                    dve.wait_ge(chosen_taken, q)
                nc.vector.scalar_tensor_tensor(out=chosen, in0=first_key, scalar=float(NKEY), in1=second_key,
                                               op0=ALU.mult, op1=ALU.add).then_inc(chosen_ready, 1)
                TT(gates.rearrange("p (h k) -> p h k", k=TOPK), best, best[:, :, 0:1].to_broadcast([P, PH, TOPK]),
                   ALU.subtract).then_inc(gate_shifted, 1)
                assert steps.n == DVE_K, steps.n

            def dot_pair(t, pair, first):
                for s in range(2 * RING):
                    i = s % RING
                    dve.wait_ge(landed[i], (t * 2 * CHOICES // RING + 2 * pair + s // RING + 1) * 16)
                    if s == 0 and not first:
                        dve.wait_ge(dots_copied, t * PAIRS + pair)
                    nc.vector.tensor_tensor_reduce(out=rows[:, i, :], in0=rows[:, i, :], in1=h, scale=1.0, scalar=0.0,
                                                   op0=ALU.mult, op1=ALU.add, accum_out=dots16[:, s:s + 1]).then_inc(u_used, 1)
                hold(dve, dve_on, u_used, t * CHOICES + (pair + 1) * 2 * RING)
                nc.vector.tensor_copy(dots[:, bass.ds(pair * 2 * RING, 2 * RING)], dots16).then_inc(dots_copied, 1)

            def normalise_gates(t, R, steps):
                per_head = gates[0:R, :].rearrange("p (h k) -> p h k", k=TOPK)
                dve.wait_ge(gexp_ready, t + 1)
                steps.link(nc.vector.tensor_reduce(sums[0:R, :], per_head, AX.X, ALU.add))
                steps.link(nc.vector.reciprocal(sums[0:R, :], sums[0:R, :]))
                return TT(per_head, per_head, sums[0:R, :].unsqueeze(2).to_broadcast([R, PH, TOPK]), ALU.mult)

            def finish_x2(f, R, v_count):
                dve.wait_ge(vp_used, v_count)
                dve.wait_ge(xf_landed, (f + 1) * 16)
                TT(xf[0:R, :], VA[0:R, :], xf[0:R, :], ALU.add).then_inc(x2_ready, 1)

            def finish_norm(f, R):
                steps = Chain(dve, dve_f, f * DVE_F)
                dve.wait_ge(x2_rms, f + 1)
                steps.link(nc.vector.reciprocal(rstd2[0:R, :], rms2[0:R, :]))
                nc.vector.tensor_scalar(h3[0:R, :], xf[0:R, :], rstd2[0:R, :], None, ALU.mult).then_inc(h3_ready, 1)

            def finish_gain(f, R):
                dve.wait_ge(h3T_ready, f + 1)
                TT(hT[:, :, 0:R], TP[:, :].rearrange("p (k t) -> p k t", t=P)[:, :, 0:R],
                   norm_cols[:, 1, :].unsqueeze(2).to_broadcast([P, KD, R]), ALU.mult).then_inc(h3T_copied, 1)

            def finish_sum(f, R):
                steps = Chain(dve, dve_f, f * DVE_F + 1)
                dve.wait_ge(fin_copied, f + 1)
                steps.link(TT(ple[0:R, :], ple[0:R, :], h3[0:R, :], ALU.mult))
                TT(xf[0:R, :], xf[0:R, :], ple[0:R, :], ALU.add).then_inc(y_ready, 1)

            def add_pair(t, pair, first):
                for half in range(2):
                    for i in range(PE_SLOTS, RING):
                        done = t * DVE_STEPS + (2 * (pair - PE_PAIRS) + half) * DVE_SLOTS + i - PE_SLOTS
                        dve.wait_ge(landed[i], ((2 * t + 1) * CHOICES // RING + 2 * pair + half + 1) * 16)
                        if not first or half or i > PE_SLOTS:
                            dve.wait_ge(vd_used, done)
                        nc.vector.scalar_tensor_tensor(out=xf, in0=rows[:, i, :],
                                                       scalar=weights[:, bass.ds((2 * pair + half) * RING + i, 1)],
                                                       in1=xf, op0=ALU.mult, op1=ALU.add).then_inc(vd_used, 1)

            def tile(t, first):
                dot_pair(t, 0, first)
                if not first:
                    finish_x2(t - 1, P, t * PE_STEPS)
                dot_pair(t, 1, False)
                normalise(t + 1)
                if not first:
                    finish_norm(t - 1, P)
                dot_pair(t, 2, False)
                if not first:
                    finish_gain(t - 1, P)
                with dve.Fori(3, PAIRS) as pair:
                    dot_pair(t, pair, False)
                if not first:
                    finish_sum(t - 1, P)
                steps = Chain(dve, dve_w, t * DVE_W)
                steps.link(normalise_gates(t, P, steps))
                assert steps.n == DVE_W
                dve.wait_ge(gelu_ready, t + 1)
                TT(weights, gates, gelu, ALU.mult).then_inc(weights_ready, 1)
                take_h(t + 1)
                hold(dve, dve_on, weights_ready, t + 1)
                choose(t + 1, False)
                dve.wait_ge(xf_landed, (t + 1) * 16)
                add_pair(t, PE_PAIRS, first)
                with dve.Fori(PE_PAIRS + 1, PAIRS) as pair:
                    add_pair(t, pair, False)

            dve.wait_ge(const_in, 2 * 16)
            dve.wait_ge(const_made, 2)
            normalise(0)
            take_h(0)
            choose(0, True)
            tile(0, True)
            with dve.Fori(1, NT) as t:
                tile(t, False)
            steps = Chain(dve, dve_w, NT * DVE_W)
            normalise_gates(NT, NB, steps).then_inc(g8_ready, 1)
            finish_x2(NT - 1, P, NT * PE_STEPS)
            finish_norm(NT - 1, P)
            finish_gain(NT - 1, P)
            dve.wait_ge(hbc_landed, NB * 16)
            for n in range(NB):
                dve.wait_ge(landed[n], (NT * 2 * CHOICES // RING + 1) * 16)
                nc.vector.tensor_tensor_reduce(out=rows[:, n, :], in0=rows[:, n, :], in1=h_bc[:, n, :], scale=1.0, scalar=0.0,
                                               op0=ALU.mult, op1=ALU.add, accum_out=dots8[:, n:n + 1]).then_inc(u_used, 1)
            finish_sum(NT - 1, P)
            dve.wait_ge(gelu_ready, NT + 1)
            dve.wait_ge(gT_landed, 16)
            steps.link(TT(w8, gatesT, gelu8, ALU.mult))
            TT(w_cols, eye8, w8.unsqueeze(2).to_broadcast([P, NB, NB]), ALU.mult).then_inc(cols_ready, 1)
            finish_x2(NT, NB, NT * PE_STEPS + NB)
            finish_norm(NT, NB)
            finish_gain(NT, NB)
            finish_sum(NT, NB)

        @block.tensor
        def _(pe):
            def transpose(out, src, rows_):
                return nc.tensor.transpose(out, src, ident[0:rows_, 0:rows_])

            def rank(q):
                pe.wait_ge(hn_ready, q + 1)
                for k in range(KD):
                    last = transpose(TP[:, k * P:(k + 1) * P], xq[:, k * P:(k + 1) * P], P)
                last.then_inc(hnT_ready, 1)
                pe.wait_ge(hT_copied, q + 1)
                for m in range(2 * PH):
                    for k in range(KD):
                        last = nc.tensor.matmul(QB[:, m * P:(m + 1) * P], wq[k][:, m * P:(m + 1) * P], hT[:, k, :],
                                                start=(k == 0), stop=(k == KD - 1))
                last.then_inc(q_ready, 1)
                pe.wait_ge(q_copied, q + 1)
                for m in range(2 * PH):
                    last = nc.tensor.matmul(QB[:, m * P:(m + 1) * P], q_cand[:, m, :], keysT[:, m % 2, :], start=True, stop=True)
                last.then_inc(sc_ready, 1)

            def finish(f, R):
                pe.wait_ge(p_landed, (f + 1) * 16)
                pe.wait_ge(sc_copied, f + 2 if R == P else NT + 1)
                for k in range(2):
                    last = transpose(QB[:, k * P:k * P + R], p_rows[0:R, k * P:(k + 1) * P], R)
                last.then_inc(pT_ready, 1)
                pe.wait_ge(h3_ready, f + 1)
                for k in range(KD):
                    last = transpose(TP[:, k * P:k * P + R], h3[0:R, k * P:(k + 1) * P], R)
                last.then_inc(h3T_ready, 1)
                pe.wait_ge(h3T_copied, f + 1)
                for c in range(0, D, BANK):
                    for k in range(KD):
                        nc.tensor.matmul(QB[0:R, D + c:D + c + BANK], hT[:, k, 0:R], w_gate[:, k, c:c + BANK],
                                         start=(k == 0), stop=(k == KD - 1))
                pe.wait_ge(pT_copied, f + 1)
                for c in range(0, D, BANK):
                    for k in range(2):
                        last = nc.tensor.matmul(QB[0:R, c:c + BANK], pT[:, k, 0:R], w_ple[:, k, c:c + BANK],
                                                start=(k == 0), stop=(k == 1))
                last.then_inc(fin_ready, 1)

            def add_row(t, count, slot, diagonal, turn, start=False, stop=False):
                pe.wait_ge(diag_ready, t * PE_STEPS + count + 1)
                pe.wait_ge(landed[slot], ((2 * t + 1) * CHOICES // RING + turn + 1) * 16)
                for c in range(0, D, BANK):
                    last = nc.tensor.matmul(VA[:, c:c + BANK], diag[:, diagonal, :], rows[:, slot, c:c + BANK], start=start, stop=stop)
                last.then_inc(vp_used, 1)

            def add_pair(t, pair, start=False):
                for s in range(2 * RING):
                    add_row(t, pair * 2 * RING + s, s % RING, s % DIAGS, 2 * pair + s // RING, start=start and s == 0)

            def add_mixed_pair(t, pair, stop=False):
                for half in range(2):
                    for i in range(PE_SLOTS):
                        k = half * PE_SLOTS + i
                        add_row(t, PE_FIRST + (pair - PE_PAIRS) * 2 * PE_SLOTS + k, i, k % DIAGS, 2 * pair + half,
                                stop=stop and k == 2 * PE_SLOTS - 1)

            def tile(t, first):
                if not first:
                    finish(t - 1, P)
                rank(t + 1)
                if not first:
                    pe.wait_ge(x2_ready, t)
                add_pair(t, 0, start=True)
                with pe.Fori(1, PE_PAIRS) as pair:
                    add_pair(t, pair)
                with pe.Fori(PE_PAIRS, PAIRS - 1) as pair:
                    add_mixed_pair(t, pair)
                add_mixed_pair(t, PAIRS - 1, stop=True)

            pe.wait_ge(const_in, 2 * 16)
            for s in range(2):
                last = transpose(TP[:, s * P:(s + 1) * P], key_rows[:, s, :], P)
            last.then_inc(keysT_ready, 1)
            pe.wait_ge(keysT_copied, 1)
            pe.wait_ge(wq_in, KD * 16)
            pe.wait_ge(w_fin_in, 2 * 16)
            rank(0)
            pe.wait_ge(sc_copied, 1)
            tile(0, True)
            with pe.Fori(1, NT) as t:
                tile(t, False)
            finish(NT - 1, P)
            pe.wait_ge(cols_ready, 1)
            for n in range(NB):
                pe.wait_ge(landed[n], (NT * 2 * CHOICES // RING + 2) * 16)
                for c in range(0, D, BANK):
                    last = nc.tensor.matmul(VA[0:NB, c:c + BANK], w_cols[:, n, :], rows[:, n, c:c + BANK], start=(n == 0),
                                            stop=(n == NB - 1))
                last.then_inc(vp_used, 1)
            finish(NT, NB)


_INS = ['x_prompt', 'x_sample', 'cache_k', 'cache_v', 'state_conv', 'p_prompt', 'p_sample', 'norm_mix', 'w_in', 'q_gain',
        'k_gain', 'attn_sinks', 'conv_dw_w', 'conv_dw_b', 'conv_ln_g', 'conv_ln_b', 'w_out', 'norm_ffn', 'peer_wq',
        'peer_sub_keys', 'peer_u', 'peer_v', 'norm_ple', 'w_ple_proj', 'w_ple_gate']
_OUTS = [(1, SEQ, D), (NB, 1, D), (1, 1, P, KV, HD), (1, 1, P, KV, HD), (1, 1, HIST, CONV), (1, NB, P, KV, HD),
         (1, NB, P, KV, HD), (1, NB, HIST, CONV)]


def kernel(**inputs):
    import numpy as _np
    import concourse.bacc as _bacc
    from concourse import mybir as _mybir
    from concourse.bass_utils import run_bass_kernel_spmd as _run

    nc = _bacc.Bacc("TRN2", target_bir_lowering=False, num_devices=1)
    arrays, args = {}, []
    for name in _INS:
        a = _np.ascontiguousarray(inputs[name])
        arrays[f"in_{name}_dram"] = a
        args.append(nc.dram_tensor(f"in_{name}_dram", a.shape, _mybir.dt.from_np(a.dtype), kind="ExternalInput").ap())
    for i, shape in enumerate(_OUTS):
        args.append(nc.dram_tensor(f"out_{i}_dram", shape, _mybir.dt.float32, kind="ExternalOutput").ap())
    hymba_step(nc, *args)
    r = _run(nc, [arrays], core_ids=[0])
    return tuple(r.results[0][f"out_{i}_dram"] for i in range(len(_OUTS)))
```

```python
import concourse.bass as bass
from concourse import mybir
from contextlib import ExitStack

F32 = mybir.dt.float32
U32 = mybir.dt.uint32
ALU = mybir.AluOpType
ACT = mybir.ActivationFunctionType
AX = mybir.AxisListType

P = 128
D = 1024
KD = D // P
SEQ = 1024
NT = SEQ // P
NB = 8
HEADS, KV, HD = 8, 2, 64
GROUP = HEADS // KV
QW, KW = HEADS * HD, KV * HD
CONV = D - QW
CT = CONV // P
TAPS = 31
HIST = TAPS - 1
DIN = QW + 2 * KW + 2 * CONV
ZK, ZV, ZA, ZG = QW, QW + KW, QW + 2 * KW, QW + 2 * KW + CONV
WIN = 2 * P
SKEYS = P + 1
EPS = 1e-6
NEG = -1e30
AHEAD = 42136
ARENA = 52900
BANK = 512
PH = 8
TOPK = 16
NKEY = 128
CHOICES = PH * TOPK
DPLE = 256
RING = 8
PAIRS = CHOICES // (2 * RING)
PE_PAIRS = 2
PE_SLOTS = 5
DVE_SLOTS = RING - PE_SLOTS
PARTS = 4
DIAGS = 2
PE_FIRST = PE_PAIRS * 2 * RING
MIXED_TURNS = 2 * (PAIRS - PE_PAIRS)
PE_STEPS = PE_FIRST + MIXED_TURNS * PE_SLOTS
DVE_STEPS = MIXED_TURNS * DVE_SLOTS


class Chain:

    def __init__(self, eng, sem, base=0):
        self.eng, self.sem, self.base, self.n = eng, sem, base, 0

    def link(self, ins):
        self.n += 1
        ins.then_inc(self.sem, 1)
        self.eng.wait_ge(self.sem, self.base + self.n)


def carve(arena, start):
    at = [start]

    def take(*shape):
        size = 1
        for s in shape:
            size *= s
        view = arena[:, at[0]:at[0] + size]
        at[0] += size
        if len(shape) == 2:
            view = view.rearrange("p (a b) -> p a b", b=shape[1])
        elif len(shape) == 3:
            view = view.rearrange("p (a b c) -> p a b c", b=shape[1], c=shape[2])
        return view
    take.at = at
    return take


def over_partitions(vector, n):
    return vector.partition_broadcast(n)


def hymba_step(nc, x_prompt, x_sample, cache_k, cache_v, state_conv, p_prompt, p_sample, norm_mix, w_in,
               q_gain, k_gain, attn_sinks, conv_dw_w, conv_dw_b, conv_ln_g, conv_ln_b, w_out, norm_ffn,
               peer_wq, peer_sub_keys, peer_u, peer_v, norm_ple, w_ple_proj, w_ple_gate,
               y_prompt, y_sample, new_k_prompt, new_v_prompt, new_conv_prompt,
               new_k_sample, new_v_sample, new_conv_sample):
    with ExitStack() as ctx:
        def sb(name, shape, dt=F32):
            return ctx.enter_context(nc.sbuf_tensor(name, shape, dt))

        ident = sb("ident", [P, P])
        eps = sb("eps", [P, 1])
        norm_cols = sb("norm_cols", [P, 2, KD])
        arena = sb("arena", [P, ARENA])
        ahead = carve(arena, 0)
        wq_main = ahead(KD - 1, 2 * PH * P)
        main_end = ahead.at[0]
        ahead.at[0] = AHEAD
        ranking = dict(
            wq_main=wq_main,
            wq_last=ahead(2 * PH * P),
            xq=ahead(D),
            gain=ahead(D),
            key_rows=ahead(2, P),
            keysT=ahead(2, NKEY),
            hT=ahead(KD, P),
            q_cand=ahead(2 * PH, P),
            scores=ahead(2 * PH, NKEY),
            current=ahead(CHOICES).bitcast(U32),
            small=ahead(8))
        for name in ("wq_in", "rank_rows_in", "xq_landed", "xq_rms", "hn_ready", "hnT_ready", "hT_copied", "keysT_ready",
                     "keysT_copied", "act_rank_step", "dve_rank_step"):
            ranking[name] = ctx.enter_context(nc.semaphore(name))
        x1 = nc.dram_tensor("x1", (NT + 1, P, D), F32, kind="Internal").ap()

        mixer(nc, ident, eps, norm_cols, arena, x1, x_prompt, x_sample, cache_k[0], cache_v[0], state_conv[0],
              norm_mix, w_in[0], q_gain, k_gain, attn_sinks, conv_dw_w[0], conv_dw_b, conv_ln_g, conv_ln_b,
              w_out[0], norm_ple, new_k_prompt, new_v_prompt, new_conv_prompt, new_k_sample, new_v_sample,
              new_conv_sample, ranking, norm_ffn, peer_wq[0], peer_sub_keys[0])
        experts(nc, ident, eps, norm_cols, arena, main_end, ahead.at[0], x1, p_prompt[0], p_sample[0],
                peer_u[0], peer_v[0], w_ple_proj[0], w_ple_gate[0], ranking, y_prompt, y_sample)


def mixer(nc, ident, eps, norm_cols, arena, x1, x_prompt, x_sample, cache_k, cache_v, state_conv, norm_mix, w_in,
          q_gain, k_gain, attn_sinks, conv_dw_w, conv_dw_b, conv_ln_g, conv_ln_b, w_out, norm_ple,
          new_k_prompt, new_v_prompt, new_conv_prompt, new_k_sample, new_v_sample, new_conv_sample, ranking,
          norm_ffn, peer_wq, sub_keys):
    wq_main, wq_last, wq_in = ranking["wq_main"], ranking["wq_last"], ranking["wq_in"]
    xq, small = ranking["xq"], ranking["small"]
    with ExitStack() as ctx:
        def sem(name):
            return ctx.enter_context(nc.semaphore(name))

        ZB = ctx.enter_context(nc.psum_tensor("ZB", [P, 4 * BANK], F32))
        TB = ctx.enter_context(nc.psum_tensor("TB", [P, 4 * BANK], F32))

        take = carve(arena, 0)
        win_w = take(KD, DIN)
        wout_w = take(KD, D)
        x_in = take(D)
        x_res = take(D)
        xn = take(D)
        hT = take(KD, P)
        squares = take(D)
        qk = take(QW + KW)
        vwin = take(2, KW)
        glu = take(CONV)
        gate = take(CONV)
        kwin = take(WIN)
        qT = take(GROUP, P)
        gluT = take(CT, HIST + P)
        bias = take(HEADS, WIN)
        bias_prev = take(HEADS, P)
        probs = take(HEADS, WIN)
        probsT = take(2 * HEADS, P)
        mixedT = take(KD, P)
        acc = take(CT, P)
        conv_y = take(CT, P)
        conv_s = take(CT, P)
        chan_rows = take(CONV)
        chan = take(CT, TAPS + 3)
        norm_rows = take(P)
        qg = take(HD)
        kg = take(HD)
        sinks = take(HEADS)
        sink_rows = take(1)
        stat = take(64)
        s_take = carve(arena, take.at[0])
        sbias = s_take(P + 4)
        new_rows = s_take(P)
        own = s_take(NB)
        new_T = s_take(P)
        take.at[0] = s_take.at[0]
        q_blocks = bias_prev.rearrange("p a b -> p (a b)")[:, 0:NB * 72]
        k_rows = probsT[:, 0:8, :]
        v_rows = probsT[:, 8:16, :]
        keysT = bias.rearrange("p a b -> p (a b)")[:, 0:NB * SKEYS].rearrange("p (b k) -> p b k", k=SKEYS)
        st_rows = probs.rearrange("p a b -> p (a b)")[:, 0:2 * CONV].rearrange("p (g c) -> p g c", g=2)
        hist = hT.rearrange("p a b -> p (a b)")[:, 0:CT * NB * TAPS].rearrange("p (c b j) -> p c b j", c=CT, b=NB)
        prod = squares[:, 0:CT * NB * TAPS].rearrange("p (c b j) -> p c b j", c=CT, b=NB)
        assert take.at[0] <= ARENA, take.at[0]
        s_qT = TB[:, 0:QW].rearrange("p (i t) -> p i t", t=P)

        ssq, rms, rstd = stat[:, 0:1], stat[:, 1:2], stat[:, 2:3]
        ss10, rms10, rstd10 = stat[:, 3:13], stat[:, 13:23], stat[:, 23:33]
        top, ntop, esink = stat[:, 33:41], stat[:, 41:49], stat[:, 49:57]
        more = take(64)
        den, rden = more[:, 0:8], more[:, 8:16]
        bn6, mv, rms_c, rstd_c, dsink = more[:, 16:22], more[:, 22:24], more[:, 24:25], more[:, 25:26], more[:, 26:34]
        assert take.at[0] <= AHEAD, take.at[0]

        const_made, const_in, out_w_in = sem("const_made"), sem("const_in"), sem("w_out_in")
        win_in = [sem(f"w_in_in{k}") for k in range(KD)]
        rows_in, cols_T, cols_made = sem("const_rows_in"), sem("const_cols_T"), sem("const_cols_made")
        window_cleared = sem("window_cleared")
        x_landed, res_landed, x1_stored = sem("x_landed"), sem("x_res_landed"), sem("x1_stored")
        squared, xn_ready, xT_ready, hT_ready, z_ready = (sem(n) for n in ("x_squared", "xn_ready", "xT_ready", "hT_ready", "z_ready"))
        qk_squared, qk_summed, qk_rms, sig_ready = sem("qk_squared"), sem("qk_summed"), sem("qk_rms_ready"), sem("gate_ready")
        v_ready = sem("v_ready")
        qk_ready, glu_ready, qkT_ready, gluT_ready = sem("qk_ready"), sem("glu_ready"), sem("qkT_ready"), sem("gluT_ready")
        qk_copied, s_ready, m_ready, bias_set, e_ready = sem("qk_copied"), sem("scores_ready"), sem("max_ready"), sem("bias_set"), sem("exp_ready")
        p_ready, pT_ready, pT_copied, att_ready, att_copied = sem("probs_ready"), sem("probsT_ready"), sem("probsT_copied"), sem("att_ready"), sem("att_copied")
        conv_done, c_ready, cvar_ready, crms_ready = sem("conv_done"), sem("conv_tok_ready"), sem("conv_var_ready"), sem("conv_rms_ready")
        ln_ready, lnT_ready, cy_ready, mix_ready, o_ready, x1_ready = (sem(n) for n in ("ln_ready", "lnT_ready", "conv_affine_ready", "mixed_ready", "w_out_ready", "x1_ready"))
        tail_stored, samples_in, outs_stored, copied_over = sem("prompt_tail_stored"), sem("samples_in"), sem("outs_stored"), sem("caches_copied")
        sbias_in, kT_ready, kT_copied, stT_ready, hist_ready = sem("sbias_in"), sem("cacheT_ready"), sem("cacheT_copied"), sem("stateT_ready"), sem("hist_ready")
        zero_stored = sem("x1_pad_stored")
        act_step, dve_step, act_on, dve_on, pool_on = sem("act_step"), sem("dve_step"), sem("act_on"), sem("dve_on"), sem("pool_on")
        kT_new, bias_out = sem("new_key_copied"), sem("bias_row_stored")
        bias_row = nc.dram_tensor("bias_row", (1, HEADS, SKEYS), F32, kind="Internal").ap()
        gluT_copied = sem("gluT_copied")
        zero_ready, new_glu_taken = sem("zeros_ready"), sem("new_glu_taken")
        s_probs = qT.rearrange("p i t -> p (i t)")[0:HEADS * NB, 0:SKEYS]
        s_probsT = qT.rearrange("p i t -> p (i t)")[:, 256:256 + HEADS * NB]
        pool_step = sem("pool_step")

        def hold(eng, carrier, s, value):
            eng.wait_ge(s, value)
            eng.sem_inc(carrier, 1)

        block = ctx.enter_context(nc.Block())

        @block.sync
        def _(sp):
            def load_x(t):
                sp.wait_ge(xn_ready, t)
                sp.dma_start(x_in, x_prompt[0, bass.ds(t * P, P), :]).then_inc(x_landed, 16)

            sp.dma_start(x_in, x_prompt[0, 0:P, :]).then_inc(x_landed, 16)
            sp.dma_start(chan_rows[0:TAPS, :], conv_dw_w).then_inc(rows_in, 16)
            sp.dma_start(chan_rows[TAPS:TAPS + 1, :], conv_dw_b).then_inc(rows_in, 16)
            sp.dma_start(chan_rows[TAPS + 1:TAPS + 2, :], conv_ln_g).then_inc(rows_in, 16)
            sp.dma_start(chan_rows[TAPS + 2:TAPS + 3, :], conv_ln_b).then_inc(rows_in, 16)
            sp.dma_start(norm_rows[0:KD, :], norm_mix[0].rearrange("(k p) -> k p", p=P)).then_inc(rows_in, 16)
            sp.dma_start(norm_rows[KD:2 * KD, :], norm_ple[0].rearrange("(k p) -> k p", p=P)).then_inc(rows_in, 16)
            for k in range(KD):
                sp.dma_start(win_w[:, k, :], w_in[k * P:(k + 1) * P, :]).then_inc(win_in[k], 16)
            sp.dma_start(qg, over_partitions(q_gain[0], P)).then_inc(const_in, 16)
            sp.dma_start(kg, over_partitions(k_gain[0], P)).then_inc(const_in, 16)
            sp.dma_start(sinks, over_partitions(attn_sinks[0], P)).then_inc(const_in, 16)
            for b in range(NB):
                sp.dma_start(sink_rows[b * HEADS:(b + 1) * HEADS, :],
                             attn_sinks[0].rearrange("(h o) -> h o", o=1)).then_inc(const_in, 16)
            load_x(1)
            for kv in range(KV):
                sp.dma_start(wout_w[kv * HD:(kv + 1) * HD, 0:GROUP, :],
                             w_out[kv * GROUP * HD:(kv + 1) * GROUP * HD, :].rearrange("(i d) n -> d i n", d=HD)
                             ).then_inc(out_w_in, 16)
            sp.dma_start(wout_w[:, GROUP:KD, :], w_out[QW:D, :].rearrange("(k p) n -> p k n", p=P)).then_inc(out_w_in, 16)
            sp.dma_start(x_res, x_prompt[0, 0:P, :]).then_inc(res_landed, 16)
            sp.dma_start(wq_last, peer_wq[(KD - 1) * P:D, :]).then_inc(wq_in, 16)
            sp.dma_start(ranking["gain"], norm_ffn[0].partition_broadcast(P)).then_inc(ranking["rank_rows_in"], 16)
            sp.dma_start(ranking["key_rows"], sub_keys.rearrange("s k d -> k s d")).then_inc(ranking["rank_rows_in"], 16)
            for b in range(NB):
                sp.dma_start(new_k_sample[0, b, 0:P - 1], cache_k[b, 1:P]).then_inc(copied_over, 16)
                sp.dma_start(new_v_sample[0, b, 0:P - 1], cache_v[b, 1:P]).then_inc(copied_over, 16)
            sp.dma_start(new_conv_sample[0, :, 0:HIST - 1, :], state_conv[:, 1:HIST, :]).then_inc(copied_over, 16)
            def swap_residual(t):
                sp.wait_ge(x1_ready, t)
                sp.dma_start(x1[bass.ds(t - 1, 1), :, :].rearrange("o p d -> (o p) d"), x_res).then_inc(x1_stored, 16)
                sp.wait_ge(x1_stored, t * 16)
                sp.dma_start(x_res, x_prompt[0, bass.ds(t * P, P), :]).then_inc(res_landed, 16)

            load_x(2)
            with sp.Fori(1, NT - 2) as t:
                load_x(t + 2)
                swap_residual(t)
            sp.wait_ge(x1_stored, 16)
            sp.dma_start(xq, x1[0]).then_inc(ranking["xq_landed"], 16)
            sp.wait_ge(xn_ready, NT)
            sp.dma_start(x_in[0:NB, :], x_sample[:, 0, :]).then_inc(x_landed, 16)
            swap_residual(NT - 2)
            sp.wait_ge(qk_ready, NT)
            sp.dma_start(new_k_prompt[0, 0].rearrange("w h d -> w (h d)"), qk[:, QW:QW + KW]).then_inc(tail_stored, 16)
            sp.wait_ge(v_ready, NT)
            sp.dma_start(new_v_prompt[0, 0].rearrange("w h d -> w (h d)"), vwin[:, 1, :]).then_inc(tail_stored, 16)
            sp.wait_ge(glu_ready, NT)
            sp.dma_start(new_conv_prompt[0, 0], glu[P - HIST:P, :]).then_inc(tail_stored, 16)
            swap_residual(NT - 1)
            sp.wait_ge(bias_set, NT + 1)
            sp.dma_start(bias_row, bias[0:1, :, 0:SKEYS]).then_inc(bias_out, 16)
            sp.wait_ge(bias_out, 16)
            for b in range(NB):
                sp.dma_start(sbias[b * HEADS:(b + 1) * HEADS, 0:SKEYS], bias_row[0]).then_inc(sbias_in, 16)
            sp.wait_ge(att_ready, NT)
            sp.dma_start(k_rows, cache_k.rearrange("b w h d -> w b (h d)")).then_inc(samples_in, 16)
            sp.dma_start(v_rows, cache_v.rearrange("b w h d -> w b (h d)")).then_inc(samples_in, 16)
            for g in range(2):
                sp.dma_start(st_rows[0:4 * HIST, g, :],
                             state_conv[4 * g:4 * g + 4].rearrange("b j c -> (b j) c")).then_inc(samples_in, 16)
            sp.wait_ge(z_ready, NT + 1)
            for k in range(KD - 1):
                sp.dma_start(wq_main[:, k, :], peer_wq[k * P:(k + 1) * P, :]).then_inc(wq_in, 16)
            sp.wait_ge(x1_ready, NT)
            sp.dma_start(x1[NT - 1], x_res).then_inc(x1_stored, 16)
            sp.wait_ge(x1_stored, NT * 16)
            sp.dma_start(x_res[0:NB, :], x_sample[:, 0, :]).then_inc(res_landed, 16)
            sp.wait_ge(zero_ready, 1)
            sp.dma_start(x1[NT, NB:P, :], probs.rearrange("p a b -> p (a b)")[NB:P, 2 * CONV:2 * CONV + D]).then_inc(zero_stored, 16)
            sp.wait_ge(qk_ready, NT + 1)
            sp.dma_start(new_k_sample[0, :, P - 1].rearrange("b h d -> b (h d)"), qk[0:NB, QW:QW + KW]).then_inc(outs_stored, 16)
            sp.wait_ge(v_ready, NT + 1)
            sp.dma_start(new_v_sample[0, :, P - 1].rearrange("b h d -> b (h d)"), vwin[0:NB, 1, :]).then_inc(outs_stored, 16)
            sp.wait_ge(glu_ready, NT + 1)
            sp.dma_start(new_conv_sample[0, :, HIST - 1, :], glu[0:NB, :]).then_inc(outs_stored, 16)
            sp.wait_ge(x1_ready, NT + 1)
            sp.dma_start(x1[NT, 0:NB, :], x_res[0:NB, :]).then_inc(x1_stored, 16)
            sp.wait_ge(x1_stored, (NT + 1) * 16)
            sp.wait_ge(zero_stored, 16)
            sp.wait_ge(tail_stored, 3 * 16)
            sp.wait_ge(copied_over, (2 * NB + 1) * 16)
            sp.wait_ge(outs_stored, 3 * 16)

        @block.gpsimd
        def _(pool):
            steps = Chain(pool, pool_step)
            steps.link(nc.gpsimd.memset(ident[:, :], 0.0))
            nc.gpsimd.affine_select(out=ident[:, :], in_=ident[:, :], compare_op=ALU.not_equal, fill=1.0, base=0,
                                    pattern=[[-1, P]], channel_multiplier=1).then_inc(const_made, 1)
            nc.gpsimd.memset(eps[:, :], EPS).then_inc(const_made, 1)
            nc.gpsimd.memset(kwin[:, 0:P], 0.0).then_inc(window_cleared, 1)
            nc.gpsimd.memset(vwin[:, 0, :], 0.0).then_inc(window_cleared, 1)
            nc.gpsimd.memset(gluT[:, :, 0:HIST], 0.0).then_inc(window_cleared, 1)
            steps.link(nc.gpsimd.iota(probs[:, 0, :], [[-1, WIN]], base=P, channel_multiplier=1,
                                      allow_small_or_imprecise_dtypes=True))
            for h in range(HEADS):
                last = nc.gpsimd.tensor_scalar(bias[:, h, :], probs[:, 0, :], -2.0 ** (-8.0 * (h + 1) / HEADS), 0.0,
                                               ALU.mult, ALU.add)
            steps.link(last)
            steps.link(nc.gpsimd.affine_select(out=bias[:, :, :], in_=bias[:, :, :], compare_op=ALU.is_ge, fill=NEG, base=P,
                                               pattern=[[0, HEADS], [-1, WIN]], channel_multiplier=1))
            steps.link(nc.gpsimd.affine_select(out=bias[:, :, :], in_=bias[:, :, :], compare_op=ALU.is_ge, fill=NEG, base=0,
                                               pattern=[[0, HEADS], [1, WIN]], channel_multiplier=-1))
            steps.link(nc.gpsimd.tensor_copy(bias_prev[:, :, :], bias[:, :, 0:P]))
            nc.gpsimd.memset(bias[:, :, 0:P], NEG).then_inc(bias_set, 1)
            steps.link(nc.gpsimd.memset(own[0:HEADS * NB, :], 1.0))
            steps.link(nc.gpsimd.affine_select(out=own[0:HEADS * NB, :], in_=own[0:HEADS * NB, :], compare_op=ALU.is_ge,
                                               fill=0.0, base=0, pattern=[[-HEADS, NB]], channel_multiplier=1))
            steps.link(nc.gpsimd.affine_select(out=own[0:HEADS * NB, :], in_=own[0:HEADS * NB, :], compare_op=ALU.is_ge,
                                               fill=0.0, base=HEADS - 1, pattern=[[HEADS, NB]], channel_multiplier=-1))
            nc.gpsimd.memset(new_rows[:, :], 0.0).then_inc(const_made, 1)
            with pool.Fori(0, NT) as t:
                hold(pool, pool_on, m_ready, t + 1)
                nc.gpsimd.tensor_copy(bias[:, :, 0:P], bias_prev[:, :, :]).then_inc(bias_set, 1)
            pool.wait_ge(bias_set, NT + 1)
            nc.gpsimd.memset(q_blocks, 0.0).then_inc(const_made, 1)
            pool.wait_ge(pT_ready, NT)
            nc.gpsimd.memset(probs.rearrange("p a b -> p (a b)")[:, 2 * CONV:2 * CONV + D], 0.0).then_inc(zero_ready, 1)

        A_FIRST, A_STEPS = 2, 11

        @block.scalar
        def _(act):
            def x_norm(t, R, steps):
                hold(act, act_on, x_landed, (t + 1) * 16)
                steps.link(nc.scalar.activation(squares[0:R, :], x_in[0:R, :], ACT.Square, accum_out=ssq[0:R, :]))
                nc.scalar.activation(rms[0:R, :], ssq[0:R, :], ACT.Sqrt, bias=eps[0:R, :], scale=1.0 / D).then_inc(squared, 1)

            def evacuate(t, R):
                act.wait_ge(z_ready, t + 1)
                nc.scalar.activation(squares[0:R, 0:QW + KW], ZB[0:R, 0:QW + KW], ACT.Square).then_inc(qk_squared, 1)
                if R == NB:
                    act.wait_ge(tail_stored, 48)
                nc.scalar.activation(vwin[0:R, 1, :], ZB[0:R, ZV:ZV + KW], ACT.Copy).then_inc(v_ready, 1)
                act.wait_ge(qk_summed, t + 1)
                nc.scalar.activation(rms10[0:R, :], ss10[0:R, :], ACT.Sqrt, bias=eps[0:R, :], scale=1.0 / HD).then_inc(qk_rms, 1)

            def gate_sigmoid(t, R):
                nc.scalar.activation(gate[0:R, :], ZB[0:R, ZG:ZG + CONV], ACT.Sigmoid).then_inc(sig_ready, 1)

            def conv_rms(t, R):
                act.wait_ge(cvar_ready, t + 1)
                nc.scalar.activation(rms_c[0:R, :], mv[0:R, 1:2], ACT.Sqrt, bias=eps[0:R, :]).then_inc(crms_ready, 1)

            def conv_affine(t, R):
                act.wait_ge(lnT_ready, t + 1)
                for c in range(CT):
                    scale, shift = chan[:, c, TAPS + 1:TAPS + 2], chan[:, c, TAPS + 2:TAPS + 3]
                    src = TB[:, 2 * BANK + c * P:2 * BANK + c * P + R]
                    nc.scalar.activation(conv_y[:, c, 0:R], src, ACT.Identity, bias=shift, scale=scale)
                    last = nc.scalar.activation(conv_s[:, c, 0:R], src, ACT.Sigmoid, bias=shift, scale=scale)
                last.then_inc(cy_ready, 1)

            act.wait_ge(cols_T, 1)
            nc.scalar.activation(chan[:, :, :], TB[:, 0:CT * P].rearrange("p (c j) -> p c j", c=CT)[:, :, 0:TAPS + 3], ACT.Copy).then_inc(cols_made, 1)
            nc.scalar.activation(norm_cols[:, :, :], TB[:, BANK:BANK + 2 * KD].rearrange("p (a k) -> p a k", a=2), ACT.Copy).then_inc(cols_made, 1)

            def heads_copy(t):
                act.wait_ge(qkT_ready, t + 1)
                nc.scalar.activation(qT[:, :, :], TB[:, 0:QW].rearrange("p (i t) -> p i t", t=P), ACT.Copy)
                nc.scalar.activation(kwin[:, P:WIN], TB[:, QW:QW + P], ACT.Copy).then_inc(qk_copied, 1)

            def prompt_tile(t, next_rows, norm_rows):
                steps = Chain(act, act_step, t * A_STEPS + A_FIRST)
                act.wait_ge(m_ready, t + 1)
                for h in range(HEADS):
                    steps.link(nc.scalar.activation(probs[:, h, :], probs[:, h, :], ACT.Exp, bias=ntop[:, h:h + 1],
                                                    accum_out=den[:, h:h + 1]))
                nc.scalar.activation(esink[:, :], dsink[:, :], ACT.Exp).then_inc(e_ready, 1)
                if norm_rows:
                    x_norm(t + 2, norm_rows, steps)
                act.wait_ge(pT_ready, t + 1)
                nc.scalar.activation(probsT[:, :, :], TB[:, :].rearrange("p (a b) -> p a b", b=P), ACT.Copy).then_inc(pT_copied, 1)
                act.wait_ge(att_ready, t + 1)
                nc.scalar.activation(mixedT[:, 0:GROUP, :], TB[:, 0:QW].rearrange("p (i t) -> p i t", t=P), ACT.Copy).then_inc(att_copied, 1)
                steps.link(nc.scalar.activation(kwin[:, 0:P], kwin[:, P:WIN], ACT.Copy))
                steps.link(nc.scalar.activation(vwin[:, 0, :], vwin[:, 1, :], ACT.Copy))
                evacuate(t + 1, next_rows)
                conv_rms(t, P)
                gate_sigmoid(t + 1, next_rows)
                conv_affine(t, P)
                if norm_rows:
                    heads_copy(t + 1)
                assert steps.n == (A_STEPS if norm_rows else A_STEPS - 1), steps.n

            steps = Chain(act, act_step)
            act.wait_ge(const_made, 2)
            x_norm(0, P, steps)
            act.wait_ge(window_cleared, 3)
            evacuate(0, P)
            gate_sigmoid(0, P)
            heads_copy(0)
            x_norm(1, P, steps)
            assert steps.n == A_FIRST, steps.n
            with act.Fori(0, NT - 2) as t:
                prompt_tile(t, P, P)
            prompt_tile(NT - 2, P, NB)
            prompt_tile(NT - 1, NB, 0)

            t, R, rows = NT, NB, HEADS * NB
            steps = Chain(act, act_step, t * A_STEPS + A_FIRST - 1)
            act.wait_ge(gluT_ready, t + 1)
            nc.scalar.activation(hist[:, :, :, HIST], ZB[:, 0:CT * P].rearrange("p (c k) -> p c k", c=CT)[:, :, 0:NB],
                                 ACT.Copy).then_inc(new_glu_taken, 1)
            act.wait_ge(qkT_ready, t + 1)
            act.wait_ge(const_made, 4)
            for kv in range(KV):
                half = slice(kv * HD, (kv + 1) * HD)
                nc.scalar.activation(q_blocks[half, :].rearrange("p (b s) -> p b s", s=72)[:, :, kv * GROUP:(kv + 1) * GROUP],
                                     s_qT[half, :, 0:NB].rearrange("p i b -> p b i"), ACT.Copy)
            act.wait_ge(sbias_in, NB * 16)
            nc.scalar.activation(keysT[:, :, P], TB[:, QW:QW + NB], ACT.Copy).then_inc(kT_new, 1)
            act.wait_ge(kT_ready, 1)
            nc.scalar.activation(keysT[:, :, 0:P], ZB[:, 0:NB * P].rearrange("p (b k) -> p b k", k=P), ACT.Copy).then_inc(kT_copied, 1)
            act.wait_ge(stT_ready, 1)
            for g in range(2):
                last = nc.scalar.activation(hist[:, :, 4 * g:4 * g + 4, 0:HIST],
                                            TB[:, 2 * BANK + g * CT * P:2 * BANK + (g + 1) * CT * P].rearrange("p (c k) -> p c k", c=CT)
                                            [:, :, 0:4 * HIST].rearrange("p c (b j) -> p c b j", j=HIST), ACT.Copy)
            last.then_inc(hist_ready, 1)
            act.wait_ge(m_ready, t + 1)
            steps.link(nc.scalar.activation(s_probs, s_probs, ACT.Exp, bias=ntop[0:rows, 0:1], accum_out=den[0:rows, 0:1]))
            nc.scalar.activation(esink[0:rows, 0:1], dsink[0:rows, 0:1], ACT.Exp).then_inc(e_ready, 1)
            act.wait_ge(pT_ready, t + 1)
            nc.scalar.activation(s_probsT, TB[:, BANK:BANK + rows], ACT.Copy)
            nc.scalar.activation(new_T[0:NB, 0:rows], TB[0:NB, 2 * BANK:2 * BANK + rows], ACT.Copy).then_inc(pT_copied, 1)
            act.wait_ge(att_ready, t + 1)
            for kv in range(KV):
                half = slice(kv * HD, (kv + 1) * HD)
                last = nc.scalar.activation(mixedT[half, 0:GROUP, 0:NB],
                                            TB[half, 3 * BANK:3 * BANK + rows].rearrange("p (b h) -> p h b", h=HEADS)
                                            [:, kv * GROUP:(kv + 1) * GROUP, :], ACT.Copy)
            last.then_inc(att_copied, 1)
            conv_rms(t, R)
            conv_affine(t, R)

            act.wait_ge(ranking["xq_landed"], 16)
            Chain(act, ranking["act_rank_step"]).link(nc.scalar.activation(
                ranking["q_cand"].rearrange("p a b -> p (a b)")[:, 0:D], xq, ACT.Square, accum_out=small[:, 0:1]))
            nc.scalar.activation(small[:, 1:2], small[:, 0:1], ACT.Sqrt, bias=eps[:, :], scale=1.0 / D).then_inc(ranking["xq_rms"], 1)
            act.wait_ge(ranking["hnT_ready"], 1)
            nc.scalar.activation(ranking["hT"], TB[:, 0:D].rearrange("p (k t) -> p k t", t=P), ACT.Copy).then_inc(ranking["hT_copied"], 1)
            act.wait_ge(ranking["keysT_ready"], 1)
            nc.scalar.activation(ranking["keysT"], TB[:, 3 * BANK:3 * BANK + 2 * P].rearrange("p (s k) -> p s k", s=2),
                                 ACT.Copy).then_inc(ranking["keysT_copied"], 1)

        FIRST_TAPS, EARLY_TAPS = 7, 7
        D_FIRST, D_STEPS = 4 + FIRST_TAPS, 42
        TT = nc.vector.tensor_tensor

        @block.vector
        def _(dve):
            def x_norm(t, R, steps):
                dve.wait_ge(squared, t + 1)
                steps.link(nc.vector.reciprocal(rstd[0:R, :], rms[0:R, :]))
                nc.vector.tensor_scalar(xn[0:R, :], x_in[0:R, :], rstd[0:R, :], None, ALU.mult).then_inc(xn_ready, 1)

            def x_gain(t, R):
                dve.wait_ge(xT_ready, t + 1)
                TT(hT[:, :, 0:R], ZB[:, 0:D].rearrange("p (k t) -> p k t", k=KD)[:, :, 0:R],
                   norm_cols[:, 0, :].unsqueeze(2).to_broadcast([P, KD, R]), ALU.mult).then_inc(hT_ready, 1)

            def qk_sums(t, R):
                dve.wait_ge(qk_squared, t + 1)
                nc.vector.tensor_reduce(ss10[0:R, :], squares[0:R, 0:QW + KW].rearrange("p (h d) -> p h d", d=HD), AX.X,
                                        ALU.add).then_inc(qk_summed, 1)

            def heads_and_glu(t, R, steps):
                dve.wait_ge(qk_rms, t + 1)
                steps.link(nc.vector.reciprocal(rstd10[0:R, :], rms10[0:R, :]))
                if R == NB:
                    dve.wait_ge(tail_stored, 48)
                q_out = qk[0:R, 0:QW].rearrange("p (i kv d) -> p kv i d", kv=KV, i=GROUP)
                k_out = qk[0:R, QW:].rearrange("p (h d) -> p h d", d=HD)
                q_by_head = qk[0:R, 0:QW].rearrange("p (h d) -> p h d", d=HD)
                TT(q_out, ZB[0:R, 0:QW].rearrange("p (kv i d) -> p kv i d", kv=KV, i=GROUP),
                   rstd10[0:R, 0:HEADS].rearrange("p (kv i) -> p kv i", kv=KV).unsqueeze(3).to_broadcast([R, KV, GROUP, HD]),
                   ALU.mult)
                steps.link(TT(k_out, ZB[0:R, ZK:ZV].rearrange("p (h d) -> p h d", d=HD),
                              rstd10[0:R, HEADS:].unsqueeze(2).to_broadcast([R, KV, HD]), ALU.mult))
                TT(q_by_head, q_by_head, qg[0:R, :].unsqueeze(1).to_broadcast([R, HEADS, HD]), ALU.mult)
                TT(k_out, k_out, kg[0:R, :].unsqueeze(1).to_broadcast([R, KV, HD]), ALU.mult).then_inc(qk_ready, 1)
                dve.wait_ge(sig_ready, t + 1)
                TT(glu[0:R, :], ZB[0:R, ZA:ZA + CONV], gate[0:R, :], ALU.mult).then_inc(glu_ready, 1)

            def gluT_copy(t):
                dve.wait_ge(gluT_ready, t + 1)
                nc.vector.tensor_copy(gluT[:, :, HIST:HIST + P], ZB[:, 0:CT * P].rearrange("p (c t) -> p c t", c=CT)
                                      ).then_inc(gluT_copied, 1)

            def conv_norm(t, R, steps):
                dve.wait_ge(c_ready, t + 1)
                steps.link(nc.vector.bn_stats(bn6[0:R, :], TB[0:R, BANK:2 * BANK]))
                hold(dve, dve_on, dve_step, steps.base + steps.n)
                nc.vector.bn_aggr(mv[0:R, :], bn6[0:R, :]).then_inc(cvar_ready, 1)
                dve.wait_ge(crms_ready, t + 1)
                steps.link(nc.vector.reciprocal(rstd_c[0:R, :], rms_c[0:R, :]))
                nc.vector.tensor_scalar(xn[0:R, 0:CONV], TB[0:R, BANK:2 * BANK], mv[0:R, 0:1], rstd_c[0:R, :], ALU.subtract,
                                        ALU.mult).then_inc(ln_ready, 1)

            def silu(t, R):
                dve.wait_ge(cy_ready, t + 1)
                TT(mixedT[:, GROUP:KD, 0:R], conv_y[:, :, 0:R], conv_s[:, :, 0:R], ALU.mult).then_inc(mix_ready, 1)

            def residual(t, R, bank=2):
                dve.wait_ge(o_ready, t + 1)
                dve.wait_ge(res_landed, (t + 1) * 16)
                TT(x_res[0:R, :], ZB[0:R, bank * BANK:(bank + 2) * BANK], x_res[0:R, :], ALU.add).then_inc(x1_ready, 1)

            def conv_tap(j):
                for c in range(CT):
                    src, w = gluT[:, c, j:j + P], chan[:, c, j:j + 1]
                    if j == 0:
                        last = nc.vector.tensor_scalar(acc[:, c, :], src, w, chan[:, c, TAPS:TAPS + 1], ALU.mult, ALU.add)
                    else:
                        last = nc.vector.scalar_tensor_tensor(out=acc[:, c, :], in0=src, scalar=w, in1=acc[:, c, :],
                                                              op0=ALU.mult, op1=ALU.add)
                return last

            def first_taps(t, steps):
                dve.wait_ge(gluT_copied, t + 1)
                for j in range(FIRST_TAPS):
                    steps.link(conv_tap(j))

            def prompt_tile(t, next_rows, norm_rows, first=False):
                steps = Chain(dve, dve_step, t * D_STEPS + D_FIRST)
                dve.wait_ge(s_ready, t + 1)
                dve.wait_ge(bias_set, t + 1)
                flat = probs.rearrange("p h k -> p (h k)")
                steps.link(nc.vector.scalar_tensor_tensor(out=flat, in0=TB[:, :], scalar=HD ** -0.5,
                                                          in1=bias.rearrange("p h k -> p (h k)"), op0=ALU.mult, op1=ALU.add))
                steps.link(nc.vector.tensor_reduce(top[:, :], probs[:, :, :], AX.X, ALU.max))
                steps.link(TT(top[:, :], top[:, :], sinks[:, :], ALU.max))
                steps.link(TT(dsink[:, :], sinks[:, :], top[:, :], ALU.subtract))
                nc.vector.tensor_scalar(ntop[:, :], top[:, :], -1.0, None, ALU.mult).then_inc(m_ready, 1)
                x_gain(t + 1, next_rows)
                if not first:
                    residual(t - 1, P)
                for j in range(FIRST_TAPS, FIRST_TAPS + EARLY_TAPS):
                    steps.link(conv_tap(j))
                dve.wait_ge(e_ready, t + 1)
                steps.link(TT(den[:, :], den[:, :], esink[:, :], ALU.add))
                steps.link(nc.vector.reciprocal(rden[:, :], den[:, :]))
                TT(probs[:, :, :], probs[:, :, :], rden[:, :].unsqueeze(2).to_broadcast([P, HEADS, WIN]), ALU.mult).then_inc(p_ready, 1)
                for j in range(FIRST_TAPS + EARLY_TAPS, TAPS - 1):
                    steps.link(conv_tap(j))
                conv_tap(TAPS - 1).then_inc(conv_done, 1)
                steps.link(nc.vector.tensor_copy(gluT[:, :, 0:HIST], gluT[:, :, P:P + HIST]))
                qk_sums(t + 1, next_rows)
                conv_norm(t, P, steps)
                heads_and_glu(t + 1, next_rows, steps)
                silu(t, P)
                if norm_rows:
                    gluT_copy(t + 1)
                    x_norm(t + 2, norm_rows, steps)
                    first_taps(t + 1, steps)
                assert steps.n == (D_STEPS if norm_rows else D_STEPS - 1 - FIRST_TAPS), steps.n

            steps = Chain(dve, dve_step)
            dve.wait_ge(cols_made, 2)
            x_norm(0, P, steps)
            x_gain(0, P)
            dve.wait_ge(const_in, (3 + NB) * 16)
            dve.wait_ge(window_cleared, 3)
            qk_sums(0, P)
            heads_and_glu(0, P, steps)
            gluT_copy(0)
            x_norm(1, P, steps)
            first_taps(0, steps)
            dve.wait_ge(const_made, 3)
            assert steps.n == D_FIRST, steps.n
            prompt_tile(0, P, P, first=True)
            with dve.Fori(1, NT - 2) as t:
                prompt_tile(t, P, P)
            prompt_tile(NT - 2, P, NB)
            prompt_tile(NT - 1, NB, 0)

            t, R, rows = NT, NB, HEADS * NB
            steps = Chain(dve, dve_step, t * D_STEPS + D_FIRST - 1 - FIRST_TAPS)
            dve.wait_ge(s_ready, t + 1)
            dve.wait_ge(sbias_in, NB * 16)
            s0 = sink_rows[0:rows, :]
            steps.link(nc.vector.scalar_tensor_tensor(out=s_probs, in0=TB[0:rows, 0:SKEYS], scalar=HD ** -0.5,
                                                      in1=sbias[0:rows, 0:SKEYS], op0=ALU.mult, op1=ALU.add))
            steps.link(nc.vector.tensor_reduce(top[0:rows, 0:1], s_probs, AX.X, ALU.max))
            steps.link(TT(top[0:rows, 0:1], top[0:rows, 0:1], s0, ALU.max))
            steps.link(TT(dsink[0:rows, 0:1], s0, top[0:rows, 0:1], ALU.subtract))
            nc.vector.tensor_scalar(ntop[0:rows, 0:1], top[0:rows, 0:1], -1.0, None, ALU.mult).then_inc(m_ready, 1)
            dve.wait_ge(hist_ready, 1)
            steps.link(TT(prod, hist, chan[:, :, 0:TAPS].unsqueeze(2).to_broadcast([P, CT, NB, TAPS]), ALU.mult))
            steps.link(nc.vector.tensor_reduce(acc[:, :, 0:NB], prod, AX.X, ALU.add))
            TT(acc[:, :, 0:NB], acc[:, :, 0:NB], chan[:, :, TAPS:TAPS + 1].to_broadcast([P, CT, NB]), ALU.add).then_inc(conv_done, 1)
            dve.wait_ge(e_ready, t + 1)
            steps.link(TT(den[0:rows, 0:1], den[0:rows, 0:1], esink[0:rows, 0:1], ALU.add))
            steps.link(nc.vector.reciprocal(rden[0:rows, 0:1], den[0:rows, 0:1]))
            steps.link(nc.vector.tensor_scalar(s_probs, s_probs, rden[0:rows, 0:1], None, ALU.mult))
            nc.vector.tensor_scalar(new_rows[0:rows, 0:NB], own[0:rows, :], s_probs[:, P:P + 1], None, ALU.mult).then_inc(p_ready, 1)
            conv_norm(t, R, steps)
            residual(t - 1, P)
            silu(t, R)
            dve.wait_ge(ranking["xq_rms"], 1)
            dve.wait_ge(ranking["rank_rows_in"], 2 * 16)
            Chain(dve, ranking["dve_rank_step"]).link(nc.vector.reciprocal(small[:, 2:3], small[:, 1:2]))
            nc.vector.scalar_tensor_tensor(out=xq, in0=xq, scalar=small[:, 2:3], in1=ranking["gain"], op0=ALU.mult,
                                           op1=ALU.mult).then_inc(ranking["hn_ready"], 1)
            residual(t, R, bank=0)

        @block.tensor
        def _(pe):
            def transpose(out, src, rows):
                return nc.tensor.transpose(out, src, ident[0:rows, 0:rows])

            def x_transposes(t, R, beside=None):
                if beside is not None:
                    pe.wait_ge(gluT_copied, beside + 1)
                pe.wait_ge(xn_ready, t + 1)
                for k in range(KD):
                    last = transpose(ZB[:, k * P:k * P + R], xn[0:R, k * P:(k + 1) * P], R)
                last.then_inc(xT_ready, 1)

            def product(R, c, k):
                cols = slice(c * BANK, min((c + 1) * BANK, DIN))
                return nc.tensor.matmul(ZB[0:R, cols], hT[:, k, 0:R], win_w[:, k, cols], start=(k == 0), stop=(k == KD - 1))

            def project(R, banks):
                for c in banks:
                    for k in range(KD):
                        last = product(R, c, k)
                return last

            def heads_and_glu(t, R):
                pe.wait_ge(qk_ready, t + 1)
                for i in range(GROUP):
                    transpose(TB[:, i * P:i * P + R], qk[0:R, i * P:(i + 1) * P], R)
                transpose(TB[:, QW:QW + R], qk[0:R, QW:QW + KW], R).then_inc(qkT_ready, 1)
                pe.wait_ge(glu_ready, t + 1)
                for c in range(CT):
                    last = transpose(ZB[:, c * P:c * P + R], glu[0:R, c * P:(c + 1) * P], R)
                last.then_inc(gluT_ready, 1)

            def scores(t):
                pe.wait_ge(qk_copied, t + 1)
                for h in range(HEADS):
                    kv, i = divmod(h, GROUP)
                    half = slice(kv * HD, (kv + 1) * HD)
                    last = nc.tensor.matmul(TB[:, h * WIN:(h + 1) * WIN], qT[half, i, :], kwin[half, :], start=True, stop=True)
                last.then_inc(s_ready, 1)

            def conv_norm(t, R):
                pe.wait_ge(conv_done, t + 1)
                pe.wait_ge(pT_copied, t + 1)
                for c in range(CT):
                    last = transpose(TB[0:R, BANK + c * P:BANK + (c + 1) * P], acc[:, c, 0:R], P)
                last.then_inc(c_ready, 1)
                pe.wait_ge(ln_ready, t + 1)
                for c in range(CT):
                    last = transpose(TB[:, 2 * BANK + c * P:2 * BANK + c * P + R], xn[0:R, c * P:(c + 1) * P], R)
                last.then_inc(lnT_ready, 1)

            def mixed_out(t, R, part, banks=(0, 1), first_bank=2):
                for c in banks:
                    for k in range(part * GROUP, (part + 1) * GROUP):
                        last = nc.tensor.matmul(ZB[0:R, (first_bank + c) * BANK:(first_bank + c + 1) * BANK], mixedT[:, k, 0:R],
                                                wout_w[:, k, c * BANK:(c + 1) * BANK], start=(k == 0), stop=(k == KD - 1))
                return last

            pe.wait_ge(const_made, 1)
            pe.wait_ge(rows_in, 6 * 16)
            for c in range(CT):
                transpose(TB[:, c * P:c * P + TAPS + 3], chan_rows[0:TAPS + 3, c * P:(c + 1) * P], TAPS + 3)
            transpose(TB[:, BANK:BANK + 2 * KD], norm_rows[0:2 * KD, :], 2 * KD).then_inc(cols_T, 1)
            pe.wait_ge(cols_made, 2)

            def prompt_tile(t, next_rows, norm_rows, first=False):
                pe.wait_ge(hT_ready, t + 2)
                project(next_rows, (0, 1))
                pe.wait_ge(p_ready, t + 1)
                for h in range(HEADS):
                    for blk in range(2):
                        s = 2 * h + blk
                        last = transpose(TB[:, s * P:(s + 1) * P], probs[:, h, blk * P:(blk + 1) * P], P)
                last.then_inc(pT_ready, 1)
                if not first:
                    pe.wait_ge(x1_ready, t)
                project(next_rows, (2,))
                pe.wait_ge(pT_copied, t + 1)
                for h in range(HEADS):
                    kv, i = divmod(h, GROUP)
                    half = slice(kv * HD, (kv + 1) * HD)
                    for blk in range(2):
                        last = nc.tensor.matmul(TB[half, i * P:(i + 1) * P], vwin[:, blk, half], probsT[:, 2 * h + blk, :],
                                                start=(blk == 0), stop=(blk == 1))
                last.then_inc(att_ready, 1)
                project(next_rows, (3,)).then_inc(z_ready, 1)
                conv_norm(t, P)
                pe.wait_ge(att_copied, t + 1)
                heads_and_glu(t + 1, next_rows)
                if first:
                    pe.wait_ge(out_w_in, 3 * 16)
                if not norm_rows:
                    return
                mixed_out(t, P, 0, banks=(0,))
                pe.wait_ge(cy_ready, t + 1)
                scores(t + 1)
                mixed_out(t, P, 0, banks=(1,))
                x_transposes(t + 2, norm_rows, beside=t + 1)
                pe.wait_ge(mix_ready, t + 1)
                mixed_out(t, P, 1).then_inc(o_ready, 1)

            x_transposes(0, P)
            pe.wait_ge(hT_ready, 1)
            for k in range(KD):
                pe.wait_ge(win_in[k], 16)
                for c in range(4):
                    last = product(P, c, k)
            last.then_inc(z_ready, 1)
            heads_and_glu(0, P)
            scores(0)
            x_transposes(1, P, beside=0)
            prompt_tile(0, P, P, first=True)
            with pe.Fori(1, NT - 2) as t:
                prompt_tile(t, P, P)
            prompt_tile(NT - 2, P, NB)
            prompt_tile(NT - 1, NB, 0)

            t, rows = NT, HEADS * NB
            pe.wait_ge(samples_in, 4 * 16)
            pe.wait_ge(new_glu_taken, 1)
            for b in range(NB):
                last = transpose(ZB[:, b * P:(b + 1) * P], k_rows[:, b, :], P)
            last.then_inc(kT_ready, 1)
            pe.wait_ge(cy_ready, t)
            for g in range(2):
                for c in range(CT):
                    at = 2 * BANK + (g * CT + c) * P
                    last = transpose(TB[:, at:at + 4 * HIST], st_rows[0:4 * HIST, g, c * P:(c + 1) * P], 4 * HIST)
            last.then_inc(stT_ready, 1)
            mixed_out(t - 1, P, 0)
            pe.wait_ge(kT_copied, 1)
            pe.wait_ge(hist_ready, 1)
            for b in range(NB):
                last = nc.tensor.matmul(TB[0:rows, 0:SKEYS], q_blocks[:, b * rows:(b + 1) * rows], keysT[:, b, :],
                                        start=(b == 0), stop=(b == NB - 1))
            last.then_inc(s_ready, 1)
            pe.wait_ge(mix_ready, t)
            mixed_out(t - 1, P, 1).then_inc(o_ready, 1)
            pe.wait_ge(p_ready, t + 1)
            transpose(TB[:, BANK:BANK + rows], s_probs[:, 0:P], rows)
            transpose(TB[:, 2 * BANK:2 * BANK + rows], new_rows[0:rows, :], rows).then_inc(pT_ready, 1)
            pe.wait_ge(pT_copied, t + 1)
            out = TB[:, 3 * BANK:3 * BANK + rows]
            nc.tensor.matmul(out, vwin[0:NB, 1, :], new_T[0:NB, 0:rows], start=True, stop=False)
            for b in range(NB):
                cols = slice(b * HEADS, (b + 1) * HEADS)
                last = nc.tensor.matmul(out[:, cols], v_rows[:, b, :], s_probsT[:, cols], start=False, stop=(b == NB - 1))
            last.then_inc(att_ready, 1)
            pe.wait_ge(att_copied, t + 1)
            pe.wait_ge(ranking["rank_rows_in"], 2 * 16)
            for s in range(2):
                last = transpose(TB[:, 3 * BANK + s * P:3 * BANK + (s + 1) * P], ranking["key_rows"][:, s, :], P)
            last.then_inc(ranking["keysT_ready"], 1)
            conv_norm(t, NB)
            mixed_out(t, NB, 0, first_bank=0)
            pe.wait_ge(mix_ready, t + 1)
            mixed_out(t, NB, 1, first_bank=0).then_inc(o_ready, 1)
            pe.wait_ge(ranking["hn_ready"], 1)
            for k in range(KD):
                last = transpose(TB[:, k * P:(k + 1) * P], xq[:, k * P:(k + 1) * P], P)
            last.then_inc(ranking["hnT_ready"], 1)


def experts(nc, ident, eps, norm_cols, arena, main_end, ahead_end, x1, p_prompt, p_sample, peer_u, peer_v,
            w_ple_proj, w_ple_gate, ranking, y_prompt, y_sample):
    wq_main, wq_last, wq_in = ranking["wq_main"], ranking["wq_last"], ranking["wq_in"]
    xq, gain, keysT, hT, q_cand, scores, current, small = (ranking[n] for n in (
        "xq", "gain", "keysT", "hT", "q_cand", "scores", "current", "small"))
    xq_landed, xq_rms, hn_ready, hnT_ready, hT_copied, act_q, dve_q = (ranking[n] for n in (
        "xq_landed", "xq_rms", "hn_ready", "hnT_ready", "hT_copied", "act_rank_step", "dve_rank_step"))
    with ExitStack() as ctx:
        def sem(name):
            return ctx.enter_context(nc.semaphore(name))

        QB = ctx.enter_context(nc.psum_tensor("QB", [P, 4 * BANK], F32))
        TP = ctx.enter_context(nc.psum_tensor("TP", [P, 2 * BANK], F32))
        VA = ctx.enter_context(nc.psum_tensor("VA", [P, 2 * BANK], F32))

        take = carve(arena, ahead_end)
        iota16 = take(TOPK)
        eye8 = take(NB, NB)
        w_cols = take(NB, NB)
        idxT = take(NB).bitcast(U32)
        gatesT = take(NB)
        dots8, gelu8, w8 = take(NB), take(NB), take(NB)
        dots16 = take(2 * RING)
        dots = take(CHOICES)
        sums = take(PH)
        idx = take(2, RING).bitcast(U32)
        assert take.at[0] <= ARENA, take.at[0]
        take = carve(arena, main_end)
        w_ple = take(DPLE // P, D)
        w_gate = take(KD, D)
        rows = take(RING, D)
        diag = take(DIAGS, P)
        h = take(D)
        xf = take(D)
        h3 = take(D)
        ple = take(D)
        match = take(CHOICES, TOPK)
        p_rows = take(DPLE)
        pT = take(2, P)
        top = take(2 * PH, TOPK)
        top_i = take(2 * PH, TOPK).bitcast(U32)
        top_f = take(2 * PH, TOPK)
        best = take(PH, TOPK)
        best_i = take(PH, TOPK).bitcast(U32)
        part_i = take(CHOICES).bitcast(U32)
        part = take(CHOICES)
        first_key = take(CHOICES)
        second_key = take(CHOICES)
        chosen = take(CHOICES).bitcast(U32)
        gelu = take(CHOICES)
        weights = take(CHOICES)
        gates = take(CHOICES)
        assert take.at[0] <= AHEAD, take.at[0]
        wq = [wq_main[:, k, :] for k in range(KD - 1)] + [wq_last]
        h_bc = wq_main.rearrange("p k n -> p (k n)")[:, 0:NB * D].rearrange("p (n d) -> p n d", d=D)
        cand = q_cand.rearrange("p a b -> p (a b)").rearrange("p (h c) -> p h c", c=TOPK * TOPK)
        q_flat = q_cand.rearrange("p a b -> p (a b)")
        best_flat = best.rearrange("p h k -> p (h k)")
        sc_flat = scores.rearrange("p a b -> p (a b)")
        ssq, rms, rstd, ssq2, rms2, rstd2 = (small[:, i:i + 1] for i in range(6))

        choice_dram = nc.dram_tensor("sample_choices", (NB, CHOICES), U32, kind="Internal").ap()
        gates_dram = nc.dram_tensor("sample_gates", (NB, CHOICES), F32, kind="Internal").ap()
        h_dram = nc.dram_tensor("sample_h", (NB, D), F32, kind="Internal").ap()

        const_made, w_fin_in = sem("b_const_made"), sem("w_finish_in")
        q_ready, q_copied, sc_ready, sc_copied = sem("q_ready"), sem("q_copied"), sem("key_scores_ready"), sem("key_scores_copied")
        chosen_ready, chosen_taken, gate_shifted, gexp_ready = sem("chosen_ready"), sem("chosen_taken"), sem("gate_shifted"), sem("gate_exp_ready")
        h_copied, idx_copied = sem("h_copied"), sem("idx_copied")
        landed = [sem(f"rows_landed{i}") for i in range(RING)]
        u_used, vp_used, vd_used, dots_copied = (sem(n) for n in ("u_rows_used", "v_rows_used_pe", "v_rows_used_dve", "dots_copied"))
        gelu_ready, weights_ready, diag_ready = sem("gelu_ready"), sem("weights_ready"), sem("diag_ready")
        xf_landed, p_landed, x2_ready, x2_rms, h3_ready = sem("xf_landed"), sem("p_landed"), sem("x2_ready"), sem("x2_rms"), sem("h3_ready")
        h3T_ready, h3T_copied, pT_ready, pT_copied = sem("h3T_ready"), sem("h3T_copied"), sem("pT_ready"), sem("pT_copied")
        fin_ready, fin_copied, y_ready, y_stored = sem("finish_products_ready"), sem("finish_copied"), sem("y_ready"), sem("y_stored")
        s_stored, hbc_landed, idxT_landed, gT_landed = (sem(n) for n in ("sample_scratch_stored", "sample_h_landed", "sample_idx_landed", "sample_gates_landed"))
        g8_ready, cols_ready = sem("sample_gates_ready"), sem("weight_cols_ready")
        act_f, dve_f, dve_k, dve_w, dve_on, act_on, pool_on = (sem(n) for n in (
            "act_finish_step", "dve_finish_step", "dve_choose_step", "dve_weigh_step",
            "b_dve_on", "b_act_on", "b_pool_on"))
        pool_step = sem("b_pool_step")
        part_q_ready, part_q_copied, part_sc_ready, part_sc_copied, part_chosen, part_taken = (sem(n) for n in (
            "part_q_ready", "part_q_copied", "part_scores_ready", "part_scores_copied", "part_chosen", "part_chosen_taken"))

        def hold(eng, carrier, s, value):
            eng.wait_ge(s, value)
            eng.sem_inc(carrier, 1)

        def mixed_slot(turn, i, vp, vd):
            if i < PE_SLOTS:
                return vp_used, vp + PE_FIRST + turn * PE_SLOTS + i + 1
            return vd_used, vd + turn * DVE_SLOTS + i - PE_SLOTS + 1

        block = ctx.enter_context(nc.Block())

        @block.sync
        def _(sp):
            def load_rank(q):
                sp.wait_ge(h_copied, q)
                sp.dma_start(xq, x1[bass.ds(q, 1), :, :].rearrange("o p d -> (o p) d")).then_inc(xq_landed, 16)

            def load_finish(f, first=False):
                if not first:
                    sp.wait_ge(y_stored, f * 16)
                    sp.wait_ge(pT_ready, f)
                sp.dma_start(xf, x1[bass.ds(f, 1), :, :].rearrange("o p d -> (o p) d")).then_inc(xf_landed, 16)
                sp.dma_start(p_rows, p_prompt[0, bass.ds(f * P, P), :]).then_inc(p_landed, 16)

            def store(f):
                sp.wait_ge(y_ready, f + 1)
                sp.dma_start(y_prompt[0, bass.ds(f * P, P), :], xf).then_inc(y_stored, 16)

            sp.dma_start(w_ple, w_ple_proj.rearrange("(k p) n -> p k n", p=P)).then_inc(w_fin_in, 16)
            load_rank(1)
            load_finish(0, first=True)
            sp.dma_start(w_gate, w_ple_gate.rearrange("(k p) n -> p k n", p=P)).then_inc(w_fin_in, 16)
            with sp.Fori(1, NT) as t:
                load_rank(t + 1)
                store(t - 1)
                load_finish(t)
            sp.wait_ge(hn_ready, NT + 1)
            sp.dma_start(h_dram, xq[0:NB, :]).then_inc(s_stored, 16)
            sp.wait_ge(q_ready, NT)
            sp.wait_ge(s_stored, 16)
            for n in range(NB):
                sp.dma_start(h_bc[:, n, :], h_dram[n].partition_broadcast(P)).then_inc(hbc_landed, 16)
            sp.wait_ge(chosen_ready, NT + 1)
            sp.dma_start(choice_dram, chosen[0:NB, :]).then_inc(s_stored, 16)
            sp.wait_ge(s_stored, 2 * 16)
            sp.dma_start(idxT, choice_dram.rearrange("n c -> c n"), allow_slow_non_contiguous=True).then_inc(idxT_landed, 16)
            sp.wait_ge(g8_ready, 1)
            sp.dma_start(gates_dram, gates[0:NB, :]).then_inc(s_stored, 16)
            sp.wait_ge(s_stored, 3 * 16)
            sp.dma_start(gatesT, gates_dram.rearrange("n c -> c n"), allow_slow_non_contiguous=True).then_inc(gT_landed, 16)
            store(NT - 1)
            sp.wait_ge(y_stored, NT * 16)
            sp.wait_ge(pT_ready, NT)
            sp.dma_start(xf[0:NB, :], x1[NT, 0:NB, :]).then_inc(xf_landed, 16)
            sp.dma_start(p_rows[0:NB, :], p_sample[:, 0, :]).then_inc(p_landed, 16)
            sp.wait_ge(y_ready, NT + 1)
            sp.dma_start(y_sample[:, 0, :], xf[0:NB, :]).then_inc(y_stored, 16)
            sp.wait_ge(y_stored, (NT + 1) * 16)

        @block.gpsimd
        def _(pool):
            nc.gpsimd.iota(iota16, [[1, TOPK]], base=0, channel_multiplier=0,
                           allow_small_or_imprecise_dtypes=True).then_inc(const_made, 1)
            steps = Chain(pool, pool_step)
            steps.link(nc.gpsimd.memset(eye8, 0.0))
            nc.gpsimd.affine_select(out=eye8, in_=eye8, compare_op=ALU.not_equal, fill=1.0, base=0,
                                    pattern=[[1, NB], [-1, NB]], channel_multiplier=0).then_inc(const_made, 1)

            def gather(table, i, index):
                nc.gpsimd.indirect_dma_start(rows[:, i, :], None, table, bass.IndirectOffsetOnAxis(ap=index, axis=0)
                                             ).then_inc(landed[i], 16)

            def gather_pair(pair, table, number, freed):
                for half in range(2):
                    nc.gpsimd.tensor_copy(idx[:, half, :], current[:, bass.ds((2 * pair + half) * RING, RING)]
                                          ).then_inc(idx_copied, 1)
                    hold(pool, pool_on, idx_copied, number + half + 1)
                    for i in range(RING):
                        if freed(half, i) is not None:
                            hold(pool, pool_on, *freed(half, i))
                        gather(table, i, idx[:, half, i:i + 1])

            def tile(t, first):
                def take_part(part):
                    picks = slice(part * CHOICES // PARTS, (part + 1) * CHOICES // PARTS)
                    if part < PARTS - 1:
                        pool.wait_ge(part_chosen, part + 1)
                        nc.gpsimd.tensor_copy(current[:, picks], chosen[:, picks]).then_inc(part_taken, 1)
                        pool.wait_ge(part_taken, part + 1)
                    else:
                        pool.wait_ge(chosen_ready, 1)
                        nc.gpsimd.tensor_copy(current[:, picks], chosen[:, picks]).then_inc(chosen_taken, 1)
                        pool.wait_ge(chosen_taken, 1)

                if first:
                    take_part(0)
                else:
                    hold(pool, pool_on, chosen_ready, t + 1)
                    nc.gpsimd.tensor_copy(current, chosen).then_inc(chosen_taken, 1)
                    hold(pool, pool_on, chosen_taken, t + 1)
                u, vp, vd = t * CHOICES, t * PE_STEPS, t * DVE_STEPS
                n = t * 2 * CHOICES // RING

                def u_freed(turn, i):
                    return u_used, u + turn * RING + i + 1

                def v_freed(turn, i):
                    return vp_used, vp + turn * RING + i + 1

                def mixed_freed(turn, i):
                    return mixed_slot(turn, i, vp, vd)

                def last_tile(i):
                    return None if first else mixed_slot(0, i, vp - PE_FIRST - PE_SLOTS, vd - DVE_SLOTS)

                gather_pair(0, peer_u, n, lambda half, i: u_freed(0, i) if half else last_tile(i))
                pairs = PAIRS // PARTS
                for part in range(PARTS if first else 0):
                    if part:
                        take_part(part)
                    with pool.Fori(max(1, part * pairs), (part + 1) * pairs) as pair:
                        gather_pair(pair, peer_u, n + 2 * pair, lambda half, i: u_freed(2 * pair + half - 1, i))
                if not first:
                    with pool.Fori(1, PAIRS) as pair:
                        gather_pair(pair, peer_u, n + 2 * pair, lambda half, i: u_freed(2 * pair + half - 1, i))
                n += CHOICES // RING
                gather_pair(0, peer_v, n, lambda half, i: v_freed(0, i) if half else u_freed(2 * PAIRS - 1, i))
                with pool.Fori(1, PE_PAIRS) as pair:
                    gather_pair(pair, peer_v, n + 2 * pair, lambda half, i: v_freed(2 * pair + half - 1, i))
                gather_pair(PE_PAIRS, peer_v, n + 2 * PE_PAIRS,
                            lambda half, i: mixed_freed(0, i) if half else v_freed(2 * PE_PAIRS - 1, i))
                with pool.Fori(PE_PAIRS + 1, PAIRS) as pair:
                    gather_pair(pair, peer_v, n + 2 * pair, lambda half, i: mixed_freed(2 * (pair - PE_PAIRS) + half - 1, i))

            tile(0, True)
            with pool.Fori(1, NT) as t:
                tile(t, False)
            pool.wait_ge(idxT_landed, 16)
            for n in range(NB):
                pool.wait_ge(*mixed_slot(0, n, (NT - 1) * PE_STEPS + (MIXED_TURNS - 1) * PE_SLOTS, NT * DVE_STEPS - DVE_SLOTS))
                gather(peer_u, n, idxT[:, n:n + 1])
            for n in range(NB):
                pool.wait_ge(u_used, NT * CHOICES + n + 1)
                gather(peer_v, n, idxT[:, n:n + 1])

        ACT_Q, ACT_F = 1, 1

        @block.scalar
        def _(act):
            def rank_norm(q):
                steps = Chain(act, act_q, q * ACT_Q)
                hold(act, act_on, xq_landed, (q + 1) * 16)
                steps.link(nc.scalar.activation(q_flat[:, 0:D], xq, ACT.Square, accum_out=ssq))
                nc.scalar.activation(rms, ssq, ACT.Sqrt, bias=eps[:, :], scale=1.0 / D).then_inc(xq_rms, 1)
                assert steps.n == ACT_Q

            def rank(q):
                act.wait_ge(hnT_ready, q + 1)
                nc.scalar.activation(hT, TP[:, :].rearrange("p (k t) -> p k t", t=P), ACT.Copy).then_inc(hT_copied, 1)
                act.wait_ge(q_ready, q)
                nc.scalar.activation(q_flat, QB[:, :], ACT.Copy).then_inc(q_copied, 1)
                act.wait_ge(sc_ready, q)
                nc.scalar.activation(scores.rearrange("p a b -> p (a b)"), QB[:, :], ACT.Copy).then_inc(sc_copied, 1)

            def finish(f, R, last_prompt=False):
                steps = Chain(act, act_f, f * ACT_F)
                act.wait_ge(pT_ready, f + 1)
                nc.scalar.activation(pT[:, :, 0:R], QB[:, 0:2 * P].rearrange("p (k t) -> p k t", t=P)[:, :, 0:R],
                                     ACT.Copy).then_inc(pT_copied, 1)
                act.wait_ge(x2_ready, f + 1)
                steps.link(nc.scalar.activation(ple[0:R, :], xf[0:R, :], ACT.Square, accum_out=ssq2[0:R, :]))
                nc.scalar.activation(rms2[0:R, :], ssq2[0:R, :], ACT.Sqrt, bias=eps[0:R, :], scale=1.0 / D).then_inc(x2_rms, 1)
                if last_prompt:
                    act.wait_ge(u_used, NT * CHOICES + NB)
                    nc.scalar.activation(gelu8, dots8, ACT.Gelu).then_inc(gelu_ready, 1)
                act.wait_ge(fin_ready, f + 1)
                nc.scalar.activation(h3[0:R, :], QB[0:R, D:2 * D], ACT.Sigmoid)
                nc.scalar.activation(ple[0:R, :], QB[0:R, 0:D], ACT.Copy).then_inc(fin_copied, 1)
                assert steps.n == ACT_F

            def exponentials(q):
                act.wait_ge(gate_shifted, q + 1)
                nc.scalar.activation(gates, gates, ACT.Exp).then_inc(gexp_ready, 1)

            def diagonal(t, count, slot, choice, first):
                if not first:
                    hold(act, act_on, vp_used, t * PE_STEPS + count - DIAGS + 1)
                nc.scalar.activation(diag[:, slot, :], ident[:, :], ACT.Copy,
                                     scale=weights[:, bass.ds(choice, 1)]).then_inc(diag_ready, 1)

            def tile(t, first):
                rank_norm(t + 1)
                if not first:
                    finish(t - 1, P)
                rank(t + 1)
                act.wait_ge(dots_copied, (t + 1) * PAIRS)
                nc.scalar.activation(gelu, dots, ACT.Gelu).then_inc(gelu_ready, 1)
                hold(act, act_on, weights_ready, t + 1)
                for s in range(2 * RING):
                    diagonal(t, s, s % DIAGS, s, first and s < DIAGS)
                with act.Fori(1, PE_PAIRS) as pair:
                    for s in range(2 * RING):
                        diagonal(t, pair * 2 * RING + s, s % DIAGS, pair * 2 * RING + s, False)
                with act.Fori(PE_PAIRS, PAIRS) as pair:
                    for half in range(2):
                        for i in range(PE_SLOTS):
                            k = half * PE_SLOTS + i
                            diagonal(t, PE_FIRST + (pair - PE_PAIRS) * 2 * PE_SLOTS + k, k % DIAGS, (2 * pair + half) * RING + i, False)
                exponentials(t + 1)

            for part in range(PARTS):
                bank = slice(part * BANK, (part + 1) * BANK)
                act.wait_ge(part_q_ready, part + 1)
                nc.scalar.activation(q_flat[:, bank], QB[:, bank], ACT.Copy).then_inc(part_q_copied, 1)
                act.wait_ge(part_sc_ready, part + 1)
                nc.scalar.activation(sc_flat[:, bank], QB[:, bank], ACT.Copy).then_inc(sc_copied if part == PARTS - 1 else part_sc_copied, 1)
            exponentials(0)
            tile(0, True)
            with act.Fori(1, NT) as t:
                tile(t, False)
            finish(NT - 1, P, last_prompt=True)
            finish(NT, NB)

        DVE_Q, DVE_F, DVE_K, DVE_W = 1, 2, 21, 3
        TT = nc.vector.tensor_tensor

        @block.vector
        def _(dve):
            def normalise(q):
                steps = Chain(dve, dve_q, q * DVE_Q)
                dve.wait_ge(xq_rms, q + 1)
                steps.link(nc.vector.reciprocal(rstd, rms))
                nc.vector.scalar_tensor_tensor(out=xq, in0=xq, scalar=rstd, in1=gain, op0=ALU.mult, op1=ALU.mult).then_inc(hn_ready, 1)
                assert steps.n == DVE_Q

            def take_h(q):
                hold(dve, dve_on, hn_ready, q + 1)
                dve.wait_ge(hnT_ready, q + 1)
                nc.vector.tensor_copy(h, xq).then_inc(h_copied, 1)
                hold(dve, dve_on, h_copied, q + 1)

            def choose(q, h0, h1, steps):
                heads, n_heads = slice(h0, h1), h1 - h0
                lists, picks = slice(2 * h0, 2 * h1), slice(h0 * TOPK, h1 * TOPK)

                def step(ins):
                    steps.link(ins)
                    dve.sem_inc(dve_on, 1)

                def best16(values, out, out_i, which):
                    for half in range(2):
                        part8 = slice(8 * half, 8 * half + 8)
                        for m in range(which.start, which.stop):
                            last = nc.vector.max(out[:, m, part8], values[:, m, :])
                        step(last)
                        for m in range(which.start, which.stop):
                            last = nc.vector.max_index(out_i[:, m, part8], out[:, m, part8], values[:, m, :])
                        step(last)
                        if half == 0:
                            for m in range(which.start, which.stop):
                                last = nc.vector.match_replace(values[:, m, :], out[:, m, part8], values[:, m, :], -3.0e38)
                            step(last)

                best16(scores, top, top_i, lists)
                nc.vector.tensor_copy(top_f[:, lists, :], top_i[:, lists, :])
                pairs = cand[:, heads, :].rearrange("p h (i j) -> p h i j", j=TOPK)
                halves = top[:, lists, :].rearrange("p (h s) k -> p h s k", s=2)
                step(TT(pairs, halves[:, :, 0, :].unsqueeze(3).to_broadcast([P, n_heads, TOPK, TOPK]),
                        halves[:, :, 1, :].unsqueeze(2).to_broadcast([P, n_heads, TOPK, TOPK]), ALU.add))
                best16(cand, best, best_i, heads)
                keys = top_f[:, lists, :].rearrange("p (h s) k -> p h s k", s=2)
                flat_i = best_i.rearrange("p h k -> p (h k)")[:, picks]
                for s, (op, arg, number) in enumerate(((ALU.logical_shift_right, 4, first_key), (ALU.bitwise_and, 15, second_key))):
                    steps.link(nc.vector.tensor_scalar(part_i[:, picks], flat_i, arg, None, op))
                    steps.link(nc.vector.tensor_copy(part[:, picks], part_i[:, picks]))
                    steps.link(TT(match[:, picks, :], part[:, picks].unsqueeze(2).to_broadcast([P, n_heads * TOPK, TOPK]),
                                  iota16.unsqueeze(1).to_broadcast([P, n_heads * TOPK, TOPK]), ALU.is_equal))
                    by_head = match[:, picks, :].rearrange("p (h k) i -> p h k i", k=TOPK)
                    steps.link(TT(by_head, by_head, keys[:, :, s, :].unsqueeze(2).to_broadcast([P, n_heads, TOPK, TOPK]), ALU.mult))
                    steps.link(nc.vector.tensor_reduce(number[:, picks], match[:, picks, :], AX.X, ALU.add))
                if n_heads == PH:
                    dve.wait_ge(chosen_taken, q)
                assert steps.n == DVE_K, steps.n
                return nc.vector.scalar_tensor_tensor(out=chosen[:, picks], in0=first_key[:, picks], scalar=float(NKEY),
                                                      in1=second_key[:, picks], op0=ALU.mult, op1=ALU.add)

            def choose_part(part):
                if part < PARTS - 1:
                    dve.wait_ge(part_sc_copied, part + 1)
                else:
                    dve.wait_ge(sc_copied, 1)
                choose(0, part * PH // PARTS, (part + 1) * PH // PARTS, Chain(dve, dve_k, part * DVE_K)).then_inc(
                    chosen_ready if part == PARTS - 1 else part_chosen, 1)

            def shift_gates():
                TT(gates.rearrange("p (h k) -> p h k", k=TOPK), best, best[:, :, 0:1].to_broadcast([P, PH, TOPK]),
                   ALU.subtract).then_inc(gate_shifted, 1)

            def dot_pair(t, pair, first):
                for s in range(2 * RING):
                    i = s % RING
                    dve.wait_ge(landed[i], (t * 2 * CHOICES // RING + 2 * pair + s // RING + 1) * 16)
                    if s == 0 and not first:
                        dve.wait_ge(dots_copied, t * PAIRS + pair)
                    nc.vector.tensor_tensor_reduce(out=rows[:, i, :], in0=rows[:, i, :], in1=h, scale=1.0, scalar=0.0,
                                                   op0=ALU.mult, op1=ALU.add, accum_out=dots16[:, s:s + 1]).then_inc(u_used, 1)
                hold(dve, dve_on, u_used, t * CHOICES + (pair + 1) * 2 * RING)
                nc.vector.tensor_copy(dots[:, bass.ds(pair * 2 * RING, 2 * RING)], dots16).then_inc(dots_copied, 1)

            def normalise_gates(t, R, steps):
                per_head = gates[0:R, :].rearrange("p (h k) -> p h k", k=TOPK)
                dve.wait_ge(gexp_ready, t + 1)
                steps.link(nc.vector.tensor_reduce(sums[0:R, :], per_head, AX.X, ALU.add))
                steps.link(nc.vector.reciprocal(sums[0:R, :], sums[0:R, :]))
                return TT(per_head, per_head, sums[0:R, :].unsqueeze(2).to_broadcast([R, PH, TOPK]), ALU.mult)

            def finish_x2(f, R, v_count):
                dve.wait_ge(vp_used, v_count)
                dve.wait_ge(xf_landed, (f + 1) * 16)
                TT(xf[0:R, :], VA[0:R, :], xf[0:R, :], ALU.add).then_inc(x2_ready, 1)

            def finish_norm(f, R):
                steps = Chain(dve, dve_f, f * DVE_F)
                dve.wait_ge(x2_rms, f + 1)
                steps.link(nc.vector.reciprocal(rstd2[0:R, :], rms2[0:R, :]))
                nc.vector.tensor_scalar(h3[0:R, :], xf[0:R, :], rstd2[0:R, :], None, ALU.mult).then_inc(h3_ready, 1)

            def finish_gain(f, R):
                dve.wait_ge(h3T_ready, f + 1)
                TT(hT[:, :, 0:R], TP[:, :].rearrange("p (k t) -> p k t", t=P)[:, :, 0:R],
                   norm_cols[:, 1, :].unsqueeze(2).to_broadcast([P, KD, R]), ALU.mult).then_inc(h3T_copied, 1)

            def finish_sum(f, R):
                steps = Chain(dve, dve_f, f * DVE_F + 1)
                dve.wait_ge(fin_copied, f + 1)
                steps.link(TT(ple[0:R, :], ple[0:R, :], h3[0:R, :], ALU.mult))
                TT(xf[0:R, :], xf[0:R, :], ple[0:R, :], ALU.add).then_inc(y_ready, 1)

            def add_pair(t, pair, first):
                for half in range(2):
                    for i in range(PE_SLOTS, RING):
                        done = t * DVE_STEPS + (2 * (pair - PE_PAIRS) + half) * DVE_SLOTS + i - PE_SLOTS
                        dve.wait_ge(landed[i], ((2 * t + 1) * CHOICES // RING + 2 * pair + half + 1) * 16)
                        if not first or half or i > PE_SLOTS:
                            dve.wait_ge(vd_used, done)
                        nc.vector.scalar_tensor_tensor(out=xf, in0=rows[:, i, :],
                                                       scalar=weights[:, bass.ds((2 * pair + half) * RING + i, 1)],
                                                       in1=xf, op0=ALU.mult, op1=ALU.add).then_inc(vd_used, 1)

            def tile(t, first):
                dot_pair(t, 0, first)
                if first:
                    dot_pair(t, 1, False)
                    for part in range(2, PARTS):
                        choose_part(part)
                        if part == PARTS - 1:
                            shift_gates()
                        dot_pair(t, 2 * part - 2, False)
                        dot_pair(t, 2 * part - 1, False)
                    normalise(t + 1)
                    with dve.Fori(2 * PARTS - 2, PAIRS) as pair:
                        dot_pair(t, pair, False)
                else:
                    finish_x2(t - 1, P, t * PE_STEPS)
                    dot_pair(t, 1, False)
                    normalise(t + 1)
                    finish_norm(t - 1, P)
                    dot_pair(t, 2, False)
                    finish_gain(t - 1, P)
                    with dve.Fori(3, PAIRS) as pair:
                        dot_pair(t, pair, False)
                    finish_sum(t - 1, P)
                steps = Chain(dve, dve_w, t * DVE_W)
                steps.link(normalise_gates(t, P, steps))
                assert steps.n == DVE_W
                dve.wait_ge(gelu_ready, t + 1)
                TT(weights, gates, gelu, ALU.mult).then_inc(weights_ready, 1)
                take_h(t + 1)
                hold(dve, dve_on, weights_ready, t + 1)
                hold(dve, dve_on, sc_copied, t + 2)
                choose(t + 1, 0, PH, Chain(dve, dve_k, (t + PARTS) * DVE_K)).then_inc(chosen_ready, 1)
                shift_gates()
                dve.wait_ge(xf_landed, (t + 1) * 16)
                add_pair(t, PE_PAIRS, first)
                with dve.Fori(PE_PAIRS + 1, PAIRS) as pair:
                    add_pair(t, pair, False)

            dve.wait_ge(const_made, 2)
            take_h(0)
            choose_part(0)
            choose_part(1)
            tile(0, True)
            with dve.Fori(1, NT) as t:
                tile(t, False)
            steps = Chain(dve, dve_w, NT * DVE_W)
            normalise_gates(NT, NB, steps).then_inc(g8_ready, 1)
            finish_x2(NT - 1, P, NT * PE_STEPS)
            finish_norm(NT - 1, P)
            finish_gain(NT - 1, P)
            dve.wait_ge(hbc_landed, NB * 16)
            for n in range(NB):
                dve.wait_ge(landed[n], (NT * 2 * CHOICES // RING + 1) * 16)
                nc.vector.tensor_tensor_reduce(out=rows[:, n, :], in0=rows[:, n, :], in1=h_bc[:, n, :], scale=1.0, scalar=0.0,
                                               op0=ALU.mult, op1=ALU.add, accum_out=dots8[:, n:n + 1]).then_inc(u_used, 1)
            dve.wait_ge(gelu_ready, NT + 1)
            dve.wait_ge(gT_landed, 16)
            steps.link(TT(w8, gatesT, gelu8, ALU.mult))
            TT(w_cols, eye8, w8.unsqueeze(2).to_broadcast([P, NB, NB]), ALU.mult).then_inc(cols_ready, 1)
            finish_sum(NT - 1, P)
            finish_x2(NT, NB, NT * PE_STEPS + NB)
            finish_norm(NT, NB)
            finish_gain(NT, NB)
            finish_sum(NT, NB)

        @block.tensor
        def _(pe):
            def transpose(out, src, rows_):
                return nc.tensor.transpose(out, src, ident[0:rows_, 0:rows_])

            def queries(halves):
                for m in halves:
                    for k in range(KD):
                        last = nc.tensor.matmul(QB[:, m * P:(m + 1) * P], wq[k][:, m * P:(m + 1) * P], hT[:, k, :],
                                                start=(k == 0), stop=(k == KD - 1))
                return last

            def key_scores(halves):
                for m in halves:
                    last = nc.tensor.matmul(QB[:, m * P:(m + 1) * P], q_cand[:, m, :], keysT[:, m % 2, :], start=True, stop=True)
                return last

            def rank(q):
                pe.wait_ge(hn_ready, q + 1)
                for k in range(KD):
                    last = transpose(TP[:, k * P:(k + 1) * P], xq[:, k * P:(k + 1) * P], P)
                last.then_inc(hnT_ready, 1)
                pe.wait_ge(hT_copied, q + 1)
                queries(range(2 * PH)).then_inc(q_ready, 1)
                pe.wait_ge(q_copied, q)
                key_scores(range(2 * PH)).then_inc(sc_ready, 1)

            def finish(f, R):
                pe.wait_ge(p_landed, (f + 1) * 16)
                if R == P:
                    pe.wait_ge(sc_copied, f + 2)
                else:
                    pe.wait_ge(fin_copied, NT)
                for k in range(2):
                    last = transpose(QB[:, k * P:k * P + R], p_rows[0:R, k * P:(k + 1) * P], R)
                last.then_inc(pT_ready, 1)
                pe.wait_ge(pT_copied, f + 1)
                for c in range(0, D, BANK):
                    for k in range(2):
                        nc.tensor.matmul(QB[0:R, c:c + BANK], pT[:, k, 0:R], w_ple[:, k, c:c + BANK],
                                         start=(k == 0), stop=(k == 1))
                pe.wait_ge(h3_ready, f + 1)
                for k in range(KD):
                    last = transpose(TP[:, k * P:k * P + R], h3[0:R, k * P:(k + 1) * P], R)
                last.then_inc(h3T_ready, 1)
                pe.wait_ge(h3T_copied, f + 1)
                for c in range(0, D, BANK):
                    for k in range(KD):
                        last = nc.tensor.matmul(QB[0:R, D + c:D + c + BANK], hT[:, k, 0:R], w_gate[:, k, c:c + BANK],
                                                start=(k == 0), stop=(k == KD - 1))
                last.then_inc(fin_ready, 1)

            def add_row(t, count, slot, diagonal, turn, start=False, stop=False):
                pe.wait_ge(diag_ready, t * PE_STEPS + count + 1)
                pe.wait_ge(landed[slot], ((2 * t + 1) * CHOICES // RING + turn + 1) * 16)
                for c in range(0, D, BANK):
                    last = nc.tensor.matmul(VA[:, c:c + BANK], diag[:, diagonal, :], rows[:, slot, c:c + BANK], start=start, stop=stop)
                last.then_inc(vp_used, 1)

            def add_pair(t, pair, start=False):
                for s in range(2 * RING):
                    add_row(t, pair * 2 * RING + s, s % RING, s % DIAGS, 2 * pair + s // RING, start=start and s == 0)

            def add_mixed_pair(t, pair, stop=False):
                for half in range(2):
                    for i in range(PE_SLOTS):
                        k = half * PE_SLOTS + i
                        add_row(t, PE_FIRST + (pair - PE_PAIRS) * 2 * PE_SLOTS + k, i, k % DIAGS, 2 * pair + half,
                                stop=stop and k == 2 * PE_SLOTS - 1)

            def tile(t, first):
                if not first:
                    finish(t - 1, P)
                rank(t + 1)
                if not first:
                    pe.wait_ge(x2_ready, t)
                add_pair(t, 0, start=True)
                with pe.Fori(1, PE_PAIRS) as pair:
                    add_pair(t, pair)
                with pe.Fori(PE_PAIRS, PAIRS - 1) as pair:
                    add_mixed_pair(t, pair)
                add_mixed_pair(t, PAIRS - 1, stop=True)

            pe.wait_ge(ranking["keysT_copied"], 1)
            pe.wait_ge(wq_in, KD * 16)
            pe.wait_ge(hT_copied, 1)
            n = 2 * PH // PARTS
            queries(range(n)).then_inc(part_q_ready, 1)
            for part in range(PARTS):
                if part < PARTS - 1:
                    queries(range((part + 1) * n, (part + 1) * n + 1))
                pe.wait_ge(part_q_copied, part + 1)
                key_scores(range(part * n, (part + 1) * n)).then_inc(part_sc_ready, 1)
                if part < PARTS - 1:
                    queries(range((part + 1) * n + 1, (part + 2) * n)).then_inc(part_q_ready, 1)
            pe.wait_ge(sc_copied, 1)
            tile(0, True)
            pe.wait_ge(w_fin_in, 2 * 16)
            with pe.Fori(1, NT) as t:
                tile(t, False)
            finish(NT - 1, P)
            pe.wait_ge(cols_ready, 1)
            for n in range(NB):
                pe.wait_ge(landed[n], (NT * 2 * CHOICES // RING + 2) * 16)
                for c in range(0, D, BANK):
                    last = nc.tensor.matmul(VA[0:NB, c:c + BANK], w_cols[:, n, :], rows[:, n, c:c + BANK], start=(n == 0),
                                            stop=(n == NB - 1))
                last.then_inc(vp_used, 1)
            finish(NT, NB)


_INS = ['x_prompt', 'x_sample', 'cache_k', 'cache_v', 'state_conv', 'p_prompt', 'p_sample', 'norm_mix', 'w_in', 'q_gain',
        'k_gain', 'attn_sinks', 'conv_dw_w', 'conv_dw_b', 'conv_ln_g', 'conv_ln_b', 'w_out', 'norm_ffn', 'peer_wq',
        'peer_sub_keys', 'peer_u', 'peer_v', 'norm_ple', 'w_ple_proj', 'w_ple_gate']
_OUTS = [(1, SEQ, D), (NB, 1, D), (1, 1, P, KV, HD), (1, 1, P, KV, HD), (1, 1, HIST, CONV), (1, NB, P, KV, HD),
         (1, NB, P, KV, HD), (1, NB, HIST, CONV)]


def kernel(**inputs):
    import numpy as _np
    import concourse.bacc as _bacc
    from concourse import mybir as _mybir
    from concourse.bass_utils import run_bass_kernel_spmd as _run

    nc = _bacc.Bacc("TRN2", target_bir_lowering=False, num_devices=1)
    arrays, args = {}, []
    for name in _INS:
        a = _np.ascontiguousarray(inputs[name])
        arrays[f"in_{name}_dram"] = a
        args.append(nc.dram_tensor(f"in_{name}_dram", a.shape, _mybir.dt.from_np(a.dtype), kind="ExternalInput").ap())
    for i, shape in enumerate(_OUTS):
        args.append(nc.dram_tensor(f"out_{i}_dram", shape, _mybir.dt.float32, kind="ExternalOutput").ap())
    hymba_step(nc, *args)
    r = _run(nc, [arrays], core_ids=[0])
    return tuple(r.results[0][f"out_{i}_dram"] for i in range(len(_OUTS)))
```
